# Optimizing a Trainium2 kernel written in Bass

```python
import jax
import jax.numpy as jnp
from jax import lax
import numpy as np

D_MODEL = 1024
BATCH = 1
SEQ = 256
DEPTH = 2
DEC_BATCH = 8
DEC_SEQ = 1
PAST_LEN = 2048
PAGE_SIZE = 128

N_EVEN = (DEPTH + 1) // 2
N_ODD = DEPTH // 2
ALPHA = (2 * DEPTH) ** 0.25
BETA = (8 * DEPTH) ** -0.25
LN_EPS = 1e-5
MIX_WIDTH = D_MODEL
A_HEADS = 4
A_DK = 128
A_DV = 128
A_WIDTH = A_HEADS * A_DV
A_CHUNK = 64
B_WIDTH = MIX_WIDTH - A_WIDTH
POOL_SIZES = (2, 4, 8, 16)
B_GROUPS = len(POOL_SIZES)
B_GW = B_WIDTH // B_GROUPS
POOL_CTX = max(POOL_SIZES) - 1
IN_A_WIDTH = 2 * A_HEADS * A_DK + 2 * A_WIDTH + B_WIDTH
C_HEADS = 16
C_KV_HEADS = 2
C_GROUP = C_HEADS // C_KV_HEADS
C_HD = 64
WINDOW = 128
C_SCALE = C_HD ** -0.5
IN_C_WIDTH = (C_HEADS + 2 * C_KV_HEADS) * C_HD
N_MEM = 256
M_HEADS = 4
M_HD = D_MODEL // M_HEADS
M_SCALE = M_HD ** -0.5
PEER_HEADS = 8
N_KEYS = 128
N_EXPERTS = N_KEYS * N_KEYS
PEER_DQ = 256
PEER_TOPK = 16
PEER_BLOCK = 128

kernel_name = 'hybrid_hgrn2_pool_swa_peer_step'

F32 = jnp.float32

def layer_norm(x, g, b):
    xf = x.astype(F32)
    mu = jnp.mean(xf, -1, keepdims=True)
    var = jnp.mean(jnp.square(xf - mu), -1, keepdims=True)
    return ((xf - mu) * lax.rsqrt(var + LN_EPS) * g.astype(F32) + b.astype(F32)).astype(x.dtype)

def post_norm(x, h, g, b):
    return layer_norm(ALPHA * x + h.astype(x.dtype), g, b)

def gla_chunked(q, k, v, log_f, s0):
    B, T, H, _ = q.shape
    DV = v.shape[-1]
    c = min(A_CHUNK, T)
    n = -(-T // c)
    tp = n * c

    def prep(a):
        a = jnp.pad(a.astype(F32), ((0, 0), (0, tp - T), (0, 0), (0, 0)))
        return jnp.moveaxis(a.reshape(B, n, c, H, a.shape[-1]), 1, 0)

    causal = jnp.tril(jnp.ones((c, c), bool))[None, :, :, None, None]

    def step(s, inp):
        qc, kc, vc, gc = inp
        b = jnp.cumsum(gc, axis=1)
        o_inter = jnp.einsum('bthk,bhkv->bthv', qc * jnp.exp(b), s)
        diff = b[:, :, None] - b[:, None, :]
        decay = jnp.where(causal, jnp.exp(jnp.minimum(diff, 0.0)), 0.0)
        att = jnp.einsum('bthk,bshk,btshk->bths', qc, kc, decay)
        o_intra = jnp.einsum('bths,bshv->bthv', att, vc)
        bl = b[:, -1]
        s_new = jnp.exp(bl)[..., None] * s + jnp.einsum('bshk,bshv->bhkv', kc * jnp.exp(bl[:, None] - b), vc)
        return s_new, o_inter + o_intra

    s_fin, o = lax.scan(step, s0.astype(F32), (prep(q), prep(k), prep(v), prep(log_f)))
    o = jnp.moveaxis(o, 0, 1).reshape(B, tp, H, DV)[:, :T]
    return o, s_fin

def pool_mixer(u, ctx, pos0, pool_w, pool_scale):
    B, T, W = u.shape
    ue = jnp.concatenate([ctx.astype(u.dtype), u], axis=1)
    cs = jnp.cumsum(ue.astype(F32), axis=1)
    cs = jnp.concatenate([jnp.zeros((B, 1, W), F32), cs], axis=1)
    pos = pos0 + jnp.arange(T)
    outs = []
    for gi, w in enumerate(POOL_SIZES):
        sl = slice(gi * B_GW, (gi + 1) * B_GW)
        hi = cs[:, POOL_CTX + 1:POOL_CTX + 1 + T, sl]
        lo = cs[:, POOL_CTX + 1 - w:POOL_CTX + 1 - w + T, sl]
        cnt = jnp.minimum(pos + 1, w).astype(F32)[None, :, None]
        outs.append((hi - lo) / cnt - u[:, :, sl].astype(F32))
    pooled = jnp.stack(outs, axis=2)
    y = jnp.einsum('btgc,gcd->btgd', pooled, pool_w.astype(F32)).reshape(B, T, W) * pool_scale.astype(F32)
    return y.astype(u.dtype), ue[:, -POOL_CTX:]

def hgrn_pool_mixer(x, a_idx, w_in, gamma, norm_g, pool_w, pool_scale, w_out, s0, pool_ctx, pos0):
    B, T, _ = x.shape
    proj = jnp.einsum('btd,de->bte', x, w_in)
    qk_w = A_HEADS * A_DK
    q, f, i, g, u = jnp.split(proj, [qk_w, 2 * qk_w, 2 * qk_w + A_WIDTH, 2 * qk_w + 2 * A_WIDTH], axis=-1)
    lb = jnp.cumsum(jax.nn.softmax(gamma.astype(F32), axis=0), axis=0)[a_idx]
    fg = lb + (1.0 - lb) * jax.nn.sigmoid(f.astype(F32))
    heads = lambda a, d: a.reshape(B, T, A_HEADS, d)
    o, s_new = gla_chunked(heads(jax.nn.silu(q.astype(F32)), A_DK), heads(1.0 - fg, A_DK),
                           heads(i, A_DV), heads(jnp.log(fg), A_DK), s0)
    o = o * lax.rsqrt(jnp.mean(jnp.square(o), -1, keepdims=True) + LN_EPS)
    o = (o.reshape(B, T, A_WIDTH) * norm_g.astype(F32) * jax.nn.silu(g.astype(F32))).astype(x.dtype)
    pooled, ctx_new = pool_mixer(u, pool_ctx, pos0, pool_w, pool_scale)
    out = jnp.einsum('bte,ed->btd', jnp.concatenate([o, pooled], axis=-1), w_out)
    return out, s_new.astype(s0.dtype), ctx_new

def sink_softmax(s, mask, sink):
    s = jnp.where(mask, s, -jnp.inf)
    m = jnp.maximum(jnp.max(s, -1, keepdims=True), sink)
    p = jnp.exp(s - m)
    return p / (jnp.sum(p, -1, keepdims=True) + jnp.exp(sink - m))

def swa_banded(q, k, v, sink):
    B, T = q.shape[:2]
    nb = -(-T // WINDOW)
    tp = nb * WINDOW
    padt = lambda a: jnp.pad(a, ((0, 0), (0, tp - T)) + ((0, 0),) * (a.ndim - 2))
    qb = padt(q).reshape(B, nb, WINDOW, C_KV_HEADS, C_GROUP, C_HD)
    kb = padt(k).reshape(B, nb, WINDOW, C_KV_HEADS, C_HD)
    vb = padt(v).reshape(B, nb, WINDOW, C_KV_HEADS, C_HD)
    prev = lambda a: jnp.pad(a, ((0, 0), (1, 0), (0, 0), (0, 0), (0, 0)))[:, :-1]
    kk = jnp.concatenate([prev(kb), kb], axis=2)
    vv = jnp.concatenate([prev(vb), vb], axis=2)
    s = jnp.einsum('bnqhgd,bnkhd->bnhgqk', qb, kk).astype(F32) * C_SCALE
    qi = jnp.arange(WINDOW)[:, None]
    kj = jnp.arange(2 * WINDOW)[None, :]
    band = (kj > qi) & (kj <= qi + WINDOW)
    first = (jnp.arange(nb)[:, None, None] > 0) | (kj >= WINDOW)[None]
    mask = (band[None] & first)[None, :, None, None]
    p = sink_softmax(s, mask, sink[None, None, :, :, None, None])
    o = jnp.einsum('bnhgqk,bnkhd->bnqhgd', p.astype(vv.dtype), vv)
    return o.reshape(B, tp, C_KV_HEADS, C_GROUP, C_HD)[:, :T]

def swa_with_buffer(q, kk, vv, sink):
    T = q.shape[1]
    s = jnp.einsum('bqhgd,bkhd->bhgqk', q, kk).astype(F32) * C_SCALE
    qi = jnp.arange(T)[:, None]
    kj = jnp.arange(WINDOW + T)[None, :]
    mask = ((kj > qi) & (kj <= qi + WINDOW))[None, None, None]
    p = sink_softmax(s, mask, sink[None, :, :, None, None])
    return jnp.einsum('bhgqk,bkhd->bqhgd', p.astype(vv.dtype), vv)

def swa_mixer(x, w_in, sinks, w_out, cache_k=None, cache_v=None):
    B, T, _ = x.shape
    proj = jnp.einsum('btd,de->bte', x, w_in)
    q, k, v = jnp.split(proj, [C_HEADS * C_HD, (C_HEADS + C_KV_HEADS) * C_HD], axis=-1)
    q = q.reshape(B, T, C_KV_HEADS, C_GROUP, C_HD)
    k = k.reshape(B, T, C_KV_HEADS, C_HD)
    v = v.reshape(B, T, C_KV_HEADS, C_HD)
    sink = sinks.astype(F32).reshape(C_KV_HEADS, C_GROUP)
    if cache_k is None:
        o = swa_banded(q, k, v, sink)
        new_k, new_v = k[:, -WINDOW:], v[:, -WINDOW:]
    else:
        kk = jnp.concatenate([cache_k.astype(k.dtype), k], axis=1)
        vv = jnp.concatenate([cache_v.astype(v.dtype), v], axis=1)
        o = swa_with_buffer(q, kk, vv, sink)
        new_k, new_v = kk[:, -WINDOW:], vv[:, -WINDOW:]
    out = jnp.einsum('bte,ed->btd', o.reshape(B, T, C_HEADS * C_HD), w_out)
    return out, new_k, new_v

def mem_kv(mem, w_kv):
    B, M, _ = mem.shape
    k, v = jnp.split(jnp.einsum('bmd,de->bme', mem, w_kv), 2, axis=-1)
    return k.reshape(B, M, M_HEADS, M_HD), v.reshape(B, M, M_HEADS, M_HD)

def cross_attn(x, mk, mv, w_q, w_o):
    B, T, _ = x.shape
    q = jnp.einsum('btd,de->bte', x, w_q).reshape(B, T, M_HEADS, M_HD)
    s = jnp.einsum('bthd,bmhd->bhtm', q, mk.astype(q.dtype)).astype(F32) * M_SCALE
    p = jax.nn.softmax(s, axis=-1)
    o = jnp.einsum('bhtm,bmhd->bthd', p.astype(q.dtype), mv.astype(q.dtype))
    return jnp.einsum('bte,ed->btd', o.reshape(B, T, M_HEADS * M_HD), w_o)

def peer_ffn(x, w_q, subkeys, u_tab, v_tab):
    B, T, D = x.shape
    xt = x.reshape(B * T, D)
    n = xt.shape[0]
    nb = -(-n // PEER_BLOCK)
    xt = jnp.pad(xt, ((0, nb * PEER_BLOCK - n), (0, 0))).reshape(nb, PEER_BLOCK, D)

    def one_block(xb):
        q = jnp.einsum('td,de->te', xb, w_q).reshape(PEER_BLOCK, PEER_HEADS, 2, PEER_DQ // 2)
        s = jnp.einsum('thpc,hpkc->thpk', q, subkeys).astype(F32)
        v1, i1 = lax.top_k(s[:, :, 0], PEER_TOPK)
        v2, i2 = lax.top_k(s[:, :, 1], PEER_TOPK)
        cand = (v1[..., :, None] + v2[..., None, :]).reshape(PEER_BLOCK, PEER_HEADS, PEER_TOPK * PEER_TOPK)
        cidx = (i1[..., :, None] * N_KEYS + i2[..., None, :]).reshape(PEER_BLOCK, PEER_HEADS, PEER_TOPK * PEER_TOPK)
        top_s, sel = lax.top_k(cand, PEER_TOPK)
        eidx = jnp.take_along_axis(cidx, sel, axis=-1).reshape(PEER_BLOCK, PEER_HEADS * PEER_TOPK)
        gates = jax.nn.softmax(top_s, axis=-1).reshape(PEER_BLOCK, PEER_HEADS * PEER_TOPK)
        h = jax.nn.gelu(jnp.einsum('td,ted->te', xb, u_tab[eidx]).astype(F32))
        w = (gates * h).astype(xb.dtype)
        return jnp.einsum('te,ted->td', w, v_tab[eidx])

    y = lax.map(one_block, xt).reshape(nb * PEER_BLOCK, D)[:n]
    return y.reshape(B, T, D)

def setup_inputs(seed: int = 0) -> dict:
    key = jax.random.key(seed)
    ks = jax.random.split(key, 40)
    nrm = lambda k, shape, scale: jax.random.normal(k, shape, F32) * scale
    d = D_MODEL
    w_in_c = jnp.concatenate([
        nrm(ks[13], (N_ODD, d, (C_HEADS + C_KV_HEADS) * C_HD), d ** -0.5),
        nrm(ks[14], (N_ODD, d, C_KV_HEADS * C_HD), d ** -0.5 * BETA)], axis=-1)
    mem_wkv = jnp.concatenate([
        nrm(ks[18], (DEPTH, d, M_HEADS * M_HD), d ** -0.5),
        nrm(ks[19], (DEPTH, d, M_HEADS * M_HD), d ** -0.5 * BETA)], axis=-1)
    return {
        'x_prompt': nrm(ks[0], (BATCH, SEQ, d), 1.0),
        'x_sample': nrm(ks[1], (DEC_BATCH, DEC_SEQ, d), 1.0),
        'mem_prompt': nrm(ks[2], (BATCH, N_MEM, d), 1.0),
        'state_hgrn': nrm(ks[3], (N_EVEN, DEC_BATCH, A_HEADS, A_DK, A_DV), 0.5),
        'state_pool': nrm(ks[4], (N_EVEN, DEC_BATCH, POOL_CTX, B_WIDTH), 1.0),
        'cache_swa_k': nrm(ks[5], (N_ODD, DEC_BATCH, WINDOW, C_KV_HEADS, C_HD), 1.0),
        'cache_swa_v': nrm(ks[6], (N_ODD, DEC_BATCH, WINDOW, C_KV_HEADS, C_HD), 1.0),
        'cache_mem_k': nrm(ks[7], (DEPTH, DEC_BATCH, N_MEM, M_HEADS, M_HD), 1.0),
        'cache_mem_v': nrm(ks[8], (DEPTH, DEC_BATCH, N_MEM, M_HEADS, M_HD), 0.5),
        'w_in_a': nrm(ks[9], (N_EVEN, d, IN_A_WIDTH), d ** -0.5),
        'hgrn_gamma': nrm(ks[10], (N_EVEN + 1, A_HEADS * A_DK), 0.5),
        'hgrn_norm_g': 1.0 + nrm(ks[11], (N_EVEN, A_WIDTH), 0.05),
        'pool_w': nrm(ks[12], (N_EVEN, B_GROUPS, B_GW, B_GW), B_GW ** -0.5),
        'pool_scale': 1.0 + nrm(ks[20], (N_EVEN, B_WIDTH), 0.05),
        'w_out_a': nrm(ks[21], (N_EVEN, MIX_WIDTH, d), MIX_WIDTH ** -0.5 * BETA),
        'w_in_c': w_in_c,
        'attn_sinks': nrm(ks[15], (N_ODD, C_HEADS), 1.0),
        'w_out_c': nrm(ks[16], (N_ODD, C_HEADS * C_HD, d), (C_HEADS * C_HD) ** -0.5 * BETA),
        'mem_wq': nrm(ks[17], (DEPTH, d, M_HEADS * M_HD), d ** -0.5),
        'mem_wkv': mem_wkv,
        'mem_wo': nrm(ks[22], (DEPTH, M_HEADS * M_HD, d), (M_HEADS * M_HD) ** -0.5 * BETA),
        'peer_wq': nrm(ks[23], (DEPTH, d, PEER_HEADS * PEER_DQ), d ** -0.5),
        'peer_subkeys': nrm(ks[24], (DEPTH, PEER_HEADS, 2, N_KEYS, PEER_DQ // 2), (PEER_DQ // 2) ** -0.5),
        'peer_u': nrm(ks[25], (DEPTH, N_EXPERTS, d), d ** -0.5),
        'peer_v': nrm(ks[26], (DEPTH, N_EXPERTS, d), BETA),
        'ln_g': 1.0 + nrm(ks[27], (DEPTH, 3, d), 0.05),
        'ln_b': nrm(ks[28], (DEPTH, 3, d), 0.02),
    }

def reference(x_prompt, x_sample, mem_prompt, state_hgrn, state_pool, cache_swa_k, cache_swa_v,
              cache_mem_k, cache_mem_v, w_in_a, hgrn_gamma, hgrn_norm_g, pool_w, pool_scale, w_out_a,
              w_in_c, attn_sinks, w_out_c, mem_wq, mem_wkv, mem_wo, peer_wq, peer_subkeys, peer_u,
              peer_v, ln_g, ln_b):
    yp, ys = x_prompt, x_sample
    bp = x_prompt.shape[0]
    hgrn_p, hgrn_s, pool_p, pool_s = [], [], [], []
    swa_kp, swa_ks, swa_vp, swa_vs = [], [], [], []
    mem_kp, mem_vp = [], []
    for l in range(DEPTH):
        if l % 2 == 0:
            a = l // 2
            s0 = jnp.zeros((bp, A_HEADS, A_DK, A_DV), yp.dtype)
            ctx0 = jnp.zeros((bp, POOL_CTX, B_WIDTH), yp.dtype)
            hp, sp_new, cp_new = hgrn_pool_mixer(yp, a, w_in_a[a], hgrn_gamma, hgrn_norm_g[a], pool_w[a],
                                                 pool_scale[a], w_out_a[a], s0, ctx0, 0)
            hs, ss_new, cs_new = hgrn_pool_mixer(ys, a, w_in_a[a], hgrn_gamma, hgrn_norm_g[a], pool_w[a],
                                                 pool_scale[a], w_out_a[a], state_hgrn[a], state_pool[a], PAST_LEN)
            hgrn_p.append(sp_new)
            hgrn_s.append(ss_new)
            pool_p.append(cp_new)
            pool_s.append(cs_new)
        else:
            c = l // 2
            hp, kp_new, vp_new = swa_mixer(yp, w_in_c[c], attn_sinks[c], w_out_c[c])
            hs, ks_new, vs_new = swa_mixer(ys, w_in_c[c], attn_sinks[c], w_out_c[c], cache_swa_k[c], cache_swa_v[c])
            swa_kp.append(kp_new)
            swa_ks.append(ks_new)
            swa_vp.append(vp_new)
            swa_vs.append(vs_new)
        yp = post_norm(yp, hp, ln_g[l, 0], ln_b[l, 0])
        ys = post_norm(ys, hs, ln_g[l, 0], ln_b[l, 0])
        mk, mv = mem_kv(mem_prompt, mem_wkv[l])
        mem_kp.append(mk)
        mem_vp.append(mv)
        yp = post_norm(yp, cross_attn(yp, mk, mv, mem_wq[l], mem_wo[l]), ln_g[l, 1], ln_b[l, 1])
        ys = post_norm(ys, cross_attn(ys, cache_mem_k[l], cache_mem_v[l], mem_wq[l], mem_wo[l]), ln_g[l, 1], ln_b[l, 1])
        yp = post_norm(yp, peer_ffn(yp, peer_wq[l], peer_subkeys[l], peer_u[l], peer_v[l]), ln_g[l, 2], ln_b[l, 2])
        ys = post_norm(ys, peer_ffn(ys, peer_wq[l], peer_subkeys[l], peer_u[l], peer_v[l]), ln_g[l, 2], ln_b[l, 2])
    return (yp, ys, jnp.stack(hgrn_p), jnp.stack(hgrn_s), jnp.stack(pool_p), jnp.stack(pool_s),
            jnp.stack(swa_kp), jnp.stack(swa_ks), jnp.stack(swa_vp), jnp.stack(swa_vs),
            jnp.stack(mem_kp), jnp.stack(mem_vp))


_drawn_inputs = setup_inputs


def setup_inputs(seed=0):
    import zlib

    import numpy as np

    out = dict(_drawn_inputs(seed))
    spreads = {}
    factors = {'attn_sinks': 8.0}
    for name, (base, spread) in spreads.items():
        noise = np.random.default_rng([zlib.crc32(name.encode()), seed]).standard_normal(out[name].shape)
        drawn = base * np.exp(spread * noise) if base else spread * noise
        out[name] = jnp.asarray(drawn.astype(out[name].dtype))
    for name, factor in factors.items():
        out[name] = (out[name] * factor).astype(out[name].dtype)
    return out
```

```python
from contextlib import ExitStack

import concourse.bass as bass
from concourse import mybir

F32 = mybir.dt.float32
F32R = mybir.dt.float32r
U32 = mybir.dt.uint32
ALU = mybir.AluOpType
ACT = mybir.ActivationFunctionType
AX = mybir.AxisListType.X

P = 128
D = 1024
DC = D // P
TP = 256
TS = 8
T = TP + TS
LAYERS = 2
ALPHA = float((2 * LAYERS) ** 0.25)
EPS = 1e-5
HEADS_A = 4
BLK = 16
NBLK = TP // BLK
POOL_SIZES = (2, 4, 8, 16)
CTX = 15
KV = 2
HEADS_C = 16
HD = 64
MH = 4
MHD = 256
NMEM = 256
PH = 8
TOPK = 16
NKEYS = 128
LOWEST = -3.0e38
SLOTS = 4

C_ID, C_ONE, C_MEAN, C_HEAD, C_IOTA = (n * P for n in range(5))
C_MASK = 5 * P
C_EPS = C_MASK + 3 * P
C_END = C_EPS + 1


def hybrid_step(nc, io):
    with ExitStack() as top:
        step = Step(nc, io, top)
        step.load_constants()
        for layer in range(LAYERS):
            with ExitStack() as attn:
                step.open_attention(layer, attn)
                if layer == 0:
                    hgrn_pool_mixer(step, layer)
                else:
                    window_mixer(step, layer)
                project_and_norm(step, layer, 0)
                cross_attention(step, layer)
                project_and_norm(step, layer, 1)
            peer(step, layer)
            step.end_layer()
        step.store_result()


class Step:

    def __init__(self, nc, io, top):
        self.nc, self.io = nc, io
        self.sb = lambda name, shape, dt=F32, ctx=top: ctx.enter_context(nc.sbuf_tensor(name, shape, dt))
        self.ring = self.sb("slab_ring", [P, SLOTS, D])
        self.x = self.sb("x_T", [P, DC, T])
        self.const = self.sb("constants", [P, C_END])
        self.ln = self.sb("ln_scale_shift", [P, LAYERS * 3, 2, DC])
        self.ps = top.enter_context(nc.psum_tensor("banks", [P, 8, 512], F32))
        self.slab_ready = [nc.alloc_semaphore(f"slab_ready{s}") for s in range(SLOTS)]
        self.product_done = nc.alloc_semaphore("projection_product_done")
        self.u_split = nc.alloc_semaphore("u_slab_split")
        self.v_split = nc.alloc_semaphore("v_slab_split")
        self.stored = nc.alloc_semaphore("outputs_stored")
        self.constants_ready = nc.alloc_semaphore("constants_ready")
        self.vector_done = nc.alloc_semaphore("vector_instruction_done")
        self.scalar_done = nc.alloc_semaphore("scalar_instruction_done")
        self.gpsimd_done = nc.alloc_semaphore("gpsimd_instruction_done")
        self.count = {"vector": 0, "scalar": 0, "gpsimd": 0}
        self.stores = 0
        self.layer_sems = []
        self.slabs = []
        kinds = {"projection": 0, "u": 0, "v": 0}
        for layer in range(LAYERS):
            n = io["proj_counts"][layer]
            run = [("projection", io["proj"], sum(io["proj_counts"][:layer]) + k) for k in range(n)]
            run += [("u", io["u"], layer * P + k) for k in range(P)]
            run += [("v", io["v"], layer * P + k) for k in range(P)]
            for kind, src, k in run:
                self.slabs.append((kind, kinds[kind], src, k))
                kinds[kind] += 1
        self.used = 0
        self.loaded = 0

    ident = property(lambda s: s.const[:, C_ID:C_ID + P])
    ones = property(lambda s: s.const[:, C_ONE:C_ONE + P])
    mean_d = property(lambda s: s.const[:, C_MEAN:C_MEAN + P])
    mean_head = property(lambda s: s.const[:, C_HEAD:C_HEAD + P])
    iota = property(lambda s: s.const[:, C_IOTA:C_IOTA + P])
    masks = property(lambda s: s.const[:, C_MASK:C_MASK + 3 * P])
    eps = property(lambda s: s.const[:, C_EPS:C_EPS + 1])

    def sem(self, name):
        s = self.nc.alloc_semaphore(name)
        self.layer_sems.append(s)
        return s

    def end_layer(self):
        self.nc.clear_and_free_semaphores(self.layer_sems)
        self.layer_sems = []
        self.nc.all_engine_barrier()

    def link(self, engine, name, instruction, wait=True):
        sem = {"vector": self.vector_done, "scalar": self.scalar_done, "gpsimd": self.gpsimd_done}[name]
        self.count[name] += 1
        instruction.then_inc(sem, 1)
        if wait:
            engine.wait_ge(sem, self.count[name])

    def store(self, engine, dst, src):
        self.stores += 1
        engine.dma_start(dst, src).then_inc(self.stored, 16)

    def slot_free(self, sp, n):
        if n < SLOTS:
            return
        kind, k = self.slabs[n - SLOTS][:2]
        sp.wait_ge({"projection": self.product_done, "u": self.u_split, "v": self.v_split}[kind], k + 1)

    def load_until(self, sp, end):
        for n in range(self.loaded, min(end, len(self.slabs))):
            _, _, src, k = self.slabs[n]
            self.slot_free(sp, n)
            sp.dma_start(self.ring[:, n % SLOTS, :], src[k]).then_inc(self.slab_ready[n % SLOTS], 16)
        self.loaded = max(self.loaded, min(end, len(self.slabs)))

    def wait_slab(self, engine, n):
        engine.wait_ge(self.slab_ready[n % SLOTS], 16 * (n // SLOTS + 1))

    def slab(self, n):
        return self.ring[:, n % SLOTS, :].rearrange("p (c m) -> p c m", c=DC)

    def product_count(self, n):
        assert self.slabs[n][0] == "projection"
        return self.slabs[n][1] + 1

    def open_attention(self, layer, ctx):
        self.mixed = self.sb(f"mixed_T{layer}", [P, DC, T], ctx=ctx)
        self.q = self.sb(f"query_T{layer}", [P, DC, T], ctx=ctx)
        self.mem_k = self.sb(f"mem_k_T{layer}", [P, DC, NMEM], ctx=ctx)
        self.mem_v = self.sb(f"mem_v{layer}", [P, NMEM // P, D], ctx=ctx)

    def load_constants(self):
        nc, io = self.nc, self.io
        with nc.Block("constants", no_gpsimd_drain=True) as block:
            @block.sync
            def _(sp):
                sp.dma_start(self.const[:], io["const"]).then_inc(self.constants_ready, 16)
                sp.dma_start(self.x[:], io["x"]).then_inc(self.constants_ready, 16)
                sp.dma_start(self.ln[:], io["ln"]).then_inc(self.constants_ready, 16)
                self.load_until(sp, SLOTS)
                sp.wait_ge(self.constants_ready, 48)

    def store_result(self):
        nc, io = self.nc, self.io
        with nc.Block("result", no_gpsimd_drain=True) as block:
            @block.sync
            def _(sp):
                self.store(sp, io["y"], self.x[:])
                sp.wait_ge(self.stored, 16 * self.stores)


def product(step, pe, n, bank, rhs, width=T):
    nc = step.nc
    step.wait_slab(pe, n)
    w = step.slab(n)
    for c in range(DC):
        last = nc.tensor.matmul(step.ps[:, bank, 0:width], w[:, c, :], rhs[:, c, :],
                                start=(c == 0), stop=(c == DC - 1))
    last.then_inc(step.product_done, 1)


def emit_norm(step, block, tag, sub, res, squares, base_bank, residual_steps, tensor_steps):
    nc = step.nc
    mean_bank, var_bank = base_bank
    s_res = step.sem(f"residual_chunk_ready_{tag}")
    s_mean = step.sem(f"mean_ready_{tag}")
    s_cent = step.sem(f"centred_chunk_ready_{tag}")
    s_sq = step.sem(f"squared_chunk_ready_{tag}")
    s_var = step.sem(f"variance_ready_{tag}")
    s_std = step.sem(f"deviation_ready_{tag}")
    s_rstd = step.sem(f"reciprocal_ready_{tag}")
    s_norm = step.sem(f"normed_chunk_ready_{tag}")
    rstd = squares[:, 0, :]
    mean = step.ps[:, mean_bank, 0:T]
    var = step.ps[:, var_bank, 0:T]

    @block.tensor
    def _(pe):
        for j in range(DC):
            tensor_steps(pe, j, s_res)
            if j >= 1:
                pe.wait_ge(s_res, j)
                nc.tensor.matmul(mean, step.mean_d, res[:, j - 1, :], start=(j == 1), stop=False)
        pe.wait_ge(s_res, DC)
        nc.tensor.matmul(mean, step.mean_d, res[:, DC - 1, :], start=False, stop=True).then_inc(s_mean, 1)
        for j in range(DC):
            pe.wait_ge(s_sq, j + 1)
            last = nc.tensor.matmul(var, step.mean_d, squares[:, j, :], start=(j == 0), stop=(j == DC - 1))
        last.then_inc(s_var, 1)

    @block.vector
    def _(dve):
        for j in range(DC):
            residual_steps(dve, j).then_inc(s_res, 1)
        dve.wait_ge(s_mean, 1)
        dve.wait_ge(s_res, DC)
        for j in range(DC):
            nc.vector.tensor_tensor(res[:, j, :], res[:, j, :], mean, ALU.subtract).then_inc(s_cent, 1)
        dve.wait_ge(s_std, 1)
        nc.vector.reciprocal(rstd, rstd).then_inc(s_rstd, 1)
        dve.wait_ge(s_rstd, 1)
        for j in range(DC):
            nc.vector.tensor_tensor(res[:, j, :], res[:, j, :], rstd, ALU.mult).then_inc(s_norm, 1)

    @block.scalar
    def _(act):
        for j in range(DC):
            act.wait_ge(s_cent, j + 1)
            nc.scalar.activation(squares[:, j, :], res[:, j, :], ACT.Square).then_inc(s_sq, 1)
        act.wait_ge(s_var, 1)
        nc.scalar.activation(rstd, var, ACT.Sqrt, bias=step.eps).then_inc(s_std, 1)
        for j in range(DC):
            act.wait_ge(s_norm, j + 1)
            nc.scalar.activation(step.x[:, j, :], res[:, j, :], ACT.Identity,
                                 scale=step.ln[:, sub, 0, j:j + 1], bias=step.ln[:, sub, 1, j:j + 1])


def project_and_norm(step, layer, which):
    nc = step.nc
    base = step.used
    tag = f"{'mixer' if which == 0 else 'cross'}_{layer}"
    with ExitStack() as ctx:
        res = step.sb(f"res_{tag}", [P, DC, T], ctx=ctx)
        squares = step.sb(f"squares_{tag}", [P, DC, T], ctx=ctx)
        with nc.Block(f"out_{tag}", no_gpsimd_drain=True) as block:
            @block.sync
            def _(sp):
                step.load_until(sp, base + DC + SLOTS)

            def tensor_steps(pe, j, s_res):
                if j >= 3:
                    pe.wait_ge(s_res, j - 2)
                product(step, pe, base + j, j % 3, step.mixed[:])

            def residual_steps(dve, j):
                dve.wait_ge(step.product_done, step.product_count(base + j))
                return nc.vector.scalar_tensor_tensor(out=res[:, j, :], in0=step.x[:, j, :], scalar=ALPHA,
                                                      in1=step.ps[:, j % 3, 0:T], op0=ALU.mult, op1=ALU.add)

            emit_norm(step, block, tag, layer * 3 + which, res, squares, (3, 4), residual_steps, tensor_steps)
    step.used += DC


def memory_product(step, pe, n, k, mem, bank, s_read):
    nc = step.nc
    if k >= 2:
        pe.wait_ge(s_read, k - 1)
    if k < DC:
        product(step, pe, n, bank, mem[:], NMEM)
    else:
        step.wait_slab(pe, n)
        w = step.slab(n)
        for m in range(NMEM // P):
            for c in range(DC):
                last = nc.tensor.matmul(step.ps[:, bank, m * P:(m + 1) * P], mem[:, c, m * P:(m + 1) * P],
                                        w[:, c, :], start=(c == 0), stop=(c == DC - 1))
        last.then_inc(step.product_done, 1)


def memory_copy(step, act, n, k, bank, s_read):
    nc = step.nc
    act.wait_ge(step.product_done, step.product_count(n))
    if k < DC:
        nc.scalar.activation(step.mem_k[:, k, :], step.ps[:, bank, 0:NMEM], ACT.Copy).then_inc(s_read, 1)
    else:
        out = step.mem_v[:, :, (k - DC) * P:(k - DC + 1) * P]
        nc.scalar.activation(out, step.ps[:, bank, 0:NMEM].rearrange("p (m f) -> p m f", m=NMEM // P),
                             ACT.Copy).then_inc(s_read, 1)


def hgrn_pool_mixer(step, layer):
    nc, io, ps = step.nc, step.io, step.ps
    H4 = HEADS_A
    NP, NS = H4 * TP, H4 * TS
    base = step.used
    with ExitStack() as ctx:
        def sb(name, shape, c=ctx):
            return step.sb(name, shape, ctx=c)

        qs = sb("silu_q", [P, NP + NS])
        fg = sb("forget_gate", [P, NP + NS])
        kk = sb("key_gate", [P, NP + NS])
        lf = sb("log_forget", [P, NP + NS])
        vi = sb("value_i", [P, NP + NS])
        sg = sb("silu_g", [P, NP + NS])
        out_h = sb("hgrn_out", [P, NP + NS])
        u_ext = sb("pool_prompt_ext", [P, H4, CTX + TP])
        s_ext = sb("pool_sample_ext", [P, H4, TS, CTX + 1])
        gam = sb("gamma_T", [P, 2, H4])
        lbt = sb("lower_bound", [P, 6, H4])
        ng = sb("norm_gain", [P, H4])
        psc = sb("pool_scale_T", [P, H4])
        pw = sb("pool_weights", [P, H4, P])
        inv = sb("window_inverse", [P, H4, T])
        smask = sb("scan_mask", [P, TP])
        s0 = sb("sample_state", [P, NS, P])
        mem = sb("memory_T", [P, DC, NMEM])
        params = step.sem("mixer_params_ready")
        late = step.sem("mixer_late_params_ready")
        lb, oml = lbt[:, 4, :], lbt[:, 5, :]

        with ExitStack() as c1, nc.Block("mixer_in", no_gpsimd_drain=True) as block:
            sig = sb("sigmoids", [P, 2, T], c1)
            s_sig = step.sem("sigmoid_ready")
            s_use = step.sem("sigmoid_used")
            s_cp = step.sem("chunk_copied")
            order = ["q"] * 4 + ["f"] * 4 + ["g"] * 4 + ["i"] * 4 + ["u"] * 4
            N_SIG = 12

            @block.sync
            def _(sp):
                for dst, name in ((gam, "gamma"), (ng, "norm_g"), (psc, "pool_scale")):
                    sp.dma_start(dst[:], io[name]).then_inc(params, 16)
                step.load_until(sp, base + 20 + SLOTS)

            @block.gpsimd
            def _(pool):
                for dst, name in ((pw[:], "pool_w"), (inv[:], "inv_count"), (smask[:], "scan_mask"),
                                  (s_ext[:, :, :, 0:CTX], "pool_ctx"), (mem[:], "mem"), (s0[:], "state")):
                    pool.dma_start(dst, io[name]).then_inc(late, 16)
                step.link(pool, "gpsimd", nc.gpsimd.memset(u_ext[:, :, 0:CTX], 0.0))

            @block.tensor
            def _(pe):
                for j in range(20):
                    if 4 <= j < N_SIG + 4:
                        pe.wait_ge(s_use, j - 3)
                    elif j >= N_SIG + 4:
                        pe.wait_ge(s_cp, j - 3 - N_SIG)
                    product(step, pe, base + j, j % 4, step.x[:])

            @block.scalar
            def _(act):
                act.wait_ge(params, 48)
                act.wait_ge(step.vector_done, step.count["vector"] + 2)
                nc.scalar.activation(lbt[:, 1:3, :], lbt[:, 1:3, :], ACT.Exp).then_inc(s_sig, 1)
                for j, what in enumerate(order):
                    act.wait_ge(step.product_done, step.product_count(base + j))
                    bank, h = ps[:, j % 4, :], j % 4
                    if j < N_SIG:
                        if j >= 2:
                            act.wait_ge(s_use, j - 1)
                        nc.scalar.activation(sig[:, j % 2, :], bank[:, 0:T], ACT.Sigmoid).then_inc(s_sig, 1)
                    elif what == "i":
                        nc.scalar.activation(vi[:, h * TP:(h + 1) * TP], bank[:, 0:TP], ACT.Copy)
                        nc.scalar.activation(vi[:, NP + h * TS:NP + (h + 1) * TS], bank[:, TP:T],
                                             ACT.Copy).then_inc(s_cp, 1)
                    else:
                        nc.scalar.activation(u_ext[:, h, CTX:CTX + TP], bank[:, 0:TP], ACT.Copy)
                        nc.scalar.activation(s_ext[:, h, :, CTX], bank[:, TP:T], ACT.Copy).then_inc(s_cp, 1)

            @block.vector
            def _(dve):
                link = lambda ins, wait=True: step.link(dve, "vector", ins, wait)
                dve.wait_ge(params, 48)
                link(nc.vector.tensor_tensor(lbt[:, 0, :], gam[:, 0, :], gam[:, 1, :], ALU.max))
                link(nc.vector.tensor_tensor(lbt[:, 1:3, :], gam[:], lbt[:, 0:1, :].to_broadcast([P, 2, H4]),
                                             ALU.subtract))
                dve.wait_ge(s_sig, 1)
                link(nc.vector.tensor_tensor(lbt[:, 3, :], lbt[:, 1, :], lbt[:, 2, :], ALU.add))
                link(nc.vector.reciprocal(lbt[:, 3, :], lbt[:, 3, :]))
                link(nc.vector.tensor_tensor(lb, lbt[:, 1, :], lbt[:, 3, :], ALU.mult))
                link(nc.vector.tensor_scalar(oml, lb, -1.0, 1.0, ALU.mult, ALU.add))
                for j, what in enumerate(order[:N_SIG]):
                    dve.wait_ge(s_sig, j + 2)
                    h, sj = j % 4, sig[:, j % 2, :]
                    for lo, hi, a, b in ((0, TP, h * TP, (h + 1) * TP), (TP, T, NP + h * TS, NP + (h + 1) * TS)):
                        if what == "f":
                            last = nc.vector.tensor_scalar(fg[:, a:b], sj[:, lo:hi], oml[:, h:h + 1], lb[:, h:h + 1],
                                                           ALU.mult, ALU.add)
                        else:
                            dst = qs if what == "q" else sg
                            last = nc.vector.tensor_tensor(dst[:, a:b], sj[:, lo:hi], ps[:, j % 4, lo:hi], ALU.mult)
                    last.then_inc(s_use, 1)
        step.used += 20

        base = step.used
        with ExitStack() as ctx2:
            cum = sb("cumulative_log", [P, NP], ctx2)
            ecum = sb("exp_cumulative", [P, NP], ctx2)
            qe = sb("q_decayed", [P, NP], ctx2)
            kd = sb("k_to_block_end", [P, NP], ctx2)
            with ExitStack() as c1, nc.Block("mixer_lags", no_gpsimd_drain=True) as block:
                dif = sb("lag_decay", [P, 2, NP], c1)
                qk = sb("lag_qk", [P, 2, NP], c1)
                pr = sb("lag_product", [P, 2, NP], c1)
                term = sb("lag_term", [P, 2, NP], c1)
                s_ln = step.sem("log_ready")
                s_b = step.sem("cumulative_ready")
                s_eb = step.sem("exp_cumulative_ready")
                s_kd = step.sem("block_end_decay_ready")
                s_ekd = step.sem("block_end_exp_ready")
                s_dif = step.sem("lag_difference_ready")
                s_edif = step.sem("lag_exp_ready")
                s_qk = step.sem("lag_qk_ready")
                s_pr = step.sem("lag_product_ready")
                s_att = step.sem("lag_attention_ready")
                s_term = step.sem("lag_term_ready")
                s_sum = step.sem("lag_term_added")
                s_mem = step.sem("memory_chunk_copied")
                blocks = lambda ap: ap.rearrange("p (n t) -> p n t", t=BLK)
                prompt = lambda t: blocks(t[:, 0:NP])
                LAG = [BLK - j for j in range(BLK)]
                HALF = NP // BLK // 2
                packed = lambda t, j: t[:, j % 2, 0:2 * HALF * LAG[j]].rearrange("p (n t) -> p n t", t=LAG[j])

                @block.sync
                def _(sp):
                    step.load_until(sp, base + 16 + SLOTS)

                @block.tensor
                def _(pe):
                    pe.wait_ge(late, 96)
                    for j in range(BLK):
                        memory_product(step, pe, base + j, j, mem, 4 + j % 2, s_mem)
                        pe.wait_ge(s_pr, j + 1)
                        if j >= 2:
                            pe.wait_ge(s_term, j - 1)
                        for half in range(2):
                            w = HALF * LAG[j]
                            last = nc.tensor.matmul(ps[:, 2 * (j % 2) + half, 0:w], step.ones,
                                                    pr[:, j % 2, half * w:(half + 1) * w], start=True, stop=True)
                        last.then_inc(s_att, 1)

                @block.scalar
                def _(act):
                    nc.scalar.activation(lf[:], fg[:], ACT.Ln).then_inc(s_ln, 1)
                    act.wait_ge(s_b, 1)
                    nc.scalar.activation(ecum[:], cum[:], ACT.Exp).then_inc(s_eb, 1)
                    act.wait_ge(s_kd, 1)
                    nc.scalar.activation(kd[:], kd[:], ACT.Exp).then_inc(s_ekd, 1)
                    for j in range(BLK):
                        if j:
                            act.wait_ge(s_dif, j)
                            nc.scalar.activation(packed(dif, j), packed(dif, j), ACT.Exp).then_inc(s_edif, 1)
                        memory_copy(step, act, base + j, j, 4 + j % 2, s_mem)

                @block.gpsimd
                def _(pool):
                    def make_qk(j):
                        if j >= 2:
                            pool.wait_ge(s_pr, j - 1)
                        nc.gpsimd.tensor_tensor(packed(qk, j), prompt(qs)[:, :, j:], prompt(kk)[:, :, :LAG[j]],
                                                ALU.mult).then_inc(s_qk, 1)
                    pool.wait_ge(s_kd, 1)
                    make_qk(0)
                    make_qk(1)
                    for j in range(1, BLK):
                        if j + 1 < BLK:
                            make_qk(j + 1)
                        pool.wait_ge(s_term, j + 1)
                        if j >= 2:
                            pool.wait_ge(s_sum, j - 1)
                        o = prompt(out_h)[:, :, j:]
                        nc.gpsimd.tensor_tensor(o, o, packed(term, j), ALU.add).then_inc(s_sum, 1)
                    pool.wait_ge(s_sum, BLK - 1)

                @block.vector
                def _(dve):
                    link = lambda ins, wait=True: step.link(dve, "vector", ins, wait)
                    dve.wait_ge(late, 96)
                    link(nc.vector.tensor_scalar(kk[:], fg[:], -1.0, 1.0, ALU.mult, ALU.add))
                    dve.wait_ge(s_ln, 1)
                    for h in range(H4):
                        cols = slice(h * TP, (h + 1) * TP)
                        last = nc.vector.tensor_tensor_scan(cum[:, cols], smask[:], lf[:, cols], 0.0,
                                                            ALU.mult, ALU.add)
                    last.then_inc(s_b, 1)
                    dve.wait_ge(s_b, 1)
                    cb = blocks(cum[:])
                    ends = cb[:, :, BLK - 1:BLK].to_broadcast([P, NP // BLK, BLK])
                    nc.vector.tensor_tensor(blocks(kd[:]), ends, cb, ALU.subtract).then_inc(s_kd, 1)
                    dve.wait_ge(s_eb, 1)
                    nc.vector.tensor_tensor(qe[:], qs[:, 0:NP], ecum[:], ALU.mult)
                    dve.wait_ge(s_ekd, 1)
                    link(nc.vector.tensor_tensor(kd[:], kd[:], kk[:, 0:NP], ALU.mult))

                    def difference(j):
                        if j >= 3:
                            dve.wait_ge(s_pr, j - 1)
                        nc.vector.tensor_tensor(packed(dif, j), cb[:, :, j:], cb[:, :, :LAG[j]],
                                                ALU.subtract).then_inc(s_dif, 1)

                    def accumulate(j):
                        dve.wait_ge(s_att, j + 1)
                        if j >= 3:
                            dve.wait_ge(s_sum, j - 2)
                        for half in range(2):
                            w = HALF * LAG[j]
                            a = ps[:, 2 * (j % 2) + half, 0:w].rearrange("p (n t) -> p n t", t=LAG[j])
                            v = prompt(vi)[:, half * HALF:(half + 1) * HALF, :LAG[j]]
                            if j == 0:
                                dst = prompt(out_h)[:, half * HALF:(half + 1) * HALF, :]
                            else:
                                dst = packed(term, j)[:, half * HALF:(half + 1) * HALF, :]
                            last = nc.vector.tensor_tensor(dst, a, v, ALU.mult)
                        last.then_inc(s_term, 1)

                    difference(1)
                    for j in range(BLK):
                        if j + 1 < BLK and j >= 1:
                            difference(j + 1)
                        dve.wait_ge(s_qk, j + 1)
                        if j >= 2:
                            dve.wait_ge(s_att, j - 1)
                        if j == 0:
                            nc.vector.tensor_copy(pr[:, 0, :], qk[:, 0, :]).then_inc(s_pr, 1)
                        else:
                            dve.wait_ge(s_edif, j)
                            w = 2 * HALF * LAG[j]
                            nc.vector.scalar_tensor_tensor(out=pr[:, j % 2, 0:w], in0=dif[:, j % 2, 0:w], scalar=1.0,
                                                           in1=qk[:, j % 2, 0:w], op0=ALU.min,
                                                           op1=ALU.mult).then_inc(s_pr, 1)
                        if j >= 1:
                            accumulate(j - 1)
                    accumulate(BLK - 1)
            step.used += 16

            with ExitStack() as c1, nc.Block("mixer_chain", no_gpsimd_drain=True) as block:
                tok = sb("token_major", [BLK, 2, 2, H4 * P], c1)
                state = sb("state", [P, 3, H4, P], c1)
                diag = sb("diagonal_values", [P, NS, P], c1)
                s_tr = step.sem("block_transposed")
                s_ck = step.sem("block_keys_copied")
                s_cv = step.sem("block_values_copied")
                s_up = step.sem("block_update_ready")
                s_st = step.sem("state_ready")
                s_oi = step.sem("inter_block_ready")
                s_dg = step.sem("diagonal_ready")
                s_fs = step.sem("sample_state_decayed")
                s_vb = step.sem("sample_values_spread")
                s_kv = step.sem("sample_outer_product_ready")
                s_os = step.sem("sample_out_ready")
                SPREAD = NS * P // 512

                @block.sync
                def _(sp):
                    for k in range(DC):
                        step.store(sp, io["mem_k_out"][layer, :, k, :], step.mem_k[:, k, :])
                    step.store(sp, io["mem_v_out"][layer], step.mem_v[:])
                    sp.wait_ge(s_st, H4 * NBLK)
                    step.store(sp, io["hgrn_prompt"], state[:, NBLK % 3, :, :])
                    sp.wait_ge(s_kv, 2 * SPREAD)
                    step.store(sp, io["hgrn_sample"], s0[:])

                @block.tensor
                def _(pe):
                    def transposes(n):
                        if n >= 1:
                            pe.wait_ge(s_ck, n)
                            pe.wait_ge(s_cv, n)
                        for which, src in enumerate((kd, vi)):
                            for h in range(H4):
                                cols = slice(h * TP + n * BLK, h * TP + (n + 1) * BLK)
                                last = nc.tensor.transpose(ps[0:BLK, 6 + which, h * P:(h + 1) * P], src[:, cols],
                                                           step.ident)
                        last.then_inc(s_tr, 1)
                    transposes(0)
                    for n in range(NBLK):
                        if n + 1 < NBLK:
                            transposes(n + 1)
                        pe.wait_ge(s_ck, n + 1)
                        pe.wait_ge(s_cv, n + 1)
                        if n >= 2:
                            pe.wait_ge(s_st, H4 * (n - 1))
                        for h in range(H4):
                            nc.tensor.matmul(ps[:, n % 2, h * P:(h + 1) * P], tok[:, n % 2, 0, h * P:(h + 1) * P],
                                             tok[:, n % 2, 1, h * P:(h + 1) * P], start=True, stop=True).then_inc(s_up, 1)
                        if n:
                            for h in range(H4):
                                pe.wait_ge(s_st, H4 * (n - 1) + h + 1)
                                col = (h % 2) * TP + n * BLK
                                nc.tensor.matmul(ps[:, 2 + h // 2, col:col + BLK], state[:, n % 3, h, :],
                                                 qe[:, h * TP + n * BLK:h * TP + (n + 1) * BLK],
                                                 start=True, stop=True).then_inc(s_oi, 1)
                    for k in range(SPREAD):
                        pe.wait_ge(s_dg, 1)
                        if k >= 2:
                            pe.wait_ge(s_kv, 2 * (k - 1) - 1)
                        nc.tensor.matmul(ps[:, 4 + k % 2, :], step.ones,
                                         diag[:, 4 * k:4 * k + 4, :].rearrange("p a b -> p (a b)"),
                                         start=True, stop=True).then_inc(s_vb, 1)
                    pe.wait_ge(s_kv, 2 * SPREAD)
                    pe.wait_ge(s_ck, NBLK)
                    pe.wait_ge(s_cv, NBLK)
                    for c in range(NS):
                        last = nc.tensor.matmul(ps[:, 6, c:c + 1], s0[:, c, :], qs[:, NP + c:NP + c + 1],
                                                start=True, stop=True)
                    last.then_inc(s_os, 1)

                @block.scalar
                def _(act):
                    for n in range(NBLK):
                        act.wait_ge(s_tr, n + 1)
                        if n >= 2:
                            act.wait_ge(s_up, H4 * (n - 1))
                        nc.scalar.activation(tok[:, n % 2, 0, :], ps[0:BLK, 6, :], ACT.Copy).then_inc(s_ck, 1)

                @block.gpsimd
                def _(pool):
                    nc.gpsimd.tensor_tensor(diag[:], step.ident.unsqueeze(1).to_broadcast([P, NS, P]),
                                            vi[:, NP:NP + NS].unsqueeze(2).to_broadcast([P, NS, P]),
                                            ALU.mult).then_inc(s_dg, 1)
                    nc.gpsimd.tensor_tensor(s0[:], s0[:], fg[:, NP:NP + NS].unsqueeze(2).to_broadcast([P, NS, P]),
                                            ALU.mult).then_inc(s_fs, 1)
                    pool.wait_ge(s_fs, 1)

                @block.vector
                def _(dve):
                    for n in range(NBLK):
                        def copy_values(m):
                            dve.wait_ge(s_tr, m + 1)
                            if m >= 2:
                                dve.wait_ge(s_up, H4 * (m - 1))
                            nc.vector.tensor_copy(tok[:, m % 2, 1, :], ps[0:BLK, 7, :]).then_inc(s_cv, 1)
                        if n == 0:
                            copy_values(0)
                        if n + 1 < NBLK:
                            copy_values(n + 1)
                        for h in range(H4):
                            dve.wait_ge(s_up, H4 * (n + 1))
                            if n == 0:
                                ins = nc.vector.tensor_copy(state[:, 1, h, :], ps[:, 0, h * P:(h + 1) * P])
                            else:
                                dve.wait_ge(s_st, H4 * (n - 1) + h + 1)
                                if n >= 3:
                                    dve.wait_ge(s_oi, H4 * (n - 3) + h + 1)
                                end = h * TP + (n + 1) * BLK - 1
                                ins = nc.vector.scalar_tensor_tensor(
                                    out=state[:, (n + 1) % 3, h, :], in0=state[:, n % 3, h, :],
                                    scalar=ecum[:, end:end + 1], in1=ps[:, n % 2, h * P:(h + 1) * P],
                                    op0=ALU.mult, op1=ALU.add)
                            ins.then_inc(s_st, 1)
                    link = lambda ins, wait=True: step.link(dve, "vector", ins, wait)
                    dve.wait_ge(s_oi, H4 * (NBLK - 1))
                    for h in range(H4):
                        o = out_h[:, h * TP + BLK:(h + 1) * TP]
                        nc.vector.tensor_tensor(o, o, ps[:, 2 + h // 2, (h % 2) * TP + BLK:(h % 2 + 1) * TP], ALU.add)
                    dve.wait_ge(s_fs, 1)
                    for k in range(SPREAD):
                        dve.wait_ge(s_vb, k + 1)
                        part = diag[:, 4 * k:4 * k + 4, :]
                        nc.vector.tensor_tensor(part, ps[:, 4 + k % 2, :].rearrange("p (a b) -> p a b", a=4),
                                                kk[:, NP + 4 * k:NP + 4 * k + 4].unsqueeze(2).to_broadcast([P, 4, P]),
                                                ALU.mult).then_inc(s_kv, 1)
                        dve.wait_ge(s_kv, 2 * k + 1)
                        st = s0[:, 4 * k:4 * k + 4, :]
                        nc.vector.tensor_tensor(st, st, part, ALU.add).then_inc(s_kv, 1)
                    dve.wait_ge(s_os, 1)
                    nc.vector.tensor_copy(out_h[:, NP:NP + NS], ps[:, 6, 0:NS])

        with ExitStack() as c1, nc.Block("mixer_gate", no_gpsimd_drain=True) as block:
            sq = sb("head_squares", [P, NP + NS], c1)
            win = sb("window_sums", [P, 2, H4, CTX + TP], c1)
            pooled = sb("pooled", [P, H4, T], c1)
            sums = sb("sample_window_sums", [P, H4, TS], c1)
            s_sq = step.sem("head_squares_ready")
            s_ms = step.sem("head_mean_ready")
            s_sd = step.sem("head_deviation_ready")
            s_win = step.sem("window_sums_ready")
            s_pool = step.sem("pooled_ready")
            s_py = step.sem("pool_product_ready")
            PARTS = ((0, 512), (512, NP), (NP, NP + NS))

            @block.sync
            def _(sp):
                step.store(sp, io["pool_prompt"], u_ext[:, :, TP:TP + CTX])
                step.store(sp, io["pool_sample"], s_ext[:, :, :, 1:CTX + 1])

            @block.gpsimd
            def _(pool):
                src, first = u_ext, 0
                for lev in range(H4):
                    shift = 1 << lev
                    first += shift
                    dst = win[:, lev % 2]
                    if lev:
                        pool.wait_ge(s_win, lev)
                    nc.gpsimd.tensor_tensor(dst[:, lev:, first:], src[:, lev:, first:],
                                            src[:, lev:, first - shift:CTX + TP - shift], ALU.add).then_inc(s_win, 1)
                    pool.wait_ge(s_win, lev + 1)
                    step.link(pool, "gpsimd", nc.gpsimd.tensor_tensor(
                        pooled[:, lev, 0:TP], dst[:, lev, CTX:], inv[:, lev, 0:TP], ALU.mult))
                    src = dst
                nc.gpsimd.tensor_tensor(pooled[:, :, 0:TP], pooled[:, :, 0:TP], u_ext[:, :, CTX:],
                                        ALU.subtract).then_inc(s_pool, 1)
                pool.wait_ge(s_pool, 2)

            @block.tensor
            def _(pe):
                pe.wait_ge(s_sq, 1)
                for k, (a, b) in enumerate(PARTS):
                    last = nc.tensor.matmul(ps[:, k, 0:b - a], step.mean_head, sq[:, a:b], start=True, stop=True)
                last.then_inc(s_ms, 1)
                pe.wait_ge(s_pool, 2)
                for g in range(H4):
                    nc.tensor.matmul(ps[:, 4 + g, 0:T], pw[:, g, :], pooled[:, g, :], start=True,
                                     stop=True).then_inc(s_py, 1)

            @block.scalar
            def _(act):
                nc.scalar.activation(sq[:], out_h[:], ACT.Square).then_inc(s_sq, 1)
                act.wait_ge(s_ms, 1)
                for k, (a, b) in enumerate(PARTS):
                    last = nc.scalar.activation(sq[:, a:b], ps[:, k, 0:b - a], ACT.Sqrt, bias=step.eps)
                last.then_inc(s_sd, 1)
                for g in range(H4):
                    act.wait_ge(s_py, g + 1)
                    nc.scalar.activation(step.mixed[:, H4 + g, :], ps[:, 4 + g, 0:T], ACT.Copy, scale=psc[:, g:g + 1])

            @block.vector
            def _(dve):
                link = lambda ins, wait=True: step.link(dve, "vector", ins, wait)
                for g, w in enumerate(POOL_SIZES):
                    last = nc.vector.reduce_sum(sums[:, g, :], s_ext[:, g, :, CTX + 1 - w:], axis=AX)
                link(last)
                link(nc.vector.tensor_tensor(sums[:], sums[:], inv[:, :, TP:T], ALU.mult))
                nc.vector.tensor_tensor(pooled[:, :, TP:T], sums[:], s_ext[:, :, :, CTX],
                                        ALU.subtract).then_inc(s_pool, 1)
                dve.wait_ge(s_sd, 1)
                link(nc.vector.reciprocal(sq[:], sq[:]))
                link(nc.vector.tensor_tensor(out_h[:], out_h[:], sq[:], ALU.mult))
                for h in range(H4):
                    for lo, hi, a, b in ((0, TP, h * TP, (h + 1) * TP), (TP, T, NP + h * TS, NP + (h + 1) * TS)):
                        nc.vector.scalar_tensor_tensor(out=step.mixed[:, h, lo:hi], in0=out_h[:, a:b],
                                                       scalar=ng[:, h:h + 1], in1=sg[:, a:b],
                                                       op0=ALU.mult, op1=ALU.mult)


def window_mixer(step, layer):
    nc, io, ps = step.nc, step.io, step.ps
    base = step.used
    with ExitStack() as ctx:
        def sb(name, shape, c=ctx):
            return step.sb(name, shape, ctx=c)
        kT = sb("window_k_T", [P, KV, T])
        vt = sb("window_v", [P, 2, KV, P])
        vs = sb("window_v_sample", [TS, KV, P])
        kx = sb("sample_k_T", [P, TS, KV, P])
        vx = sb("sample_v", [P, TS, KV, P])
        snk = sb("sinks", [P, HEADS_C + 1])
        nsnk = sb("negative_sinks", [P, HEADS_C + 1])
        mem = sb("memory_T1", [P, DC, NMEM])
        late = step.sem("window_inputs_ready")
        s_vrow = step.sem("sample_value_row_stored")

        with nc.Block("window_in", no_gpsimd_drain=True) as block:
            s_cp = step.sem("window_chunk_copied")

            @block.sync
            def _(sp):
                step.load_until(sp, base + 12 + SLOTS)

            @block.gpsimd
            def _(pool):
                for dst, name in ((snk[:], "sinks"), (mem[:], "mem"), (kx[:, :, :, 0:P - 1], "window_k"),
                                  (vx[0:P - 1], "window_v")):
                    pool.dma_start(dst, io[name]).then_inc(late, 16)

            @block.tensor
            def _(pe):
                for j in range(12):
                    if j >= 4:
                        pe.wait_ge(s_cp, j - 3)
                    if j < 10:
                        product(step, pe, base + j, j % 4, step.x[:])
                        continue
                    step.wait_slab(pe, base + j)
                    w = step.slab(base + j)
                    for t, (a, b) in enumerate(((0, P), (P, TP), (TP, T))):
                        for c in range(DC):
                            last = nc.tensor.matmul(ps[0:b - a, j % 4, t * P:(t + 1) * P], step.x[:, c, a:b], w[:, c, :],
                                                    start=(c == 0), stop=(c == DC - 1))
                    last.then_inc(step.product_done, 1)

            @block.scalar
            def _(act):
                for j in range(12):
                    act.wait_ge(step.product_done, step.product_count(base + j))
                    if j < 8:
                        ins = nc.scalar.activation(step.q[:, j, :], ps[:, j % 4, 0:T], ACT.Copy, scale=HD ** -0.5)
                    elif j < 10:
                        ins = nc.scalar.activation(kT[:, j - 8, :], ps[:, j % 4, 0:T], ACT.Copy)
                    else:
                        nc.scalar.activation(vt[:, :, j - 10, :], ps[:, j % 4, 0:TP].rearrange("p (a b) -> p a b", a=2),
                                             ACT.Copy)
                        ins = nc.scalar.activation(vs[:, j - 10, :], ps[0:TS, j % 4, TP:TP + P], ACT.Copy)
                    ins.then_inc(s_cp, 1)
        step.used += 12

        base = step.used
        with ExitStack() as c1, nc.Block("window_prompt", no_gpsimd_drain=True) as block:
            sc = sb("scores", [P, 2, 3 * P], c1)
            pt = sb("probabilities_T", [P, 2, 3 * P], c1)
            neg = sb("negative_maxima", [P, 2, 2], c1)
            den = sb("denominators", [P, 2, 2], c1)
            esk = sb("sink_terms", [P, 2, 2], c1)
            s_s = step.sem("window_scores_ready")
            s_mk = step.sem("window_scores_masked")
            s_m = step.sem("window_maxima_ready")
            s_e = step.sem("window_exp_ready")
            s_p = step.sem("window_probabilities_ready")
            s_t = step.sem("window_transposed")
            s_pt = step.sem("window_transposed_copied")
            s_o = step.sem("window_output_ready")
            s_oc = step.sem("window_output_copied")
            s_mem = step.sem("memory_chunk_copied1")
            QK = ((0, P), (P, 3 * P))

            @block.sync
            def _(sp):
                sp.dma_start(vx[P - 1:P], vs[:]).then_inc(s_vrow, 16)
                step.store(sp, io["window_k_prompt"], kT[0:HD, :, P:TP])
                step.store(sp, io["window_v_prompt"], vt[:, 1, :, 0:HD])
                step.load_until(sp, base + 16 + SLOTS)

            @block.tensor
            def _(pe):
                def scores(h):
                    e, j, kv = h % 2, h // 2, h // (HEADS_C // KV)
                    rows = slice(e * HD, (e + 1) * HD)
                    if h >= 2:
                        pe.wait_ge(s_mk, h - 1)
                    nc.tensor.matmul(ps[:, h % 2, 0:P], step.q[rows, j, 0:P], kT[rows, kv, 0:P], start=True, stop=True)
                    nc.tensor.matmul(ps[:, h % 2, P:3 * P], step.q[rows, j, P:TP], kT[rows, kv, 0:TP], start=True,
                                     stop=True).then_inc(s_s, 1)

                def transposes(h):
                    pe.wait_ge(s_p, h + 1)
                    if h >= 2:
                        pe.wait_ge(s_pt, h - 1)
                    for k in range(3):
                        last = nc.tensor.transpose(ps[:, 2 + h % 2, k * P:(k + 1) * P], sc[:, h % 2, k * P:(k + 1) * P],
                                                   step.ident)
                    last.then_inc(s_t, 1)

                def values(h):
                    kv = h // (HEADS_C // KV)
                    pe.wait_ge(s_pt, h + 1)
                    if h >= 2:
                        pe.wait_ge(s_oc, h - 1)
                    bank = ps[:, 4 + h % 2, :]
                    nc.tensor.matmul(bank[:, 0:P], vt[:, 0, kv, :], pt[:, h % 2, 0:P], start=True, stop=True)
                    nc.tensor.matmul(bank[:, P:TP], vt[:, 0, kv, :], pt[:, h % 2, P:2 * P], start=True, stop=False)
                    nc.tensor.matmul(bank[:, P:TP], vt[:, 1, kv, :], pt[:, h % 2, 2 * P:3 * P], start=False,
                                     stop=True).then_inc(s_o, 1)

                pe.wait_ge(late, 64)
                scores(0)
                for h in range(HEADS_C):
                    memory_product(step, pe, base + h, h, mem, 6 + h % 2, s_mem)
                    if h + 1 < HEADS_C:
                        scores(h + 1)
                    transposes(h)
                    if h:
                        values(h - 1)
                values(HEADS_C - 1)

            @block.vector
            def _(dve):
                link = lambda ins, wait=True: step.link(dve, "vector", ins, wait)
                dve.wait_ge(late, 64)
                link(nc.vector.tensor_scalar(nsnk[:], snk[:], -1.0, None, ALU.mult))

                def head_scores(h):
                    b = h % 2
                    dve.wait_ge(s_s, h + 1)
                    if h >= 2:
                        dve.wait_ge(s_t, h - 1)
                    nc.vector.tensor_tensor(sc[:, b, :], ps[:, b, 0:3 * P], step.masks, ALU.add).then_inc(s_mk, 1)
                    dve.wait_ge(s_mk, h + 1)
                    for t, (lo, hi) in enumerate(QK):
                        last = nc.vector.tensor_reduce(neg[:, b, t:t + 1], sc[:, b, lo:hi], AX, ALU.max, negate=True)
                    link(last)
                    nc.vector.tensor_scalar(neg[:, b, :], neg[:, b, :], nsnk[:, h:h + 1], None, ALU.min).then_inc(s_m, 1)

                def head_rest(h):
                    b = h % 2
                    dve.wait_ge(s_e, h + 1)
                    link(nc.vector.tensor_tensor(den[:, b, :], den[:, b, :], esk[:, b, :], ALU.add))
                    link(nc.vector.reciprocal(den[:, b, :], den[:, b, :]))
                    for t, (lo, hi) in enumerate(QK):
                        last = nc.vector.tensor_scalar(sc[:, b, lo:hi], sc[:, b, lo:hi], den[:, b, t:t + 1], None, ALU.mult)
                    last.then_inc(s_p, 1)

                def head_out(h):
                    e = h % 2
                    rows = slice(e * HD, (e + 1) * HD)
                    dve.wait_ge(s_o, h + 1)
                    nc.vector.tensor_copy(step.mixed[rows, h // 2, 0:TP], ps[rows, 4 + h % 2, 0:TP]).then_inc(s_oc, 1)

                for h in range(HEADS_C):
                    head_scores(h)
                    if h >= 1:
                        head_rest(h - 1)
                    if h >= 3:
                        head_out(h - 3)
                head_rest(HEADS_C - 1)
                for h in range(HEADS_C - 3, HEADS_C):
                    head_out(h)

            @block.scalar
            def _(act):
                def head_exp(h):
                    b = h % 2
                    act.wait_ge(s_m, h + 1)
                    if h >= 2:
                        act.wait_ge(s_p, h - 1)
                    for t, (lo, hi) in enumerate(QK):
                        nc.scalar.activation(sc[:, b, lo:hi], sc[:, b, lo:hi], ACT.Exp, bias=neg[:, b, t:t + 1],
                                             accum_out=den[:, b, t:t + 1])
                    nc.scalar.activation(esk[:, b, :], neg[:, b, :], ACT.Exp, bias=snk[:, h:h + 1]).then_inc(s_e, 1)

                def head_copy(h):
                    act.wait_ge(s_t, h + 1)
                    if h >= 2:
                        act.wait_ge(s_o, h - 1)
                    nc.scalar.activation(pt[:, h % 2, :], ps[:, 2 + h % 2, 0:3 * P], ACT.Copy).then_inc(s_pt, 1)

                for h in range(HEADS_C):
                    head_exp(h)
                    if h:
                        head_copy(h - 1)
                    memory_copy(step, act, base + h, h, 6 + h % 2, s_mem)
                head_copy(HEADS_C - 1)
        step.used += 16

        with ExitStack() as c1, nc.Block("window_sample", no_gpsimd_drain=True) as block:
            st = sb("sample_scores_T", [P, P], c1)
            ss = sb("sample_scores", [P, P], c1)
            sp_t = sb("sample_probabilities_T", [P, P], c1)
            sm = sb("sample_small", [P, 3], c1)
            s_k = step.sem("sample_key_column_ready")
            s_s = step.sem("sample_scores_T_ready")
            s_sc = step.sem("sample_scores_T_copied")
            s_t = step.sem("sample_scores_ready")
            s_m = step.sem("sample_maxima_ready")
            s_e = step.sem("sample_exp_ready")
            s_p = step.sem("sample_probabilities_ready")
            s_pt = step.sem("sample_probabilities_T_ready")
            s_pc = step.sem("sample_probabilities_T_copied")
            s_o = step.sem("sample_output_ready")

            @block.sync
            def _(sp):
                for k in range(DC):
                    step.store(sp, io["mem_k_out"][layer, :, k, :], step.mem_k[:, k, :])
                step.store(sp, io["mem_v_out"][layer], step.mem_v[:])
                sp.wait_ge(s_k, 1)
                step.store(sp, io["window_k_sample"], kx[0:HD])
                sp.wait_ge(s_vrow, 16)
                step.store(sp, io["window_v_sample"], vx[:, :, :, 0:HD])

            @block.tensor
            def _(pe):
                pe.wait_ge(s_k, 1)
                for b in range(TS):
                    for kv in range(KV):
                        for e in range(2):
                            rows = slice(e * HD, (e + 1) * HD)
                            col = (b * KV + kv) * 4
                            last = nc.tensor.matmul(ps[:, 4 * e, col:col + 4], kx[rows, b, kv, :],
                                                    step.q[rows, kv * 4:kv * 4 + 4, TP + b], start=True, stop=True)
                last.then_inc(s_s, 1)
                pe.wait_ge(s_sc, 1)
                nc.tensor.transpose(ps[:, 1, 0:P], st[:], step.ident).then_inc(s_t, 1)
                pe.wait_ge(s_p, 1)
                nc.tensor.transpose(ps[:, 2, 0:P], ss[:], step.ident).then_inc(s_pt, 1)
                pe.wait_ge(s_pc, 1)
                pe.wait_ge(s_vrow, 16)
                for b in range(TS):
                    for kv in range(KV):
                        col = (b * KV + kv) * 8
                        last = nc.tensor.matmul(ps[:, 3, col:col + 8], vx[:, b, kv, :], sp_t[:, col:col + 8],
                                                start=True, stop=True)
                last.then_inc(s_o, 1)

            @block.scalar
            def _(act):
                act.wait_ge(s_m, 1)
                nc.scalar.activation(ss[:], ss[:], ACT.Exp, bias=sm[:, 0:1], accum_out=sm[:, 1:2])
                nc.scalar.activation(sm[:, 2:3], sm[:, 0:1], ACT.Exp, bias=snk[:, HEADS_C:]).then_inc(s_e, 1)
                act.wait_ge(s_pt, 1)
                nc.scalar.activation(sp_t[:], ps[:, 2, 0:P], ACT.Copy).then_inc(s_pc, 1)

            @block.vector
            def _(dve):
                link = lambda ins, wait=True: step.link(dve, "vector", ins, wait)
                nc.vector.tensor_copy(kx[:, :, :, P - 1], kT[:, :, TP:T].rearrange("p k b -> p b k")).then_inc(s_k, 1)
                dve.wait_ge(s_s, 1)
                for e in range(2):
                    last = nc.vector.tensor_copy(st[:].rearrange("p (g e j) -> p g e j", e=2, j=4)[:, :, e],
                                                 ps[:, 4 * e, 0:HD].rearrange("p (g j) -> p g j", j=4))
                last.then_inc(s_sc, 1)
                dve.wait_ge(s_t, 1)
                link(nc.vector.tensor_copy(ss[:], ps[:, 1, 0:P]))
                link(nc.vector.tensor_reduce(sm[:, 0:1], ss[:], AX, ALU.max, negate=True))
                nc.vector.tensor_scalar(sm[:, 0:1], sm[:, 0:1], nsnk[:, HEADS_C:], None, ALU.min).then_inc(s_m, 1)
                dve.wait_ge(s_e, 1)
                link(nc.vector.tensor_tensor(sm[:, 1:2], sm[:, 1:2], sm[:, 2:3], ALU.add))
                link(nc.vector.reciprocal(sm[:, 1:2], sm[:, 1:2]))
                nc.vector.tensor_scalar(ss[:], ss[:], sm[:, 1:2], None, ALU.mult).then_inc(s_p, 1)
                dve.wait_ge(s_o, 1)
                o = ps[:, 3, 0:P].rearrange("p (b k e j) -> p k e j b", b=TS, k=KV, e=2)
                dst = step.mixed[:].rearrange("p (k j) t -> p k j t", k=KV)
                for e in range(2):
                    rows = slice(e * HD, (e + 1) * HD)
                    nc.vector.tensor_copy(dst[rows, :, :, TP:T], o[rows, :, e])


def cross_attention(step, layer):
    nc, io, ps = step.nc, step.io, step.ps
    base = step.used
    L = f"_{layer}"
    with ExitStack() as ctx:
        BUF = 3
        ck = step.sb("cache_k_T" + L, [P, BUF, DC, NMEM], ctx=ctx)
        cv = step.sb("cache_v" + L, [P, BUF, 2, D], ctx=ctx)
        s_ck = [step.sem(f"cache_k_ready{b}{L}") for b in range(BUF)]
        s_cv = [step.sem(f"cache_v_ready{b}{L}") for b in range(BUF)]
        s_ku = step.sem("cache_k_used" + L)
        s_vu = step.sem("cache_v_used" + L)

        def load_k(pool, b):
            if b >= BUF:
                pool.wait_ge(s_ku, b - BUF + 1)
            pool.dma_start(ck[:, b % BUF], io["cache_k"][layer, b]).then_inc(s_ck[b % BUF], 16)

        def load_v(pool, b):
            if b >= BUF:
                pool.wait_ge(s_vu, b - BUF + 1)
            pool.dma_start(cv[:, b % BUF], io["cache_v"][layer, b]).then_inc(s_cv[b % BUF], 16)

        with nc.Block("cross_query" + L, no_gpsimd_drain=True) as block:
            s_cp = step.sem("query_chunk_copied" + L)

            @block.sync
            def _(sp):
                step.load_until(sp, base + DC + SLOTS)

            @block.gpsimd
            def _(pool):
                for b in range(BUF):
                    load_k(pool, b)
                    load_v(pool, b)

            @block.tensor
            def _(pe):
                for j in range(DC):
                    if j >= 4:
                        pe.wait_ge(s_cp, j - 3)
                    product(step, pe, base + j, j % 4, step.x[:])

            @block.scalar
            def _(act):
                for j in range(DC):
                    act.wait_ge(step.product_done, step.product_count(base + j))
                    nc.scalar.activation(step.q[:, j, :], ps[:, j % 4, 0:T], ACT.Copy, scale=MHD ** -0.5).then_inc(s_cp, 1)
        step.used += DC

        with ExitStack() as c1, nc.Block("cross_attention" + L, no_gpsimd_drain=True) as block:
            pr = step.sb("cross_p" + L, [P, 2, 2, NMEM], ctx=c1)
            pt = step.sb("cross_p_T" + L, [P, 2, 2, TP], ctx=c1)
            sm = step.sb("cross_small" + L, [P, 2, 2, 2], ctx=c1)
            NR = MH * TS
            sst = step.sb("cross_sample_scores_T" + L, [P, 2, NR], ctx=c1)
            ss = step.sb("cross_sample_p" + L, [NR, NMEM], ctx=c1)
            spt = step.sb("cross_sample_p_T" + L, [P, 2, NR], ctx=c1)
            ssm = step.sb("cross_sample_small" + L, [NR, 2], ctx=c1)
            s_s = step.sem("cross_scores_ready" + L)
            s_m = step.sem("cross_maxima_ready" + L)
            s_e = step.sem("cross_exp_ready" + L)
            s_p = step.sem("cross_probabilities_ready" + L)
            s_t = step.sem("cross_transposed" + L)
            s_pt = step.sem("cross_transposed_copied" + L)
            s_o = step.sem("cross_output_ready" + L)
            s_oc = step.sem("cross_output_copied" + L)
            s_sc = step.sem("cross_sample_scores_copied" + L)
            s_sx = step.sem("cross_sample_transposed" + L)
            s_sm = step.sem("cross_sample_maxima_ready" + L)
            s_se = step.sem("cross_sample_exp_ready" + L)
            s_sp = step.sem("cross_sample_probabilities_ready" + L)
            s_st = step.sem("cross_sample_probabilities_transposed" + L)
            s_sy = step.sem("cross_sample_probabilities_copied" + L)
            s_so = step.sem("cross_sample_output_ready" + L)

            @block.gpsimd
            def _(pool):
                for b in range(BUF, TS):
                    load_k(pool, b)
                for b in range(BUF, TS):
                    load_v(pool, b)

            @block.tensor
            def _(pe):
                def scores(h):
                    if h >= 2:
                        pe.wait_ge(s_e, h - 1)
                    for t in range(2):
                        for c in range(2):
                            last = nc.tensor.matmul(ps[:, h % 2, t * NMEM:(t + 1) * NMEM],
                                                    step.q[:, 2 * h + c, t * P:(t + 1) * P], step.mem_k[:, 2 * h + c, :],
                                                    start=(c == 0), stop=(c == 1))
                    last.then_inc(s_s, 1)

                def transposes(h):
                    pe.wait_ge(s_p, h + 1)
                    if h >= 2:
                        pe.wait_ge(s_pt, h - 1)
                    for m in range(2):
                        for t in range(2):
                            col = m * TP + t * P
                            last = nc.tensor.transpose(ps[:, 2 + h % 2, col:col + P], pr[:, h % 2, t, m * P:(m + 1) * P],
                                                       step.ident)
                    last.then_inc(s_t, 1)

                def values(h):
                    pe.wait_ge(s_pt, h + 1)
                    if h >= 2:
                        pe.wait_ge(s_oc, h - 1)
                    for d in range(2):
                        for m in range(2):
                            f = h * MHD + d * P
                            last = nc.tensor.matmul(ps[:, 4 + h % 2, d * TP:(d + 1) * TP], step.mem_v[:, m, f:f + P],
                                                    pt[:, h % 2, m, :], start=(m == 0), stop=(m == 1))
                    last.then_inc(s_o, 1)

                def sample_scores(b):
                    pe.wait_ge(s_ck[b % BUF], 16 * (b // BUF + 1))
                    for h in range(MH):
                        for m in range(2):
                            col = m * NR + b * MH + h
                            for c in range(2):
                                last = nc.tensor.matmul(ps[:, 6, col:col + 1], ck[:, b % BUF, 2 * h + c, m * P:(m + 1) * P],
                                                        step.q[:, 2 * h + c, TP + b:TP + b + 1],
                                                        start=(c == 0), stop=(c == 1))
                    last.then_inc(s_ku, 1)

                def sample_values(b):
                    pe.wait_ge(s_cv[b % BUF], 16 * (b // BUF + 1))
                    for h in range(MH):
                        for d in range(2):
                            f = h * MHD + d * P
                            col = 128 + (h * 2 + d) * TS + b
                            for m in range(2):
                                last = nc.tensor.matmul(ps[:, 6, col:col + 1], cv[:, b % BUF, m, f:f + P],
                                                        spt[:, m, b * MH + h:b * MH + h + 1], start=(m == 0), stop=(m == 1))
                    last.then_inc(s_vu, 1)

                scores(0)
                for h in range(MH):
                    if h + 1 < MH:
                        scores(h + 1)
                    sample_scores(2 * h)
                    transposes(h)
                    sample_scores(2 * h + 1)
                    values(h)
                pe.wait_ge(s_sc, 1)
                for m in range(2):
                    last = nc.tensor.transpose(ps[0:NR, 7, m * P:(m + 1) * P], sst[:, m, :], step.ident)
                last.then_inc(s_sx, 1)
                pe.wait_ge(s_sp, 1)
                for m in range(2):
                    last = nc.tensor.transpose(ps[:, 7, 256 + m * NR:256 + (m + 1) * NR], ss[:, m * P:(m + 1) * P],
                                               step.ident[0:NR, 0:NR])
                last.then_inc(s_st, 1)
                pe.wait_ge(s_sy, 1)
                for b in range(TS):
                    sample_values(b)

            @block.scalar
            def _(act):
                def head_exp(h):
                    act.wait_ge(s_m, h + 1)
                    if h >= 2:
                        act.wait_ge(s_t, h - 1)
                    for t in range(2):
                        last = nc.scalar.activation(pr[:, h % 2, t, :], ps[:, h % 2, t * NMEM:(t + 1) * NMEM], ACT.Exp,
                                                    bias=sm[:, h % 2, 0, t:t + 1], accum_out=sm[:, h % 2, 1, t:t + 1])
                    last.then_inc(s_e, 1)

                def head_copy(h):
                    act.wait_ge(s_t, h + 1)
                    if h >= 2:
                        act.wait_ge(s_o, h - 1)
                    nc.scalar.activation(pt[:, h % 2].rearrange("p a b -> p (a b)"), ps[:, 2 + h % 2, :],
                                         ACT.Copy).then_inc(s_pt, 1)
                for h in range(MH):
                    head_exp(h)
                    if h:
                        head_copy(h - 1)
                head_copy(MH - 1)
                act.wait_ge(s_sm, 1)
                nc.scalar.activation(ss[:], ps[0:NR, 7, 0:NMEM], ACT.Exp, bias=ssm[:, 0:1],
                                     accum_out=ssm[:, 1:2]).then_inc(s_se, 1)
                act.wait_ge(s_st, 1)
                nc.scalar.activation(spt[:].rearrange("p a b -> p (a b)"), ps[:, 7, 256:256 + 2 * NR],
                                     ACT.Copy).then_inc(s_sy, 1)

            @block.vector
            def _(dve):
                link = lambda ins, wait=True: step.link(dve, "vector", ins, wait)

                def head_max(h):
                    dve.wait_ge(s_s, h + 1)
                    if h >= 2:
                        dve.wait_ge(s_p, h - 1)
                    nc.vector.tensor_reduce(sm[:, h % 2, 0, :], ps[:, h % 2, :].rearrange("p (t m) -> p t m", t=2), AX,
                                            ALU.max, negate=True).then_inc(s_m, 1)

                def head_norm(h):
                    dve.wait_ge(s_e, h + 1)
                    link(nc.vector.reciprocal(sm[:, h % 2, 1, :], sm[:, h % 2, 1, :]))
                    for t in range(2):
                        last = nc.vector.tensor_scalar(pr[:, h % 2, t, :], pr[:, h % 2, t, :], sm[:, h % 2, 1, t:t + 1],
                                                       None, ALU.mult)
                    last.then_inc(s_p, 1)

                def head_out(h):
                    dve.wait_ge(s_o, h + 1)
                    nc.vector.tensor_copy(step.mixed[:, 2 * h:2 * h + 2, 0:TP],
                                          ps[:, 4 + h % 2, :].rearrange("p (d t) -> p d t", d=2)).then_inc(s_oc, 1)

                head_max(0)
                for h in range(MH):
                    if h + 1 < MH:
                        head_max(h + 1)
                    head_norm(h)
                    if h:
                        head_out(h - 1)
                head_out(MH - 1)
                dve.wait_ge(s_ku, TS)
                nc.vector.tensor_copy(sst[:].rearrange("p a b -> p (a b)"), ps[:, 6, 0:2 * NR]).then_inc(s_sc, 1)
                dve.wait_ge(s_sx, 1)
                nc.vector.tensor_reduce(ssm[:, 0:1], ps[0:NR, 7, 0:NMEM], AX, ALU.max, negate=True).then_inc(s_sm, 1)
                dve.wait_ge(s_se, 1)
                link(nc.vector.reciprocal(ssm[:, 1:2], ssm[:, 1:2]))
                nc.vector.tensor_scalar(ss[:], ss[:], ssm[:, 1:2], None, ALU.mult).then_inc(s_sp, 1)
                dve.wait_ge(s_vu, TS)
                nc.vector.tensor_copy(step.mixed[:, :, TP:T],
                                      ps[:, 6, 128:128 + DC * TS].rearrange("p (c b) -> p c b", c=DC))


TILES = ((0, P), (P, TP), (TP, T))


def peer(step, layer):
    nc, io, ps = step.nc, step.io, step.ps
    L = f"_{layer}"
    with ExitStack() as ctx:
        big = step.sb("expert_activations" + L, [P, NKEYS, T], ctx=ctx)
        qT = big[:, NKEYS - 2 * PH:, :]
        scratch = big[:, NKEYS - 80:NKEYS - 2 * PH, :].rearrange("p a b -> p (a b)")
        FIRST_BORROWED = NKEYS - 80
        pick = step.sb("selections" + L, [P, 3, 3, P], ctx=ctx)
        with ExitStack() as c1:
            xh = step.sb("x_hi" + L, [P, DC, T], F32R, ctx=c1)
            xl = step.sb("x_lo" + L, [P, DC, T], F32R, ctx=c1)
            keys_ready = step.sem("subkeys_ready" + L)
            peer_query(step, layer, qT, scratch[:, 0:2 * PH * P], xh, xl, keys_ready)
            peer_up(step, layer, big, qT, scratch, pick, xh, xl, keys_ready, FIRST_BORROWED)
        with ExitStack() as c1:
            selT = step.sb("selections_T" + L, [P, 3, T], ctx=c1)
            peer_gates(step, layer, big, pick, selT, c1)
        peer_down(step, layer, big)


def peer_query(step, layer, qT, keys, xh, xl, keys_ready):
    nc, io, ps = step.nc, step.io, step.ps
    L = f"_{layer}"
    base = step.used
    NQ = 2 * PH
    with nc.Block("peer_query" + L, no_gpsimd_drain=True) as block:
        s_cp = step.sem("peer_query_chunk_copied" + L)
        s_hi = step.sem("x_hi_ready" + L)

        @block.sync
        def _(sp):
            sp.dma_start(keys, io["subkeys"][layer]).then_inc(keys_ready, 16)
            step.load_until(sp, base + NQ + SLOTS)

        @block.tensor
        def _(pe):
            for j in range(NQ):
                if j >= 4:
                    pe.wait_ge(s_cp, j - 3)
                product(step, pe, base + j, j % 4, step.x[:])

        @block.scalar
        def _(act):
            nc.scalar.activation(xh[:], step.x[:], ACT.Copy).then_inc(s_hi, 1)
            for j in range(NQ):
                act.wait_ge(step.product_done, step.product_count(base + j))
                nc.scalar.activation(qT[:, j, :], ps[:, j % 4, 0:T], ACT.Copy).then_inc(s_cp, 1)

        @block.vector
        def _(dve):
            dve.wait_ge(s_hi, 1)
            nc.vector.tensor_tensor(xl[:], step.x[:], xh[:].bitcast(F32), ALU.subtract)
    step.used += NQ


def peer_up(step, layer, big, qT, scratch, pick, xh, xl, keys_ready, first_borrowed):
    nc, io, ps = step.nc, step.io, step.ps
    L = f"_{layer}"
    base = step.used
    ub = step.slabs[base][1]
    keys = scratch[:, 0:2 * PH * P].rearrange("p (k n) -> p k n", n=P)
    with ExitStack() as c1, nc.Block("peer_up" + L, no_gpsimd_drain=True) as block:
        hi = step.sb("u_hi" + L, [P, 2, DC, P], F32R, ctx=c1)
        lo = step.sb("u_lo" + L, [P, 2, DC, P], F32R, ctx=c1)
        s_hi = step.sem("u_hi_ready" + L)
        s_h = step.sem("up_product_ready" + L)
        s_g = step.sem("up_product_read" + L)
        s_sc = step.sem("routing_scores_ready" + L)
        s_sr = step.sem("routing_scores_read" + L)
        s_rt = step.sem("routing_done" + L)
        SPLIT = (0, 20, 44, NKEYS)

        @block.sync
        def _(sp):
            with sp.Fori(1, NKEYS // SLOTS) as i:
                for s in range(SLOTS):
                    sp.wait_ge(step.u_split, ub + SLOTS * i + s + 1 - SLOTS)
                    sp.dma_start(step.ring[:, s, :], io["u"][layer * P + SLOTS * i + s]).then_inc(step.slab_ready[s], 16)
            step.loaded = base + NKEYS
            step.load_until(sp, base + NKEYS + SLOTS)

        def ready(i):
            return 16 * (base // SLOTS + 1) + 16 * i

        @block.gpsimd
        def _(pool):
            def split(i, s, first):
                pool.wait_ge(s_hi, SLOTS * i + s + 1)
                nc.gpsimd.tensor_tensor(lo[:, s % 2], step.slab(s), hi[:, s % 2].bitcast(F32),
                                        ALU.subtract).then_inc(step.u_split, 1)
            for s in range(SLOTS):
                split(0, s, True)
            with pool.Fori(1, NKEYS // SLOTS) as i:
                for s in range(SLOTS):
                    split(i, s, False)
            pool.wait_ge(step.u_split, ub + NKEYS)

        @block.tensor
        def _(pe):
            def scores(t):
                a, b = TILES[t]
                if t:
                    pe.wait_ge(s_sr, t)
                else:
                    pe.wait_ge(keys_ready, 16)
                for k in range(2 * PH):
                    last = nc.tensor.matmul(ps[0:b - a, 2 + k // 4, (k % 4) * P:(k % 4 + 1) * P], qT[:, k, a:b], keys[:, k, :],
                                            start=True, stop=True)
                last.then_inc(s_sc, 1)

            def up(i, s, first):
                pe.wait_ge(step.u_split, ub + SLOTS * i + s + 1)
                if not (first and s < 2):
                    pe.wait_ge(s_g, SLOTS * i + s - 1)
                bank = ps[:, s % 2, 0:T]
                for c in range(DC):
                    nc.tensor.matmul(bank, hi[:, s % 2, c, :], xh[:, c, :], start=(c == 0), stop=False)
                    nc.tensor.matmul(bank, hi[:, s % 2, c, :], xl[:, c, :], start=False, stop=False)
                    last = nc.tensor.matmul(bank, lo[:, s % 2, c, :], xh[:, c, :], start=False, stop=(c == DC - 1))
                last.then_inc(s_h, 1)

            scores(0)
            for s in range(SLOTS):
                up(0, s, True)
            for t in range(3):
                if t:
                    scores(t)
                with pe.Fori(max(1, SPLIT[t] // SLOTS), SPLIT[t + 1] // SLOTS) as i:
                    for s in range(SLOTS):
                        up(i, s, False)

        @block.scalar
        def _(act):
            def high(i, s, first):
                act.wait_ge(step.slab_ready[s], ready(i))
                if not (first and s < 2):
                    act.wait_ge(s_h, SLOTS * i + s - 1)
                nc.scalar.activation(hi[:, s % 2], step.slab(s), ACT.Copy).then_inc(s_hi, 1)

            def gelu(i, s):
                act.wait_ge(s_h, SLOTS * i + s + 1)
                nc.scalar.activation(big[:, SLOTS * i + s, :], ps[:, s % 2, 0:T], ACT.Gelu_apprx_tanh).then_inc(s_g, 1)

            nc.scalar.preload_act_table(ACT.Gelu_apprx_tanh)
            high(0, 0, True)
            high(0, 1, True)
            for lo_i, hi_i in ((0, first_borrowed // SLOTS), (first_borrowed // SLOTS, NKEYS // SLOTS - 1)):
                if lo_i:
                    act.wait_ge(s_rt, 3)
                with act.Fori(lo_i, hi_i) as i:
                    for s in range(SLOTS):
                        gelu(i, s)
                        if s < 2:
                            high(i, s + 2, False)
                        else:
                            high(i + 1, s - 2, False)
            for s in range(SLOTS):
                gelu(NKEYS // SLOTS - 1, s)
                if s < 2:
                    high(NKEYS // SLOTS - 1, s + 2, False)

        @block.vector
        def _(dve):
            link = lambda ins, wait=True: step.link(dve, "vector", ins, wait)
            at = 2 * PH * P

            def take(n, dt=F32):
                nonlocal at
                at += n
                v = scratch[:, at - n:at]
                return v if dt == F32 else v.bitcast(dt)
            NQ = 2 * PH
            rest = take(NQ * P).rearrange("p (k n) -> p k n", n=P)
            val = take(NQ * TOPK).rearrange("p (k n) -> p k n", n=TOPK)
            idx = take(NQ * TOPK, U32).rearrange("p (k n) -> p k n", n=TOPK)
            idxf = take(NQ * TOPK).rearrange("p (h q n) -> p h q n", h=PH, q=2)
            cand = take(PH * TOPK * TOPK).rearrange("p (h n) -> p h n", h=PH)
            best = take(PH * TOPK).rearrange("p (h n) -> p h n", h=PH)
            sel = take(PH * TOPK, U32).rearrange("p (h n) -> p h n", h=PH)
            part = take(PH * TOPK, U32).rearrange("p (h n) -> p h n", h=PH)
            partf = take(PH * TOPK).rearrange("p (h n) -> p h n", h=PH)
            cand2 = rest.rearrange("p k n -> p (k n)").rearrange("p (h n) -> p h n", h=PH)
            for t, (a, b) in enumerate(TILES):
                n = b - a
                r = slice(0, n)
                dve.wait_ge(s_sc, t + 1)
                score = lambda k: ps[r, 2 + k // 4, (k % 4) * P:(k % 4 + 1) * P]
                for k in range(NQ):
                    last = nc.vector.max(val[r, k, 0:8], score(k))
                link(last)
                for k in range(NQ):
                    nc.vector.max_index(idx[r, k, 0:8], val[r, k, 0:8], score(k))
                    last = nc.vector.match_replace(out=rest[r, k, :], in_to_replace=val[r, k, 0:8], in_values=score(k),
                                                   imm_value=LOWEST)
                last.then_inc(s_sr, 1)
                dve.wait_ge(s_sr, t + 1)
                for k in range(NQ):
                    last = nc.vector.max(val[r, k, 8:16], rest[r, k, :])
                link(last)
                for k in range(NQ):
                    last = nc.vector.max_index(idx[r, k, 8:16], val[r, k, 8:16], rest[r, k, :])
                v4 = val.rearrange("p (h q) n -> p h q n", h=PH)
                shape = [n, PH, TOPK, TOPK]
                link(nc.vector.tensor_tensor(cand[r].rearrange("p h (a b) -> p h a b", a=TOPK),
                                             v4[r, :, 0, :].unsqueeze(3).to_broadcast(shape),
                                             v4[r, :, 1, :].unsqueeze(2).to_broadcast(shape), ALU.add))
                link(nc.vector.tensor_copy(idxf[r].rearrange("p h q n -> p (h q n)"), idx[r].rearrange("p k n -> p (k n)")))
                for h in range(PH):
                    last = nc.vector.max(best[r, h, 0:8], cand[r, h, :])
                link(last)
                for h in range(PH):
                    nc.vector.max_index(sel[r, h, 0:8], best[r, h, 0:8], cand[r, h, :])
                    last = nc.vector.match_replace(out=cand2[r, h, :], in_to_replace=best[r, h, 0:8],
                                                   in_values=cand[r, h, :], imm_value=LOWEST)
                link(last)
                for h in range(PH):
                    last = nc.vector.max(best[r, h, 8:16], cand2[r, h, :])
                link(last)
                for h in range(PH):
                    last = nc.vector.max_index(sel[r, h, 8:16], best[r, h, 8:16], cand2[r, h, :])
                nc.vector.tensor_tensor(pick[r, t, 2, :].rearrange("p (h n) -> p h n", h=PH), best[r],
                                        best[r, :, 0:1].to_broadcast([n, PH, TOPK]), ALU.subtract)
                link(last)
                for half, (op, by) in enumerate(((ALU.logical_shift_right, 4), (ALU.bitwise_and, TOPK - 1))):
                    link(nc.vector.tensor_scalar(part[r], sel[r], by, None, op))
                    link(nc.vector.tensor_copy(partf[r], part[r]))
                    eq = cand[r].rearrange("p h (k a) -> p (h k) a", k=TOPK)
                    link(nc.vector.tensor_tensor(eq, partf[r].rearrange("p h n -> p (h n)").unsqueeze(2)
                                                 .to_broadcast([n, PH * TOPK, TOPK]),
                                                 step.iota[r, 0:TOPK].unsqueeze(1).to_broadcast([n, PH * TOPK, TOPK]),
                                                 ALU.is_equal))
                    e4 = cand[r].rearrange("p h (k a) -> p h k a", k=TOPK)
                    link(nc.vector.tensor_tensor(e4, e4, idxf[r, :, half, :].unsqueeze(2).to_broadcast(shape), ALU.mult))
                    link(nc.vector.reduce_sum(pick[r, t, half, :], eq, axis=AX))
                nc.vector.tensor_copy(partf[r, 0, 0:1], part[r, 0, 0:1]).then_inc(s_rt, 1)
    step.used += NKEYS


def peer_gates(step, layer, big, pick, selT, ctx):
    nc, ps = step.nc, step.ps
    L = f"_{layer}"
    with ExitStack() as c1, nc.Block("peer_softmax" + L, no_gpsimd_drain=True) as block:
        den = step.sb("gate_sums" + L, [P, 3, PH], ctx=c1)
        s_e = step.sem("gate_exp_ready" + L)
        s_w = step.sem("gates_ready" + L)
        s_t = step.sem("selections_transposed" + L)
        s_c = step.sem("selections_copied" + L)

        @block.scalar
        def _(act):
            for t, (a, b) in enumerate(TILES):
                w = pick[0:b - a, t, 2, :]
                nc.scalar.activation(w, w, ACT.Exp).then_inc(s_e, 1)

        @block.vector
        def _(dve):
            link = lambda ins, wait=True: step.link(dve, "vector", ins, wait)
            for t, (a, b) in enumerate(TILES):
                n = b - a
                dve.wait_ge(s_e, t + 1)
                w = pick[0:n, t, 2, :].rearrange("p (h k) -> p h k", h=PH)
                d = den[0:n, t, :]
                link(nc.vector.reduce_sum(d, w, axis=AX))
                link(nc.vector.reciprocal(d, d))
                nc.vector.tensor_tensor(w, w, d.unsqueeze(2).to_broadcast([n, PH, TOPK]), ALU.mult).then_inc(s_w, 1)
                dve.wait_ge(s_t, t + 1)
                src = ps[:, t, 0:3 * P].rearrange("p (w n) -> p w n", w=3)[:, :, 0:n]
                nc.vector.tensor_copy(selT[:, :, a:b], src).then_inc(s_c, 1)

        @block.tensor
        def _(pe):
            for t, (a, b) in enumerate(TILES):
                n = b - a
                pe.wait_ge(s_w, t + 1)
                for w in range(3):
                    last = nc.tensor.transpose(ps[:, t, w * P:w * P + n], pick[0:n, t, w, :], step.ident[0:n, 0:n])
                last.then_inc(s_t, 1)

    GT = 4
    NG = T // GT
    with ExitStack() as c1, nc.Block("peer_gate_matrix" + L, no_gpsimd_drain=True) as block:
        rows = step.sb("one_hot_weighted" + L, [P, 2, GT, P], ctx=c1)
        cols = step.sb("one_hot" + L, [P, 2, GT, P], ctx=c1)
        gate = step.sb("gate_matrix" + L, [P, 2, GT * P], ctx=c1)
        s_oh = step.sem("one_hots_ready" + L)
        s_g = step.sem("gate_product_ready" + L)
        s_gc = step.sem("gate_product_copied" + L)
        s_gm = step.sem("gate_applied" + L)

        @block.vector
        def _(dve):
            def one_hots(i, b, first):
                if not first:
                    dve.wait_ge(s_g, 2 * i + b - 1)
                for k in range(GT):
                    tok = (2 * i + b) * GT + k
                    col = lambda w: selT[:, w, bass.ds(tok, 1)]
                    nc.vector.tensor_scalar(rows[:, b, k, :], step.iota, col(0), col(2), ALU.is_equal, ALU.mult)
                    last = nc.vector.tensor_scalar(cols[:, b, k, :], step.iota, col(1), None, ALU.is_equal)
                last.then_inc(s_oh, 1)
            for b in range(2):
                one_hots(0, b, True)
            with dve.Fori(1, NG // 2) as i:
                for b in range(2):
                    one_hots(i, b, False)

        @block.tensor
        def _(pe):
            def products(i, b, first):
                pe.wait_ge(s_oh, 2 * i + b + 1)
                if not first:
                    pe.wait_ge(s_gc, 2 * i + b - 1)
                for k in range(GT):
                    last = nc.tensor.matmul(ps[:, b, k * P:(k + 1) * P], rows[:, b, k, :], cols[:, b, k, :],
                                            start=True, stop=True)
                last.then_inc(s_g, 1)
            for b in range(2):
                products(0, b, True)
            with pe.Fori(1, NG // 2) as i:
                for b in range(2):
                    products(i, b, False)

        @block.scalar
        def _(act):
            def copy(i, b, first):
                act.wait_ge(s_g, 2 * i + b + 1)
                if not first:
                    act.wait_ge(s_gm, 2 * i + b - 1)
                nc.scalar.activation(gate[:, b, :], ps[:, b, :], ACT.Copy).then_inc(s_gc, 1)
            for b in range(2):
                copy(0, b, True)
            with act.Fori(1, NG // 2) as i:
                for b in range(2):
                    copy(i, b, False)

        @block.gpsimd
        def _(pool):
            with pool.Fori(0, NG // 2) as i:
                for b in range(2):
                    pool.wait_ge(s_gc, 2 * i + b + 1)
                    h = big[:, :, bass.ds((2 * i + b) * GT, GT)]
                    nc.gpsimd.tensor_tensor(h, h, gate[:, b, :].rearrange("p (k n) -> p n k", k=GT),
                                            ALU.mult).then_inc(s_gm, 1)
            pool.wait_ge(s_gm, NG)


def peer_down(step, layer, big):
    nc, io, ps = step.nc, step.io, step.ps
    L = f"_{layer}"
    base = step.used
    vb = step.slabs[base][1]
    with ExitStack() as c1, nc.Block("peer_down" + L, no_gpsimd_drain=True) as block:
        hi = step.sb("v_hi" + L, [P, 2, D], F32R, ctx=c1)
        lo = step.sb("v_lo" + L, [P, 2, D], F32R, ctx=c1)
        wh = step.sb("w_hi" + L, [P, 2, T], F32R, ctx=c1)
        wl = step.sb("w_lo" + L, [P, 2, T], F32R, ctx=c1)
        s_hi = step.sem("v_hi_ready" + L)
        s_y = step.sem("down_product_ready" + L)

        @block.sync
        def _(sp):
            with sp.Fori(1, NKEYS // SLOTS) as i:
                for s in range(SLOTS):
                    sp.wait_ge(step.v_split, vb + SLOTS * i + s + 1 - SLOTS)
                    sp.dma_start(step.ring[:, s, :], io["v"][layer * P + SLOTS * i + s]).then_inc(step.slab_ready[s], 16)
            step.loaded = base + NKEYS
            step.load_until(sp, base + NKEYS + SLOTS)

        @block.scalar
        def _(act):
            def high(i, s, first):
                act.wait_ge(step.slab_ready[s], 16 * (base // SLOTS + 1) + 16 * i)
                if not (first and s < 2):
                    act.wait_ge(s_y, SLOTS * i + s - 1)
                nc.scalar.activation(wh[:, s % 2, :], big[:, SLOTS * i + s, :], ACT.Copy)
                nc.scalar.activation(hi[:, s % 2, :], step.ring[:, s, :], ACT.Copy).then_inc(s_hi, 1)
            nc.scalar.preload_act_table(ACT.Copy)
            for s in range(SLOTS):
                high(0, s, True)
            with act.Fori(1, NKEYS // SLOTS) as i:
                for s in range(SLOTS):
                    high(i, s, False)

        @block.vector
        def _(dve):
            with dve.Fori(0, NKEYS // SLOTS) as i:
                for s in range(SLOTS):
                    dve.wait_ge(s_hi, SLOTS * i + s + 1)
                    nc.vector.tensor_tensor(wl[:, s % 2, :], big[:, SLOTS * i + s, :], wh[:, s % 2, :].bitcast(F32),
                                            ALU.subtract)
                    nc.vector.tensor_tensor(lo[:, s % 2, :], step.ring[:, s, :], hi[:, s % 2, :].bitcast(F32),
                                            ALU.subtract).then_inc(step.v_split, 1)

        @block.tensor
        def _(pe):
            def down(i, s, first, final):
                pe.wait_ge(step.v_split, vb + SLOTS * i + s + 1)
                b = s % 2
                for c in range(DC):
                    cs = slice(c * P, (c + 1) * P)
                    bank = ps[:, c, 0:T]
                    nc.tensor.matmul(bank, hi[:, b, cs], wh[:, b, :], start=first, stop=False)
                    nc.tensor.matmul(bank, hi[:, b, cs], wl[:, b, :], start=False, stop=False)
                    last = nc.tensor.matmul(bank, lo[:, b, cs], wh[:, b, :], start=False, stop=final)
                last.then_inc(s_y, 1)
            for s in range(SLOTS):
                down(0, s, s == 0, False)
            with pe.Fori(1, NKEYS // SLOTS - 1) as i:
                for s in range(SLOTS):
                    down(i, s, False, False)
            for s in range(SLOTS):
                down(NKEYS // SLOTS - 1, s, False, s == SLOTS - 1)
    step.used += NKEYS

    with ExitStack() as c1, nc.Block("peer_norm" + L, no_gpsimd_drain=True) as block:
        res = step.sb("res_peer" + L, [P, DC, T], ctx=c1)
        squares = step.sb("squares_peer" + L, [P, DC, T], ctx=c1)

        def residual_steps(dve, j):
            return nc.vector.scalar_tensor_tensor(out=res[:, j, :], in0=step.x[:, j, :], scalar=ALPHA,
                                                  in1=ps[:, j, 0:T], op0=ALU.mult, op1=ALU.add)
        emit_norm(step, block, "peer" + L, layer * 3 + 2, res, squares, (0, 1), residual_steps,
                  lambda pe, j, s_res: None)


_PROJ_COUNTS = (20 + 16 + 8 + 8 + 8 + 16, 12 + 16 + 8 + 8 + 8 + 16)

_OUTS = {
    "y": (P, DC, T),
    "hgrn_prompt": (P, HEADS_A, P), "hgrn_sample": (P, HEADS_A * TS, P),
    "pool_prompt": (P, HEADS_A, CTX), "pool_sample": (P, HEADS_A, TS, CTX),
    "window_k_prompt": (HD, KV, P), "window_k_sample": (HD, TS, KV, P),
    "window_v_prompt": (P, KV, HD), "window_v_sample": (P, TS, KV, HD),
    "mem_k_out": (LAYERS, P, DC, NMEM), "mem_v_out": (LAYERS, P, NMEM // P, D),
}


def _constants():
    import numpy as np
    c = np.zeros((P, C_END), np.float32)
    c[:, C_ID:C_ID + P] = np.eye(P)
    c[:, C_ONE:C_ONE + P] = 1
    c[:, C_MEAN:C_MEAN + P] = 1 / D
    c[:, C_HEAD:C_HEAD + P] = 1 / P
    c[:, C_IOTA:C_IOTA + P] = np.arange(P)
    q = np.arange(P)[:, None]
    k = np.arange(P)[None, :]
    c[:, C_MASK:C_MASK + P] = np.where(k <= q, 0, LOWEST)
    k = np.arange(2 * P)[None, :]
    c[:, C_MASK + P:C_MASK + 3 * P] = np.where((k > q) & (k <= q + P), 0, LOWEST)
    c[:, C_EPS] = EPS
    scan = np.ones((P, TP), np.float32)
    scan[:, ::BLK] = 0
    inv = np.zeros((P, HEADS_A, T), np.float32)
    for g, w in enumerate(POOL_SIZES):
        inv[:, g, :TP] = 1 / np.minimum(np.arange(TP) + 1, w)
        inv[:, g, TP:] = 1 / w
    return c, scan, inv


def kernel(**inputs):
    import numpy as np
    import concourse.bacc as bacc
    from concourse.bass_utils import run_bass_kernel_spmd

    a = {k: np.asarray(v) for k, v in inputs.items()}

    def chunks(m):
        return m.reshape(m.shape[0], -1, P).transpose(2, 1, 0)

    def slabs(w):
        return w.reshape(DC, P, -1, P).transpose(2, 1, 0, 3).reshape(-1, P, D)

    const, scan, inv = _constants()
    arrays = {"const": const, "scan_mask": scan, "inv_count": inv}
    arrays["x"] = chunks(np.concatenate([a["x_prompt"][0], a["x_sample"][:, 0]]))
    arrays["mem"] = chunks(a["mem_prompt"][0])
    arrays["ln"] = np.stack([a["ln_g"], a["ln_b"]], 2).reshape(LAYERS * 3, 2, DC, P).transpose(3, 0, 1, 2)
    arrays["gamma"] = a["hgrn_gamma"].reshape(2, HEADS_A, P).transpose(2, 0, 1)
    arrays["norm_g"] = a["hgrn_norm_g"][0].reshape(HEADS_A, P).T
    arrays["pool_scale"] = a["pool_scale"][0].reshape(HEADS_A, P).T
    arrays["pool_w"] = a["pool_w"][0].transpose(1, 0, 2)
    arrays["pool_ctx"] = a["state_pool"][0].reshape(TS, CTX, HEADS_A, P).transpose(3, 2, 0, 1)
    arrays["state"] = a["state_hgrn"][0].transpose(2, 1, 0, 3).reshape(P, -1, P)
    wc = a["w_in_c"][0]
    nq = HEADS_C * HD
    dup = [wc[:, nq + i * HD:nq + (i + 1) * HD] for i in (0, 0, 1, 1, 2, 2, 3, 3)]
    w = a["w_in_a"][0]
    part = [w[:, i * 512:(i + 1) * 512] for i in (0, 1, 3, 2, 4)]
    first = (part, [wc[:, :nq]] + dup)
    outs = (a["w_out_a"][0], a["w_out_c"][0])
    cols = []
    for layer in range(LAYERS):
        cols += [*first[layer], a["mem_wkv"][layer], outs[layer], a["mem_wq"][layer], a["mem_wo"][layer],
                 a["peer_wq"][layer]]
    arrays["proj"] = slabs(np.concatenate(cols, 1))
    arrays["u"] = a["peer_u"].reshape(LAYERS, P, P, DC, P).transpose(0, 2, 4, 3, 1).reshape(-1, P, D)
    arrays["v"] = a["peer_v"].reshape(LAYERS, P, P, D).transpose(0, 2, 1, 3).reshape(-1, P, D)
    arrays["subkeys"] = a["peer_subkeys"].transpose(0, 4, 1, 2, 3).reshape(LAYERS, P, -1)
    ckm = a["cache_mem_k"].reshape(LAYERS, TS, NMEM, DC, P)
    arrays["cache_k"] = ckm.transpose(0, 1, 4, 3, 2)
    arrays["cache_v"] = a["cache_mem_v"].reshape(LAYERS, TS, 2, P, D).transpose(0, 1, 3, 2, 4)
    k = a["cache_swa_k"][0][:, 1:].transpose(3, 0, 2, 1)
    arrays["window_k"] = np.concatenate([k, k])
    v = a["cache_swa_v"][0][:, 1:].transpose(1, 0, 2, 3)
    arrays["window_v"] = np.concatenate([v, v], 3)
    s = a["attn_sinks"][0]
    order = s.reshape(KV, 4, 2).transpose(0, 2, 1).reshape(-1)
    arrays["sinks"] = np.concatenate([np.tile(s, (P, 1)), np.tile(order, TS)[:, None]], 1)
    arrays = {k: np.ascontiguousarray(v) for k, v in arrays.items()}

    nc = bacc.Bacc("TRN2", target_bir_lowering=False, num_devices=1)
    io = {k: nc.dram_tensor(f"in_{k}", v.shape, F32, kind="ExternalInput").ap() for k, v in arrays.items()}
    for k, shape in _OUTS.items():
        io[k] = nc.dram_tensor(f"out_{k}", shape, F32, kind="ExternalOutput").ap()
    io["proj_counts"] = _PROJ_COUNTS
    hybrid_step(nc, io)
    r = run_bass_kernel_spmd(nc, [{f"in_{k}": v for k, v in arrays.items()}], core_ids=[0]).results[0]
    o = {k: r[f"out_{k}"] for k in _OUTS}

    y = o["y"].transpose(2, 1, 0).reshape(T, D)
    return (
        y[None, :TP], y[TP:, None],
        o["hgrn_prompt"].transpose(1, 0, 2)[None, None],
        o["hgrn_sample"].reshape(P, HEADS_A, TS, P).transpose(2, 1, 0, 3)[None],
        o["pool_prompt"].transpose(2, 1, 0).reshape(CTX, -1)[None, None],
        o["pool_sample"].transpose(2, 3, 1, 0).reshape(TS, CTX, -1)[None],
        o["window_k_prompt"].transpose(2, 1, 0)[None, None],
        o["window_k_sample"].transpose(1, 3, 2, 0)[None],
        o["window_v_prompt"][None, None],
        o["window_v_sample"].transpose(1, 0, 2, 3)[None],
        o["mem_k_out"].transpose(0, 3, 2, 1).reshape(LAYERS, 1, NMEM, MH, MHD),
        o["mem_v_out"].transpose(0, 2, 1, 3).reshape(LAYERS, 1, NMEM, MH, MHD),
    )
```

```python
from contextlib import ExitStack

import concourse.bass as bass
from concourse import mybir

F32 = mybir.dt.float32
F32R = mybir.dt.float32r
U32 = mybir.dt.uint32
ALU = mybir.AluOpType
ACT = mybir.ActivationFunctionType
AX = mybir.AxisListType.X

P = 128
D = 1024
DC = D // P
TP = 256
TS = 8
T = TP + TS
LAYERS = 2
ALPHA = float((2 * LAYERS) ** 0.25)
EPS = 1e-5
HEADS_A = 4
BLK = 16
NBLK = TP // BLK
POOL_SIZES = (2, 4, 8, 16)
CTX = 15
KV = 2
HEADS_C = 16
HD = 64
MH = 4
MHD = 256
NMEM = 256
PH = 8
TOPK = 16
NKEYS = 128
LOWEST = -3.0e38
SLOTS = 4
HC = DC // 2

C_ID, C_ONE, C_MEAN, C_HEAD, C_IOTA = (n * P for n in range(5))
C_MASK = 5 * P
C_EPS = C_MASK + 3 * P
C_END = C_EPS + 1


def hybrid_step(nc, io):
    with ExitStack() as top:
        step = Step(nc, io, top)
        step.load_constants()
        for layer in range(LAYERS):
            with ExitStack() as attn:
                step.open_attention(layer, attn)
                if layer == 0:
                    hgrn_pool_mixer(step, layer)
                else:
                    window_mixer(step, layer)
                step.open_caches(layer, attn)
                project_and_norm(step, layer, 0)
                cross_attention(step, layer)
                project_and_norm(step, layer, 1)
            peer(step, layer)
            step.end_layer()
        step.store_result()


class Step:

    def __init__(self, nc, io, top):
        self.nc, self.io = nc, io
        self.sb = lambda name, shape, dt=F32, ctx=top: ctx.enter_context(nc.sbuf_tensor(name, shape, dt))
        self.ring, self.ring_lo = self.pair("slab_ring", [P, SLOTS, D], "slab_ring_lo", [P, SLOTS, DC, P])
        self.x = self.sb("x_T", [P, DC, T])
        self.const = self.sb("constants", [P, C_END])
        self.ln = self.sb("ln_scale_shift", [P, LAYERS * 3, 2, DC])
        self.own, operand_hi = self.pair("sample_own_rows", [P, DC * T], "operand_hi", [P, DC, T])
        self.mixed, operand_lo = self.pair("mixed_T", [P, DC, T], "operand_lo", [P, DC, T])
        self.operand = (operand_hi, operand_lo)
        self.squares, self.slab_hi = self.pair("squares", [P, DC, T], "slab_hi", [P, 2, DC, P])
        self.ps = top.enter_context(nc.psum_tensor("banks", [P, 8, 512], F32))
        self.slab_ready = [nc.alloc_semaphore(f"slab_ready{s}") for s in range(SLOTS)]
        self.product_done = nc.alloc_semaphore("projection_product_done")
        self.slab_hi_ready = nc.alloc_semaphore("projection_slab_hi_ready")
        self.slab_lo_ready = nc.alloc_semaphore("projection_slab_lo_ready")
        self.half_product_done = nc.alloc_semaphore("projection_half_product_done")
        self.split_number = {}
        self.u_split = nc.alloc_semaphore("u_half_slab_split")
        self.v_split = nc.alloc_semaphore("v_half_slab_split")
        self.stored = nc.alloc_semaphore("outputs_stored")
        self.constants_ready = nc.alloc_semaphore("constants_ready")
        self.vector_done = nc.alloc_semaphore("vector_instruction_done")
        self.scalar_done = nc.alloc_semaphore("scalar_instruction_done")
        self.gpsimd_done = nc.alloc_semaphore("gpsimd_instruction_done")
        self.count = {"vector": 0, "scalar": 0, "gpsimd": 0}
        self.stores = 0
        self.layer_sems = []
        self.slabs = []
        kinds = {"projection": 0, "u": 0, "v": 0}
        for layer in range(LAYERS):
            n = io["proj_counts"][layer]
            run = [("projection", io["proj"], sum(io["proj_counts"][:layer]) + k) for k in range(n)]
            run += [("u", io["u"], layer * P + k) for k in range(P)]
            run += [("v", io["v"], layer * P + k) for k in range(P)]
            for kind, src, k in run:
                self.slabs.append((kind, kinds[kind], src, k))
                kinds[kind] += 1
        self.used = 0
        self.loaded = 0

    def pair(self, name, shape, name_r, shape_r):
        address = (self.nc.sbuf_base + 31) // 32 * 32
        one = self.sb(name, shape)
        return one, self.nc.alloc_sbuf_tensor_at(name_r, shape_r, F32R, offset=address)

    ident = property(lambda s: s.const[:, C_ID:C_ID + P])
    ones = property(lambda s: s.const[:, C_ONE:C_ONE + P])
    mean_d = property(lambda s: s.const[:, C_MEAN:C_MEAN + P])
    mean_head = property(lambda s: s.const[:, C_HEAD:C_HEAD + P])
    iota = property(lambda s: s.const[:, C_IOTA:C_IOTA + P])
    masks = property(lambda s: s.const[:, C_MASK:C_MASK + 3 * P])
    eps = property(lambda s: s.const[:, C_EPS:C_EPS + 1])

    def sem(self, name):
        s = self.nc.alloc_semaphore(name)
        self.layer_sems.append(s)
        return s

    def end_layer(self):
        self.nc.clear_and_free_semaphores(self.layer_sems)
        self.layer_sems = []
        self.nc.all_engine_barrier()

    def link(self, engine, name, instruction, wait=True):
        sem = {"vector": self.vector_done, "scalar": self.scalar_done, "gpsimd": self.gpsimd_done}[name]
        self.count[name] += 1
        instruction.then_inc(sem, 1)
        if wait:
            engine.wait_ge(sem, self.count[name])

    def store(self, engine, dst, src):
        self.stores += 1
        engine.dma_start(dst, src).then_inc(self.stored, 16)

    def slot_free(self, sp, n):
        if n < SLOTS:
            return
        kind, k = self.slabs[n - SLOTS][:2]
        if kind == "projection":
            sp.wait_ge(self.product_done, k + 1)
        else:
            sp.wait_ge(self.u_split if kind == "u" else self.v_split, 2 * (k + 1))

    def load_until(self, sp, end):
        for n in range(self.loaded, min(end, len(self.slabs))):
            _, _, src, k = self.slabs[n]
            self.slot_free(sp, n)
            sp.dma_start(self.ring[:, n % SLOTS, :], src[k]).then_inc(self.slab_ready[n % SLOTS], 16)
        self.loaded = max(self.loaded, min(end, len(self.slabs)))

    def wait_slab(self, engine, n):
        engine.wait_ge(self.slab_ready[n % SLOTS], 16 * (n // SLOTS + 1))

    def slab(self, n):
        return self.ring[:, n % SLOTS, :].rearrange("p (c m) -> p c m", c=DC)

    def product_count(self, n):
        assert self.slabs[n][0] == "projection"
        return self.slabs[n][1] + 1

    def open_attention(self, layer, ctx):
        self.q = self.sb(f"query_T{layer}", [P, DC, T], ctx=ctx)
        self.mem_k = self.sb(f"mem_k_T{layer}", [P, DC, NMEM], ctx=ctx)
        self.mem_v = self.sb(f"mem_v{layer}", [P, NMEM // P, D], ctx=ctx)

    def open_caches(self, layer, ctx):
        self.cache = [self.sb(f"cache_k_T{layer}", [P, TS, DC, NMEM], ctx=ctx),
                      self.sb(f"cache_v{layer}", [P, TS, NMEM // P, D], ctx=ctx)]
        self.cache_ready = [self.sem(f"cache_{w}_ready{layer}") for w in "kv"]

    def load_cache(self, sp, layer, which, b):
        name = ("cache_k", "cache_v")[which]
        sp.dma_start(self.cache[which][:, b], self.io[name][layer, b]).then_inc(self.cache_ready[which], 16)

    def load_constants(self):
        nc, io = self.nc, self.io
        with nc.Block("constants", no_gpsimd_drain=True) as block:
            @block.sync
            def _(sp):
                sp.dma_start(self.const[:], io["const"]).then_inc(self.constants_ready, 16)
                sp.dma_start(self.x[:], io["x"]).then_inc(self.constants_ready, 16)
                sp.dma_start(self.ln[:], io["ln"]).then_inc(self.constants_ready, 16)
                self.load_until(sp, SLOTS)
                sp.wait_ge(self.constants_ready, 48)

            number_slabs(self, 0, 1)
            xh, xl = self.operand
            x_split = self.sem("x_hi_ready")

            @block.scalar
            def _(act):
                split_high(self, act, 0)
                act.wait_ge(self.constants_ready, 48)
                nc.scalar.activation(xh[:], self.x[:], ACT.Copy).then_inc(x_split, 1)

            @block.vector
            def _(dve):
                dve.wait_ge(x_split, 1)
                nc.vector.tensor_tensor(xl[:], self.x[:], xh[:].bitcast(F32), ALU.subtract)

            @block.gpsimd
            def _(pool):
                split_low(self, pool, 0)
                slabs_split(self, pool, 0)

    def store_result(self):
        nc, io = self.nc, self.io
        with nc.Block("result", no_gpsimd_drain=True) as block:
            @block.sync
            def _(sp):
                self.store(sp, io["y"], self.x[:])
                sp.wait_ge(self.stored, 16 * self.stores)


def number_slabs(step, first, count):
    for n in range(first, first + count):
        step.split_number.setdefault(n, len(step.split_number))


def split_high(step, act, n):
    nc, k = step.nc, step.split_number[n]
    step.wait_slab(act, n)
    for g in range(2):
        if n - 2 in step.split_number:
            if g == 0:
                act.wait_ge(step.half_product_done, step.split_number[n - 2] + 1)
            else:
                act.wait_ge(step.product_done, step.product_count(n - 2))
        cs = slice(g * HC, (g + 1) * HC)
        nc.scalar.activation(step.slab_hi[:, (k + 1) % 2, cs], step.slab(n)[:, cs], ACT.Copy).then_inc(step.slab_hi_ready, 1)


def split_low(step, pool, n):
    nc, k = step.nc, step.split_number[n]
    step.wait_slab(pool, n)
    for g in range(2):
        cs = slice(g * HC, (g + 1) * HC)
        pool.wait_ge(step.slab_hi_ready, 2 * k + g + 1)
        nc.gpsimd.tensor_tensor(step.ring_lo[:, n % SLOTS, cs], step.slab(n)[:, cs],
                                step.slab_hi[:, (k + 1) % 2, cs].bitcast(F32), ALU.subtract).then_inc(step.slab_lo_ready, 1)


def slabs_split(step, pool, n):
    pool.wait_ge(step.slab_lo_ready, 2 * (step.split_number[n] + 1))


def product(step, pe, n, bank, s_part=None):
    nc, k = step.nc, step.split_number[n]
    xh, xl = step.operand
    wh, wl = step.slab_hi[:, (k + 1) % 2], step.ring_lo[:, n % SLOTS]
    for c in range(DC):
        if c % HC == 0:
            pe.wait_ge(step.slab_lo_ready, 2 * k + c // HC + 1)
        if s_part is not None:
            pe.wait_ge(s_part, c + 1)
        nc.tensor.matmul(step.ps[:, bank, 0:T], wh[:, c, :], xh[:, c, :], start=(c == 0), stop=False)
        nc.tensor.matmul(step.ps[:, bank, 0:T], wh[:, c, :], xl[:, c, :], start=False, stop=False)
        last = nc.tensor.matmul(step.ps[:, bank, 0:T], wl[:, c, :], xh[:, c, :], start=False, stop=(c == DC - 1))
        if c == HC - 1:
            last.then_inc(step.half_product_done, 1)
    last.then_inc(step.product_done, 1)


def emit_norm(step, block, tag, sub, res, base_bank, residual_steps, tensor_steps, next_slab, early=None):
    nc = step.nc
    squares = step.squares
    early = early or {}
    mean_bank, var_bank = base_bank
    s_res = step.sem(f"residual_chunk_ready_{tag}")
    s_mean = step.sem(f"mean_ready_{tag}")
    s_cent = step.sem(f"centred_chunk_ready_{tag}")
    s_sq = step.sem(f"squared_chunk_ready_{tag}")
    s_var = step.sem(f"variance_ready_{tag}")
    s_std = step.sem(f"deviation_ready_{tag}")
    s_rstd = step.sem(f"reciprocal_ready_{tag}")
    s_norm = step.sem(f"normed_chunk_ready_{tag}")
    s_x = step.sem(f"x_chunk_ready_{tag}")
    s_xh = step.sem(f"x_chunk_hi_ready_{tag}")
    s_xl = step.sem(f"x_chunk_lo_ready_{tag}")
    xh, xl = step.operand
    if next_slab is not None:
        number_slabs(step, next_slab, 1)
    rstd = squares[:, 0, :]
    mean = step.ps[:, mean_bank, 0:T]
    var = step.ps[:, var_bank, 0:T]

    @block.tensor
    def _(pe):
        for j in range(DC):
            tensor_steps(pe, j, s_res)
            if j >= 1:
                pe.wait_ge(s_res, j)
                nc.tensor.matmul(mean, step.mean_d, res[:, j - 1, :], start=(j == 1), stop=False)
        pe.wait_ge(s_res, DC)
        nc.tensor.matmul(mean, step.mean_d, res[:, DC - 1, :], start=False, stop=True).then_inc(s_mean, 1)
        for j in range(DC):
            pe.wait_ge(s_sq, j + 1)
            last = nc.tensor.matmul(var, step.mean_d, squares[:, j, :], start=(j == 0), stop=(j == DC - 1))
        last.then_inc(s_var, 1)

    @block.vector
    def _(dve):
        if "vector" in early:
            early["vector"](dve)
        for j in range(DC):
            residual_steps(dve, j).then_inc(s_res, 1)
        dve.wait_ge(s_mean, 1)
        dve.wait_ge(s_res, DC)
        for j in range(DC):
            nc.vector.tensor_tensor(res[:, j, :], res[:, j, :], mean, ALU.subtract).then_inc(s_cent, 1)
        dve.wait_ge(s_std, 1)
        nc.vector.reciprocal(rstd, rstd).then_inc(s_rstd, 1)
        dve.wait_ge(s_rstd, 1)
        for j in range(DC + 2):
            if j < DC:
                nc.vector.tensor_tensor(res[:, j, :], res[:, j, :], rstd, ALU.mult).then_inc(s_norm, 1)
            if j >= 2 and next_slab is not None:
                dve.wait_ge(s_x, j - 1)
                nc.vector.tensor_copy(xh[:, j - 2, :], step.x[:, j - 2, :]).then_inc(s_xh, 1)

    @block.gpsimd
    def _(pool):
        if "gpsimd" in early:
            early["gpsimd"](pool)
        if next_slab is None:
            return
        split_low(step, pool, next_slab)
        for j in range(DC):
            pool.wait_ge(s_xh, j + 1)
            nc.gpsimd.tensor_tensor(xl[:, j, :], step.x[:, j, :], xh[:, j, :].bitcast(F32),
                                    ALU.subtract).then_inc(s_xl, 1)
        pool.wait_ge(s_xl, DC)

    @block.scalar
    def _(act):
        if "scalar" in early:
            early["scalar"](act)
        for j in range(DC):
            act.wait_ge(s_cent, j + 1)
            nc.scalar.activation(squares[:, j, :], res[:, j, :], ACT.Square).then_inc(s_sq, 1)
        act.wait_ge(s_var, 1)
        nc.scalar.activation(rstd, var, ACT.Sqrt, bias=step.eps).then_inc(s_std, 1)
        if next_slab is not None:
            split_high(step, act, next_slab)
        for j in range(DC):
            act.wait_ge(s_norm, j + 1)
            nc.scalar.activation(step.x[:, j, :], res[:, j, :], ACT.Identity,
                                 scale=step.ln[:, sub, 0, j:j + 1], bias=step.ln[:, sub, 1, j:j + 1]).then_inc(s_x, 1)


def project_and_norm(step, layer, which):
    nc = step.nc
    base = step.used
    tag = f"{'mixer' if which == 0 else 'cross'}_{layer}"
    number_slabs(step, base, DC)
    hi, lo = step.operand
    res = step.q
    with nc.Block(f"out_{tag}", no_gpsimd_drain=True) as block:
        s_mh = step.sem(f"mixed_chunk_hi_ready_{tag}")
        s_part = step.sem(f"mixed_chunk_split_{tag}")

        @block.sync
        def _(sp):
            if which == 0:
                sp.wait_ge(step.stored, 16 * step.stores)
            for j in range(DC):
                if which == 0:
                    step.load_cache(sp, layer, 0, j)
                step.load_until(sp, base + j + 1 + SLOTS)

        def scalar_early(act):
            split_high(step, act, base)
            for c in range(DC):
                nc.scalar.activation(hi[:, c, :], step.mixed[:, c, :], ACT.Copy).then_inc(s_mh, 1)
            for j in range(1, DC):
                split_high(step, act, base + j)

        def vector_early(dve):
            for c in range(DC):
                dve.wait_ge(s_mh, c + 1)
                nc.vector.tensor_tensor(lo[:, c, :], step.mixed[:, c, :], hi[:, c, :].bitcast(F32),
                                        ALU.subtract).then_inc(s_part, 1)

        def gpsimd_early(pool):
            for j in range(DC):
                split_low(step, pool, base + j)

        def tensor_steps(pe, j, s_res):
            if j >= 3:
                pe.wait_ge(s_res, j - 2)
            product(step, pe, base + j, j % 3, s_part if j == 0 else None)

        def residual_steps(dve, j):
            dve.wait_ge(step.product_done, step.product_count(base + j))
            return nc.vector.scalar_tensor_tensor(out=res[:, j, :], in0=step.x[:, j, :], scalar=ALPHA,
                                                  in1=step.ps[:, j % 3, 0:T], op0=ALU.mult, op1=ALU.add)

        emit_norm(step, block, tag, layer * 3 + which, res, (3, 4), residual_steps, tensor_steps, base + DC,
                  {"scalar": scalar_early, "vector": vector_early, "gpsimd": gpsimd_early})
    step.used += DC


def memory_product(step, pe, n, k, mem, bank, s_read):
    nc = step.nc
    if k >= 2:
        pe.wait_ge(s_read, k - 1)
    step.wait_slab(pe, n)
    w = step.slab(n)
    if k < DC:
        for c in range(DC):
            last = nc.tensor.matmul(step.ps[:, bank, 0:NMEM], w[:, c, :], mem[:, c, :],
                                    start=(c == 0), stop=(c == DC - 1))
    else:
        for m in range(NMEM // P):
            for c in range(DC):
                last = nc.tensor.matmul(step.ps[:, bank, m * P:(m + 1) * P], mem[:, c, m * P:(m + 1) * P],
                                        w[:, c, :], start=(c == 0), stop=(c == DC - 1))
    last.then_inc(step.product_done, 1)


def memory_copy(step, act, n, k, bank, s_read):
    nc = step.nc
    act.wait_ge(step.product_done, step.product_count(n))
    if k < DC:
        nc.scalar.activation(step.mem_k[:, k, :], step.ps[:, bank, 0:NMEM], ACT.Copy).then_inc(s_read, 1)
    else:
        out = step.mem_v[:, :, (k - DC) * P:(k - DC + 1) * P]
        nc.scalar.activation(out, step.ps[:, bank, 0:NMEM].rearrange("p (m f) -> p m f", m=NMEM // P),
                             ACT.Copy).then_inc(s_read, 1)


def hgrn_pool_mixer(step, layer):
    nc, io, ps = step.nc, step.io, step.ps
    H4 = HEADS_A
    NP, NS = H4 * TP, H4 * TS
    base = step.used
    with ExitStack() as ctx:
        def sb(name, shape, c=ctx):
            return step.sb(name, shape, ctx=c)

        qs = sb("silu_q", [P, NP + NS])
        fg = sb("forget_gate", [P, NP + NS])
        kk = sb("key_gate", [P, NP + NS])
        lf = sb("log_forget", [P, NP + NS])
        vi = sb("value_i", [P, NP + NS])
        sg = sb("silu_g", [P, NP + NS])
        out_h = sb("hgrn_out", [P, NP + NS])
        u_ext = sb("pool_prompt_ext", [P, H4, CTX + TP])
        s_ext = sb("pool_sample_ext", [P, H4, TS, CTX + 1])
        gam = sb("gamma_T", [P, 2, H4])
        lbt = sb("lower_bound", [P, 6, H4])
        ng = sb("norm_gain", [P, H4])
        psc = sb("pool_scale_T", [P, H4])
        pw = sb("pool_weights", [P, H4, P])
        inv = sb("window_inverse", [P, H4, T])
        smask = sb("scan_mask", [P, TP])
        s0 = sb("sample_state", [P, NS, P])
        mem = sb("memory_T", [P, DC, NMEM])
        params = step.sem("mixer_params_ready")
        late = step.sem("mixer_late_params_ready")
        lb, oml = lbt[:, 4, :], lbt[:, 5, :]

        with ExitStack() as c1, nc.Block("mixer_in", no_gpsimd_drain=True) as block:
            sig = sb("sigmoids", [P, 2, T], c1)
            s_sig = step.sem("sigmoid_ready")
            s_use = step.sem("sigmoid_used")
            s_cp = step.sem("chunk_copied")
            order = ["q"] * 4 + ["f"] * 4 + ["g"] * 4 + ["i"] * 4 + ["u"] * 4
            N_SIG = 12
            number_slabs(step, base, 20)

            @block.sync
            def _(sp):
                for dst, name in ((gam, "gamma"), (ng, "norm_g"), (psc, "pool_scale")):
                    sp.dma_start(dst[:], io[name]).then_inc(params, 16)
                step.load_until(sp, base + 20 + SLOTS)

            @block.gpsimd
            def _(pool):
                late_loads = ((pw[:], "pool_w"), (inv[:], "inv_count"), (smask[:], "scan_mask"),
                              (s_ext[:, :, :, 0:CTX], "pool_ctx"), (mem[:], "mem"), (s0[:], "state"))
                for j in range(1, 20):
                    split_low(step, pool, base + j)
                    if j <= len(late_loads):
                        dst, name = late_loads[j - 1]
                        pool.dma_start(dst, io[name]).then_inc(late, 16)
                step.link(pool, "gpsimd", nc.gpsimd.memset(u_ext[:, :, 0:CTX], 0.0))
                slabs_split(step, pool, base + 19)

            @block.tensor
            def _(pe):
                for j in range(20):
                    if 4 <= j < N_SIG + 4:
                        pe.wait_ge(s_use, j - 3)
                    elif j >= N_SIG + 4:
                        pe.wait_ge(s_cp, j - 3 - N_SIG)
                    product(step, pe, base + j, j % 4)

            @block.scalar
            def _(act):
                act.wait_ge(params, 48)
                act.wait_ge(step.vector_done, step.count["vector"] + 2)
                nc.scalar.activation(lbt[:, 1:3, :], lbt[:, 1:3, :], ACT.Exp).then_inc(s_sig, 1)
                split_high(step, act, base + 1)
                for j, what in enumerate(order):
                    act.wait_ge(step.product_done, step.product_count(base + j))
                    if j + 2 < 20:
                        split_high(step, act, base + j + 2)
                    bank, h = ps[:, j % 4, :], j % 4
                    if j < N_SIG:
                        if j >= 2:
                            act.wait_ge(s_use, j - 1)
                        nc.scalar.activation(sig[:, j % 2, :], bank[:, 0:T], ACT.Sigmoid).then_inc(s_sig, 1)
                    elif what == "i":
                        nc.scalar.activation(vi[:, h * TP:(h + 1) * TP], bank[:, 0:TP], ACT.Copy)
                        nc.scalar.activation(vi[:, NP + h * TS:NP + (h + 1) * TS], bank[:, TP:T],
                                             ACT.Copy).then_inc(s_cp, 1)
                    else:
                        nc.scalar.activation(u_ext[:, h, CTX:CTX + TP], bank[:, 0:TP], ACT.Copy)
                        nc.scalar.activation(s_ext[:, h, :, CTX], bank[:, TP:T], ACT.Copy).then_inc(s_cp, 1)

            @block.vector
            def _(dve):
                link = lambda ins, wait=True: step.link(dve, "vector", ins, wait)
                dve.wait_ge(params, 48)
                link(nc.vector.tensor_tensor(lbt[:, 0, :], gam[:, 0, :], gam[:, 1, :], ALU.max))
                link(nc.vector.tensor_tensor(lbt[:, 1:3, :], gam[:], lbt[:, 0:1, :].to_broadcast([P, 2, H4]),
                                             ALU.subtract))
                dve.wait_ge(s_sig, 1)
                link(nc.vector.tensor_tensor(lbt[:, 3, :], lbt[:, 1, :], lbt[:, 2, :], ALU.add))
                link(nc.vector.reciprocal(lbt[:, 3, :], lbt[:, 3, :]))
                link(nc.vector.tensor_tensor(lb, lbt[:, 1, :], lbt[:, 3, :], ALU.mult))
                link(nc.vector.tensor_scalar(oml, lb, -1.0, 1.0, ALU.mult, ALU.add))
                for j, what in enumerate(order[:N_SIG]):
                    dve.wait_ge(s_sig, j + 2)
                    h, sj = j % 4, sig[:, j % 2, :]
                    for lo, hi, a, b in ((0, TP, h * TP, (h + 1) * TP), (TP, T, NP + h * TS, NP + (h + 1) * TS)):
                        if what == "f":
                            last = nc.vector.tensor_scalar(fg[:, a:b], sj[:, lo:hi], oml[:, h:h + 1], lb[:, h:h + 1],
                                                           ALU.mult, ALU.add)
                        else:
                            dst = qs if what == "q" else sg
                            last = nc.vector.tensor_tensor(dst[:, a:b], sj[:, lo:hi], ps[:, j % 4, lo:hi], ALU.mult)
                    last.then_inc(s_use, 1)
        step.used += 20

        base = step.used
        with ExitStack() as ctx2:
            cum = sb("cumulative_log", [P, NP], ctx2)
            ecum = sb("exp_cumulative", [P, NP], ctx2)
            qe = sb("q_decayed", [P, NP], ctx2)
            kd = sb("k_to_block_end", [P, NP], ctx2)
            with ExitStack() as c1, nc.Block("mixer_lags", no_gpsimd_drain=True) as block:
                dif = sb("lag_decay", [P, 2, NP], c1)
                qk = sb("lag_qk", [P, 2, NP], c1)
                pr = sb("lag_product", [P, 2, NP], c1)
                term = sb("lag_term", [P, 2, NP], c1)
                s_ln = step.sem("log_ready")
                s_b = step.sem("cumulative_ready")
                s_eb = step.sem("exp_cumulative_ready")
                s_kd = step.sem("block_end_decay_ready")
                s_ekd = step.sem("block_end_exp_ready")
                s_dif = step.sem("lag_difference_ready")
                s_edif = step.sem("lag_exp_ready")
                s_qk = step.sem("lag_qk_ready")
                s_pr = step.sem("lag_product_ready")
                s_att = step.sem("lag_attention_ready")
                s_term = step.sem("lag_term_ready")
                s_sum = step.sem("lag_term_added")
                s_mem = step.sem("memory_chunk_copied")
                blocks = lambda ap: ap.rearrange("p (n t) -> p n t", t=BLK)
                prompt = lambda t: blocks(t[:, 0:NP])
                LAG = [BLK - j for j in range(BLK)]
                HALF = NP // BLK // 2
                packed = lambda t, j: t[:, j % 2, 0:2 * HALF * LAG[j]].rearrange("p (n t) -> p n t", t=LAG[j])

                @block.sync
                def _(sp):
                    step.load_until(sp, base + 16 + SLOTS)

                @block.tensor
                def _(pe):
                    pe.wait_ge(late, 96)
                    for j in range(BLK):
                        memory_product(step, pe, base + j, j, mem, 4 + j % 2, s_mem)
                        pe.wait_ge(s_pr, j + 1)
                        if j >= 2:
                            pe.wait_ge(s_term, j - 1)
                        for half in range(2):
                            w = HALF * LAG[j]
                            last = nc.tensor.matmul(ps[:, 2 * (j % 2) + half, 0:w], step.ones,
                                                    pr[:, j % 2, half * w:(half + 1) * w], start=True, stop=True)
                        last.then_inc(s_att, 1)

                @block.scalar
                def _(act):
                    nc.scalar.activation(lf[:], fg[:], ACT.Ln).then_inc(s_ln, 1)
                    act.wait_ge(s_b, 1)
                    nc.scalar.activation(ecum[:], cum[:], ACT.Exp).then_inc(s_eb, 1)
                    act.wait_ge(s_kd, 1)
                    nc.scalar.activation(kd[:], kd[:], ACT.Exp).then_inc(s_ekd, 1)
                    for j in range(BLK):
                        if j:
                            act.wait_ge(s_dif, j)
                            nc.scalar.activation(packed(dif, j), packed(dif, j), ACT.Exp).then_inc(s_edif, 1)
                        memory_copy(step, act, base + j, j, 4 + j % 2, s_mem)

                @block.gpsimd
                def _(pool):
                    def make_qk(j):
                        if j >= 2:
                            pool.wait_ge(s_pr, j - 1)
                        nc.gpsimd.tensor_tensor(packed(qk, j), prompt(qs)[:, :, j:], prompt(kk)[:, :, :LAG[j]],
                                                ALU.mult).then_inc(s_qk, 1)
                    pool.wait_ge(s_kd, 1)
                    make_qk(0)
                    make_qk(1)
                    for j in range(1, BLK):
                        if j + 1 < BLK:
                            make_qk(j + 1)
                        pool.wait_ge(s_term, j + 1)
                        if j >= 2:
                            pool.wait_ge(s_sum, j - 1)
                        o = prompt(out_h)[:, :, j:]
                        nc.gpsimd.tensor_tensor(o, o, packed(term, j), ALU.add).then_inc(s_sum, 1)
                    pool.wait_ge(s_sum, BLK - 1)

                @block.vector
                def _(dve):
                    link = lambda ins, wait=True: step.link(dve, "vector", ins, wait)
                    dve.wait_ge(late, 96)
                    link(nc.vector.tensor_scalar(kk[:], fg[:], -1.0, 1.0, ALU.mult, ALU.add))
                    dve.wait_ge(s_ln, 1)
                    for h in range(H4):
                        cols = slice(h * TP, (h + 1) * TP)
                        last = nc.vector.tensor_tensor_scan(cum[:, cols], smask[:], lf[:, cols], 0.0,
                                                            ALU.mult, ALU.add)
                    last.then_inc(s_b, 1)
                    dve.wait_ge(s_b, 1)
                    cb = blocks(cum[:])
                    ends = cb[:, :, BLK - 1:BLK].to_broadcast([P, NP // BLK, BLK])
                    nc.vector.tensor_tensor(blocks(kd[:]), ends, cb, ALU.subtract).then_inc(s_kd, 1)
                    dve.wait_ge(s_eb, 1)
                    nc.vector.tensor_tensor(qe[:], qs[:, 0:NP], ecum[:], ALU.mult)
                    dve.wait_ge(s_ekd, 1)
                    link(nc.vector.tensor_tensor(kd[:], kd[:], kk[:, 0:NP], ALU.mult))

                    def difference(j):
                        if j >= 3:
                            dve.wait_ge(s_pr, j - 1)
                        nc.vector.tensor_tensor(packed(dif, j), cb[:, :, j:], cb[:, :, :LAG[j]],
                                                ALU.subtract).then_inc(s_dif, 1)

                    def accumulate(j):
                        dve.wait_ge(s_att, j + 1)
                        if j >= 3:
                            dve.wait_ge(s_sum, j - 2)
                        for half in range(2):
                            w = HALF * LAG[j]
                            a = ps[:, 2 * (j % 2) + half, 0:w].rearrange("p (n t) -> p n t", t=LAG[j])
                            v = prompt(vi)[:, half * HALF:(half + 1) * HALF, :LAG[j]]
                            if j == 0:
                                dst = prompt(out_h)[:, half * HALF:(half + 1) * HALF, :]
                            else:
                                dst = packed(term, j)[:, half * HALF:(half + 1) * HALF, :]
                            last = nc.vector.tensor_tensor(dst, a, v, ALU.mult)
                        last.then_inc(s_term, 1)

                    difference(1)
                    for j in range(BLK):
                        if j + 1 < BLK and j >= 1:
                            difference(j + 1)
                        dve.wait_ge(s_qk, j + 1)
                        if j >= 2:
                            dve.wait_ge(s_att, j - 1)
                        if j == 0:
                            nc.vector.tensor_copy(pr[:, 0, :], qk[:, 0, :]).then_inc(s_pr, 1)
                        else:
                            dve.wait_ge(s_edif, j)
                            w = 2 * HALF * LAG[j]
                            nc.vector.scalar_tensor_tensor(out=pr[:, j % 2, 0:w], in0=dif[:, j % 2, 0:w], scalar=1.0,
                                                           in1=qk[:, j % 2, 0:w], op0=ALU.min,
                                                           op1=ALU.mult).then_inc(s_pr, 1)
                        if j >= 1:
                            accumulate(j - 1)
                    accumulate(BLK - 1)
            step.used += 16

            with ExitStack() as c1, nc.Block("mixer_chain", no_gpsimd_drain=True) as block:
                tok = sb("token_major", [BLK, 2, 2, H4 * P], c1)
                state = sb("state", [P, 3, H4, P], c1)
                diag = sb("diagonal_values", [P, NS, P], c1)
                s_tr = step.sem("block_transposed")
                s_ck = step.sem("block_keys_copied")
                s_cv = step.sem("block_values_copied")
                s_up = step.sem("block_update_ready")
                s_st = step.sem("state_ready")
                s_oi = step.sem("inter_block_ready")
                s_dg = step.sem("diagonal_ready")
                s_fs = step.sem("sample_state_decayed")
                s_vb = step.sem("sample_values_spread")
                s_kv = step.sem("sample_outer_product_ready")
                s_os = step.sem("sample_out_ready")
                SPREAD = NS * P // 512

                @block.sync
                def _(sp):
                    for k in range(DC):
                        step.store(sp, io["mem_k_out"][layer, :, k, :], step.mem_k[:, k, :])
                    step.store(sp, io["mem_v_out"][layer], step.mem_v[:])
                    sp.wait_ge(s_st, H4 * NBLK)
                    step.store(sp, io["hgrn_prompt"], state[:, NBLK % 3, :, :])
                    sp.wait_ge(s_kv, 2 * SPREAD)
                    step.store(sp, io["hgrn_sample"], s0[:])

                @block.tensor
                def _(pe):
                    def transposes(n):
                        if n >= 1:
                            pe.wait_ge(s_ck, n)
                            pe.wait_ge(s_cv, n)
                        for which, src in enumerate((kd, vi)):
                            for h in range(H4):
                                cols = slice(h * TP + n * BLK, h * TP + (n + 1) * BLK)
                                last = nc.tensor.transpose(ps[0:BLK, 6 + which, h * P:(h + 1) * P], src[:, cols],
                                                           step.ident)
                        last.then_inc(s_tr, 1)
                    transposes(0)
                    for n in range(NBLK):
                        if n + 1 < NBLK:
                            transposes(n + 1)
                        pe.wait_ge(s_ck, n + 1)
                        pe.wait_ge(s_cv, n + 1)
                        if n >= 2:
                            pe.wait_ge(s_st, H4 * (n - 1))
                        for h in range(H4):
                            nc.tensor.matmul(ps[:, n % 2, h * P:(h + 1) * P], tok[:, n % 2, 0, h * P:(h + 1) * P],
                                             tok[:, n % 2, 1, h * P:(h + 1) * P], start=True, stop=True).then_inc(s_up, 1)
                        if n:
                            for h in range(H4):
                                pe.wait_ge(s_st, H4 * (n - 1) + h + 1)
                                col = (h % 2) * TP + n * BLK
                                nc.tensor.matmul(ps[:, 2 + h // 2, col:col + BLK], state[:, n % 3, h, :],
                                                 qe[:, h * TP + n * BLK:h * TP + (n + 1) * BLK],
                                                 start=True, stop=True).then_inc(s_oi, 1)
                    for k in range(SPREAD):
                        pe.wait_ge(s_dg, 1)
                        if k >= 2:
                            pe.wait_ge(s_kv, 2 * (k - 1) - 1)
                        nc.tensor.matmul(ps[:, 4 + k % 2, :], step.ones,
                                         diag[:, 4 * k:4 * k + 4, :].rearrange("p a b -> p (a b)"),
                                         start=True, stop=True).then_inc(s_vb, 1)
                    pe.wait_ge(s_kv, 2 * SPREAD)
                    pe.wait_ge(s_ck, NBLK)
                    pe.wait_ge(s_cv, NBLK)
                    for c in range(NS):
                        last = nc.tensor.matmul(ps[:, 6, c:c + 1], s0[:, c, :], qs[:, NP + c:NP + c + 1],
                                                start=True, stop=True)
                    last.then_inc(s_os, 1)

                @block.scalar
                def _(act):
                    for n in range(NBLK):
                        act.wait_ge(s_tr, n + 1)
                        if n >= 2:
                            act.wait_ge(s_up, H4 * (n - 1))
                        nc.scalar.activation(tok[:, n % 2, 0, :], ps[0:BLK, 6, :], ACT.Copy).then_inc(s_ck, 1)

                @block.gpsimd
                def _(pool):
                    nc.gpsimd.tensor_tensor(diag[:], step.ident.unsqueeze(1).to_broadcast([P, NS, P]),
                                            vi[:, NP:NP + NS].unsqueeze(2).to_broadcast([P, NS, P]),
                                            ALU.mult).then_inc(s_dg, 1)
                    nc.gpsimd.tensor_tensor(s0[:], s0[:], fg[:, NP:NP + NS].unsqueeze(2).to_broadcast([P, NS, P]),
                                            ALU.mult).then_inc(s_fs, 1)
                    pool.wait_ge(s_fs, 1)

                @block.vector
                def _(dve):
                    for n in range(NBLK):
                        def copy_values(m):
                            dve.wait_ge(s_tr, m + 1)
                            if m >= 2:
                                dve.wait_ge(s_up, H4 * (m - 1))
                            nc.vector.tensor_copy(tok[:, m % 2, 1, :], ps[0:BLK, 7, :]).then_inc(s_cv, 1)
                        if n == 0:
                            copy_values(0)
                        if n + 1 < NBLK:
                            copy_values(n + 1)
                        for h in range(H4):
                            dve.wait_ge(s_up, H4 * (n + 1))
                            if n == 0:
                                ins = nc.vector.tensor_copy(state[:, 1, h, :], ps[:, 0, h * P:(h + 1) * P])
                            else:
                                dve.wait_ge(s_st, H4 * (n - 1) + h + 1)
                                if n >= 3:
                                    dve.wait_ge(s_oi, H4 * (n - 3) + h + 1)
                                end = h * TP + (n + 1) * BLK - 1
                                ins = nc.vector.scalar_tensor_tensor(
                                    out=state[:, (n + 1) % 3, h, :], in0=state[:, n % 3, h, :],
                                    scalar=ecum[:, end:end + 1], in1=ps[:, n % 2, h * P:(h + 1) * P],
                                    op0=ALU.mult, op1=ALU.add)
                            ins.then_inc(s_st, 1)
                    link = lambda ins, wait=True: step.link(dve, "vector", ins, wait)
                    dve.wait_ge(s_oi, H4 * (NBLK - 1))
                    for h in range(H4):
                        o = out_h[:, h * TP + BLK:(h + 1) * TP]
                        nc.vector.tensor_tensor(o, o, ps[:, 2 + h // 2, (h % 2) * TP + BLK:(h % 2 + 1) * TP], ALU.add)
                    dve.wait_ge(s_fs, 1)
                    for k in range(SPREAD):
                        dve.wait_ge(s_vb, k + 1)
                        part = diag[:, 4 * k:4 * k + 4, :]
                        nc.vector.tensor_tensor(part, ps[:, 4 + k % 2, :].rearrange("p (a b) -> p a b", a=4),
                                                kk[:, NP + 4 * k:NP + 4 * k + 4].unsqueeze(2).to_broadcast([P, 4, P]),
                                                ALU.mult).then_inc(s_kv, 1)
                        dve.wait_ge(s_kv, 2 * k + 1)
                        st = s0[:, 4 * k:4 * k + 4, :]
                        nc.vector.tensor_tensor(st, st, part, ALU.add).then_inc(s_kv, 1)
                    dve.wait_ge(s_os, 1)
                    nc.vector.tensor_copy(out_h[:, NP:NP + NS], ps[:, 6, 0:NS])

        with ExitStack() as c1, nc.Block("mixer_gate", no_gpsimd_drain=True) as block:
            sq = sb("head_squares", [P, NP + NS], c1)
            win = sb("window_sums", [P, 2, H4, CTX + TP], c1)
            pooled = sb("pooled", [P, H4, T], c1)
            sums = sb("sample_window_sums", [P, H4, TS], c1)
            s_sq = step.sem("head_squares_ready")
            s_ms = step.sem("head_mean_ready")
            s_sd = step.sem("head_deviation_ready")
            s_win = step.sem("window_sums_ready")
            s_pool = step.sem("pooled_ready")
            s_py = step.sem("pool_product_ready")
            PARTS = ((0, 512), (512, NP), (NP, NP + NS))

            @block.sync
            def _(sp):
                step.store(sp, io["pool_prompt"], u_ext[:, :, TP:TP + CTX])
                step.store(sp, io["pool_sample"], s_ext[:, :, :, 1:CTX + 1])

            @block.gpsimd
            def _(pool):
                src, first = u_ext, 0
                for lev in range(H4):
                    shift = 1 << lev
                    first += shift
                    dst = win[:, lev % 2]
                    if lev:
                        pool.wait_ge(s_win, lev)
                    nc.gpsimd.tensor_tensor(dst[:, lev:, first:], src[:, lev:, first:],
                                            src[:, lev:, first - shift:CTX + TP - shift], ALU.add).then_inc(s_win, 1)
                    pool.wait_ge(s_win, lev + 1)
                    step.link(pool, "gpsimd", nc.gpsimd.tensor_tensor(
                        pooled[:, lev, 0:TP], dst[:, lev, CTX:], inv[:, lev, 0:TP], ALU.mult))
                    src = dst
                nc.gpsimd.tensor_tensor(pooled[:, :, 0:TP], pooled[:, :, 0:TP], u_ext[:, :, CTX:],
                                        ALU.subtract).then_inc(s_pool, 1)
                pool.wait_ge(s_pool, 2)

            @block.tensor
            def _(pe):
                pe.wait_ge(s_sq, 1)
                for k, (a, b) in enumerate(PARTS):
                    last = nc.tensor.matmul(ps[:, k, 0:b - a], step.mean_head, sq[:, a:b], start=True, stop=True)
                last.then_inc(s_ms, 1)
                pe.wait_ge(s_pool, 2)
                for g in range(H4):
                    nc.tensor.matmul(ps[:, 4 + g, 0:T], pw[:, g, :], pooled[:, g, :], start=True,
                                     stop=True).then_inc(s_py, 1)

            @block.scalar
            def _(act):
                nc.scalar.activation(sq[:], out_h[:], ACT.Square).then_inc(s_sq, 1)
                act.wait_ge(s_ms, 1)
                for k, (a, b) in enumerate(PARTS):
                    last = nc.scalar.activation(sq[:, a:b], ps[:, k, 0:b - a], ACT.Sqrt, bias=step.eps)
                last.then_inc(s_sd, 1)
                for g in range(H4):
                    act.wait_ge(s_py, g + 1)
                    nc.scalar.activation(step.mixed[:, H4 + g, :], ps[:, 4 + g, 0:T], ACT.Copy, scale=psc[:, g:g + 1])

            @block.vector
            def _(dve):
                link = lambda ins, wait=True: step.link(dve, "vector", ins, wait)
                for g, w in enumerate(POOL_SIZES):
                    last = nc.vector.reduce_sum(sums[:, g, :], s_ext[:, g, :, CTX + 1 - w:], axis=AX)
                link(last)
                link(nc.vector.tensor_tensor(sums[:], sums[:], inv[:, :, TP:T], ALU.mult))
                nc.vector.tensor_tensor(pooled[:, :, TP:T], sums[:], s_ext[:, :, :, CTX],
                                        ALU.subtract).then_inc(s_pool, 1)
                dve.wait_ge(s_sd, 1)
                link(nc.vector.reciprocal(sq[:], sq[:]))
                link(nc.vector.tensor_tensor(out_h[:], out_h[:], sq[:], ALU.mult))
                for h in range(H4):
                    for lo, hi, a, b in ((0, TP, h * TP, (h + 1) * TP), (TP, T, NP + h * TS, NP + (h + 1) * TS)):
                        nc.vector.scalar_tensor_tensor(out=step.mixed[:, h, lo:hi], in0=out_h[:, a:b],
                                                       scalar=ng[:, h:h + 1], in1=sg[:, a:b],
                                                       op0=ALU.mult, op1=ALU.mult)


def window_mixer(step, layer):
    nc, io, ps = step.nc, step.io, step.ps
    base = step.used
    with ExitStack() as ctx:
        def sb(name, shape, c=ctx):
            return step.sb(name, shape, ctx=c)
        kT = sb("window_k_T", [P, KV, T])
        vt = sb("window_v", [P, 2, KV, P])
        vs = sb("window_v_sample", [TS, KV, P])
        kx = sb("sample_k_T", [P, TS, KV, P])
        vx = sb("sample_v", [P, TS, KV, P])
        snk = sb("sinks", [P, HEADS_C + 1])
        nsnk = sb("negative_sinks", [P, HEADS_C + 1])
        mem = sb("memory_T1", [P, DC, NMEM])
        late = step.sem("window_inputs_ready")
        s_vrow = step.sem("sample_value_row_stored")

        with nc.Block("window_in", no_gpsimd_drain=True) as block:
            s_cp = step.sem("window_chunk_copied")
            number_slabs(step, base, 10)

            @block.sync
            def _(sp):
                step.load_until(sp, base + 12 + SLOTS)

            @block.gpsimd
            def _(pool):
                for dst, name in ((snk[:], "sinks"), (mem[:], "mem"), (kx[:, :, :, 0:P - 1], "window_k"),
                                  (vx[0:P - 1], "window_v")):
                    pool.dma_start(dst, io[name]).then_inc(late, 16)
                for j in range(1, 10):
                    split_low(step, pool, base + j)
                slabs_split(step, pool, base + 9)

            @block.tensor
            def _(pe):
                for j in range(12):
                    if j >= 4:
                        pe.wait_ge(s_cp, j - 3)
                    if j < 10:
                        product(step, pe, base + j, j % 4)
                        continue
                    step.wait_slab(pe, base + j)
                    w = step.slab(base + j)
                    for t, (a, b) in enumerate(((0, P), (P, TP), (TP, T))):
                        for c in range(DC):
                            last = nc.tensor.matmul(ps[0:b - a, j % 4, t * P:(t + 1) * P], step.x[:, c, a:b], w[:, c, :],
                                                    start=(c == 0), stop=(c == DC - 1))
                    last.then_inc(step.product_done, 1)

            @block.scalar
            def _(act):
                split_high(step, act, base + 1)
                for j in range(12):
                    act.wait_ge(step.product_done, step.product_count(base + j))
                    if j + 2 < 10:
                        split_high(step, act, base + j + 2)
                    if j < 8:
                        ins = nc.scalar.activation(step.q[:, j, :], ps[:, j % 4, 0:T], ACT.Copy, scale=HD ** -0.5)
                    elif j < 10:
                        ins = nc.scalar.activation(kT[:, j - 8, :], ps[:, j % 4, 0:T], ACT.Copy)
                    else:
                        nc.scalar.activation(vt[:, :, j - 10, :], ps[:, j % 4, 0:TP].rearrange("p (a b) -> p a b", a=2),
                                             ACT.Copy)
                        ins = nc.scalar.activation(vs[:, j - 10, :], ps[0:TS, j % 4, TP:TP + P], ACT.Copy)
                    ins.then_inc(s_cp, 1)
        step.used += 12

        base = step.used
        with ExitStack() as c1, nc.Block("window_prompt", no_gpsimd_drain=True) as block:
            sc = sb("scores", [P, 2, 3 * P], c1)
            pt = sb("probabilities_T", [P, 2, 3 * P], c1)
            neg = sb("negative_maxima", [P, 2, 2], c1)
            den = sb("denominators", [P, 2, 2], c1)
            esk = sb("sink_terms", [P, 2, 2], c1)
            s_s = step.sem("window_scores_ready")
            s_mk = step.sem("window_scores_masked")
            s_m = step.sem("window_maxima_ready")
            s_e = step.sem("window_exp_ready")
            s_p = step.sem("window_probabilities_ready")
            s_t = step.sem("window_transposed")
            s_pt = step.sem("window_transposed_copied")
            s_o = step.sem("window_output_ready")
            s_oc = step.sem("window_output_copied")
            s_mem = step.sem("memory_chunk_copied1")
            QK = ((0, P), (P, 3 * P))

            @block.sync
            def _(sp):
                sp.dma_start(vx[P - 1:P], vs[:]).then_inc(s_vrow, 16)
                step.store(sp, io["window_k_prompt"], kT[0:HD, :, P:TP])
                step.store(sp, io["window_v_prompt"], vt[:, 1, :, 0:HD])
                step.load_until(sp, base + 16 + SLOTS)

            @block.tensor
            def _(pe):
                def scores(h):
                    e, j, kv = h % 2, h // 2, h // (HEADS_C // KV)
                    rows = slice(e * HD, (e + 1) * HD)
                    if h >= 2:
                        pe.wait_ge(s_mk, h - 1)
                    nc.tensor.matmul(ps[:, h % 2, 0:P], step.q[rows, j, 0:P], kT[rows, kv, 0:P], start=True, stop=True)
                    nc.tensor.matmul(ps[:, h % 2, P:3 * P], step.q[rows, j, P:TP], kT[rows, kv, 0:TP], start=True,
                                     stop=True).then_inc(s_s, 1)

                def transposes(h):
                    pe.wait_ge(s_p, h + 1)
                    if h >= 2:
                        pe.wait_ge(s_pt, h - 1)
                    for k in range(3):
                        last = nc.tensor.transpose(ps[:, 2 + h % 2, k * P:(k + 1) * P], sc[:, h % 2, k * P:(k + 1) * P],
                                                   step.ident)
                    last.then_inc(s_t, 1)

                def values(h):
                    kv = h // (HEADS_C // KV)
                    pe.wait_ge(s_pt, h + 1)
                    if h >= 2:
                        pe.wait_ge(s_oc, h - 1)
                    bank = ps[:, 4 + h % 2, :]
                    nc.tensor.matmul(bank[:, 0:P], vt[:, 0, kv, :], pt[:, h % 2, 0:P], start=True, stop=True)
                    nc.tensor.matmul(bank[:, P:TP], vt[:, 0, kv, :], pt[:, h % 2, P:2 * P], start=True, stop=False)
                    nc.tensor.matmul(bank[:, P:TP], vt[:, 1, kv, :], pt[:, h % 2, 2 * P:3 * P], start=False,
                                     stop=True).then_inc(s_o, 1)

                pe.wait_ge(late, 64)
                scores(0)
                for h in range(HEADS_C):
                    memory_product(step, pe, base + h, h, mem, 6 + h % 2, s_mem)
                    if h + 1 < HEADS_C:
                        scores(h + 1)
                    transposes(h)
                    if h:
                        values(h - 1)
                values(HEADS_C - 1)

            @block.vector
            def _(dve):
                link = lambda ins, wait=True: step.link(dve, "vector", ins, wait)
                dve.wait_ge(late, 64)
                link(nc.vector.tensor_scalar(nsnk[:], snk[:], -1.0, None, ALU.mult))

                def head_scores(h):
                    b = h % 2
                    dve.wait_ge(s_s, h + 1)
                    if h >= 2:
                        dve.wait_ge(s_t, h - 1)
                    nc.vector.tensor_tensor(sc[:, b, :], ps[:, b, 0:3 * P], step.masks, ALU.add).then_inc(s_mk, 1)
                    dve.wait_ge(s_mk, h + 1)
                    for t, (lo, hi) in enumerate(QK):
                        last = nc.vector.tensor_reduce(neg[:, b, t:t + 1], sc[:, b, lo:hi], AX, ALU.max, negate=True)
                    link(last)
                    nc.vector.tensor_scalar(neg[:, b, :], neg[:, b, :], nsnk[:, h:h + 1], None, ALU.min).then_inc(s_m, 1)

                def head_rest(h):
                    b = h % 2
                    dve.wait_ge(s_e, h + 1)
                    link(nc.vector.tensor_tensor(den[:, b, :], den[:, b, :], esk[:, b, :], ALU.add))
                    link(nc.vector.reciprocal(den[:, b, :], den[:, b, :]))
                    for t, (lo, hi) in enumerate(QK):
                        last = nc.vector.tensor_scalar(sc[:, b, lo:hi], sc[:, b, lo:hi], den[:, b, t:t + 1], None, ALU.mult)
                    last.then_inc(s_p, 1)

                def head_out(h):
                    e = h % 2
                    rows = slice(e * HD, (e + 1) * HD)
                    dve.wait_ge(s_o, h + 1)
                    nc.vector.tensor_copy(step.mixed[rows, h // 2, 0:TP], ps[rows, 4 + h % 2, 0:TP]).then_inc(s_oc, 1)

                for h in range(HEADS_C):
                    head_scores(h)
                    if h >= 1:
                        head_rest(h - 1)
                    if h >= 3:
                        head_out(h - 3)
                head_rest(HEADS_C - 1)
                for h in range(HEADS_C - 3, HEADS_C):
                    head_out(h)

            @block.scalar
            def _(act):
                def head_exp(h):
                    b = h % 2
                    act.wait_ge(s_m, h + 1)
                    if h >= 2:
                        act.wait_ge(s_p, h - 1)
                    for t, (lo, hi) in enumerate(QK):
                        nc.scalar.activation(sc[:, b, lo:hi], sc[:, b, lo:hi], ACT.Exp, bias=neg[:, b, t:t + 1],
                                             accum_out=den[:, b, t:t + 1])
                    nc.scalar.activation(esk[:, b, :], neg[:, b, :], ACT.Exp, bias=snk[:, h:h + 1]).then_inc(s_e, 1)

                def head_copy(h):
                    act.wait_ge(s_t, h + 1)
                    if h >= 2:
                        act.wait_ge(s_o, h - 1)
                    nc.scalar.activation(pt[:, h % 2, :], ps[:, 2 + h % 2, 0:3 * P], ACT.Copy).then_inc(s_pt, 1)

                for h in range(HEADS_C):
                    head_exp(h)
                    if h:
                        head_copy(h - 1)
                    memory_copy(step, act, base + h, h, 6 + h % 2, s_mem)
                head_copy(HEADS_C - 1)
        step.used += 16

        with ExitStack() as c1, nc.Block("window_sample", no_gpsimd_drain=True) as block:
            st = sb("sample_scores_T", [P, P], c1)
            ss = sb("sample_scores", [P, P], c1)
            sp_t = sb("sample_probabilities_T", [P, P], c1)
            sm = sb("sample_small", [P, 3], c1)
            s_k = step.sem("sample_key_column_ready")
            s_s = step.sem("sample_scores_T_ready")
            s_sc = step.sem("sample_scores_T_copied")
            s_t = step.sem("sample_scores_ready")
            s_m = step.sem("sample_maxima_ready")
            s_e = step.sem("sample_exp_ready")
            s_p = step.sem("sample_probabilities_ready")
            s_pt = step.sem("sample_probabilities_T_ready")
            s_pc = step.sem("sample_probabilities_T_copied")
            s_o = step.sem("sample_output_ready")

            @block.sync
            def _(sp):
                for k in range(DC):
                    step.store(sp, io["mem_k_out"][layer, :, k, :], step.mem_k[:, k, :])
                step.store(sp, io["mem_v_out"][layer], step.mem_v[:])
                sp.wait_ge(s_k, 1)
                step.store(sp, io["window_k_sample"], kx[0:HD])
                sp.wait_ge(s_vrow, 16)
                step.store(sp, io["window_v_sample"], vx[:, :, :, 0:HD])

            @block.tensor
            def _(pe):
                pe.wait_ge(s_k, 1)
                for b in range(TS):
                    for kv in range(KV):
                        for e in range(2):
                            rows = slice(e * HD, (e + 1) * HD)
                            col = (b * KV + kv) * 4
                            last = nc.tensor.matmul(ps[:, 4 * e, col:col + 4], kx[rows, b, kv, :],
                                                    step.q[rows, kv * 4:kv * 4 + 4, TP + b], start=True, stop=True)
                last.then_inc(s_s, 1)
                pe.wait_ge(s_sc, 1)
                nc.tensor.transpose(ps[:, 1, 0:P], st[:], step.ident).then_inc(s_t, 1)
                pe.wait_ge(s_p, 1)
                nc.tensor.transpose(ps[:, 2, 0:P], ss[:], step.ident).then_inc(s_pt, 1)
                pe.wait_ge(s_pc, 1)
                pe.wait_ge(s_vrow, 16)
                for b in range(TS):
                    for kv in range(KV):
                        col = (b * KV + kv) * 8
                        last = nc.tensor.matmul(ps[:, 3, col:col + 8], vx[:, b, kv, :], sp_t[:, col:col + 8],
                                                start=True, stop=True)
                last.then_inc(s_o, 1)

            @block.scalar
            def _(act):
                act.wait_ge(s_m, 1)
                nc.scalar.activation(ss[:], ss[:], ACT.Exp, bias=sm[:, 0:1], accum_out=sm[:, 1:2])
                nc.scalar.activation(sm[:, 2:3], sm[:, 0:1], ACT.Exp, bias=snk[:, HEADS_C:]).then_inc(s_e, 1)
                act.wait_ge(s_pt, 1)
                nc.scalar.activation(sp_t[:], ps[:, 2, 0:P], ACT.Copy).then_inc(s_pc, 1)

            @block.vector
            def _(dve):
                link = lambda ins, wait=True: step.link(dve, "vector", ins, wait)
                nc.vector.tensor_copy(kx[:, :, :, P - 1], kT[:, :, TP:T].rearrange("p k b -> p b k")).then_inc(s_k, 1)
                dve.wait_ge(s_s, 1)
                for e in range(2):
                    last = nc.vector.tensor_copy(st[:].rearrange("p (g e j) -> p g e j", e=2, j=4)[:, :, e],
                                                 ps[:, 4 * e, 0:HD].rearrange("p (g j) -> p g j", j=4))
                last.then_inc(s_sc, 1)
                dve.wait_ge(s_t, 1)
                link(nc.vector.tensor_copy(ss[:], ps[:, 1, 0:P]))
                link(nc.vector.tensor_reduce(sm[:, 0:1], ss[:], AX, ALU.max, negate=True))
                nc.vector.tensor_scalar(sm[:, 0:1], sm[:, 0:1], nsnk[:, HEADS_C:], None, ALU.min).then_inc(s_m, 1)
                dve.wait_ge(s_e, 1)
                link(nc.vector.tensor_tensor(sm[:, 1:2], sm[:, 1:2], sm[:, 2:3], ALU.add))
                link(nc.vector.reciprocal(sm[:, 1:2], sm[:, 1:2]))
                nc.vector.tensor_scalar(ss[:], ss[:], sm[:, 1:2], None, ALU.mult).then_inc(s_p, 1)
                dve.wait_ge(s_o, 1)
                o = ps[:, 3, 0:P].rearrange("p (b k e j) -> p k e j b", b=TS, k=KV, e=2)
                dst = step.mixed[:].rearrange("p (k j) t -> p k j t", k=KV)
                for e in range(2):
                    rows = slice(e * HD, (e + 1) * HD)
                    nc.vector.tensor_copy(dst[rows, :, :, TP:T], o[rows, :, e])


def cross_attention(step, layer):
    nc, io, ps = step.nc, step.io, step.ps
    base = step.used
    L = f"_{layer}"
    ck, cv = step.cache
    NR = MH * TS
    with ExitStack() as ctx:
        own = step.own[:, 0:TS * MH * 2 * NR]
        own_row = bass.AP(step.own, 0, [step.own[:].ap[0], [MH * 2 * NR + MH, TS], [2 * NR + 1, MH], [NR, 2]])
        number_slabs(step, base, DC)
        with nc.Block("cross_query" + L, no_gpsimd_drain=True) as block:
            s_cp = step.sem("query_chunk_copied" + L)

            @block.gpsimd
            def _(pool):
                for j in range(1, DC):
                    split_low(step, pool, base + j)
                slabs_split(step, pool, base + DC - 1)

            @block.sync
            def _(sp):
                for j in range(DC):
                    step.load_cache(sp, layer, 1, j)
                    step.load_until(sp, base + j + 1 + SLOTS)

            @block.tensor
            def _(pe):
                for j in range(DC):
                    if j >= 4:
                        pe.wait_ge(s_cp, j - 3)
                    product(step, pe, base + j, j % 4)

            @block.scalar
            def _(act):
                split_high(step, act, base + 1)
                for j in range(DC):
                    act.wait_ge(step.product_done, step.product_count(base + j))
                    if j + 2 < DC:
                        split_high(step, act, base + j + 2)
                    nc.scalar.activation(step.q[:, j, :], ps[:, j % 4, 0:T], ACT.Copy, scale=MHD ** -0.5).then_inc(s_cp, 1)
        step.used += DC

        with ExitStack() as c1, nc.Block("cross_attention" + L, no_gpsimd_drain=True) as block:
            room = step.squares[:].rearrange("p c t -> p (c t)")
            pr = room[:, 0:4 * NMEM].rearrange("p (a b m) -> p a b m", a=2, b=2)
            pt = room[:, 4 * NMEM:4 * NMEM + 4 * TP].rearrange("p (a b t) -> p a b t", a=2, b=2)
            sm = step.sb("cross_small" + L, [P, 2, 2, 2], ctx=c1)
            ss = step.sb("cross_sample_p" + L, [NR, NMEM], ctx=c1)
            ssm = step.sb("cross_sample_small" + L, [NR, 2], ctx=c1)
            s_ks = step.sem("cross_sample_scores_made" + L)
            s_vs = step.sem("cross_sample_values_made" + L)
            s_s = step.sem("cross_scores_ready" + L)
            s_m = step.sem("cross_maxima_ready" + L)
            s_e = step.sem("cross_exp_ready" + L)
            s_p = step.sem("cross_probabilities_ready" + L)
            s_t = step.sem("cross_transposed" + L)
            s_pt = step.sem("cross_transposed_copied" + L)
            s_o = step.sem("cross_output_ready" + L)
            s_oc = step.sem("cross_output_copied" + L)
            s_sq = step.sem("cross_sample_queries_placed" + L)
            s_zero = step.sem("cross_own_rows_zeroed" + L)

            @block.gpsimd
            def _(pool):
                nc.gpsimd.memset(own, 0.0).then_inc(s_zero, 1)
                pool.wait_ge(s_zero, 1)
            s_sm = step.sem("cross_sample_maxima_ready" + L)
            s_se = step.sem("cross_sample_exp_ready" + L)
            s_sp = step.sem("cross_sample_probabilities_ready" + L)
            s_st = step.sem("cross_sample_probabilities_transposed" + L)
            s_sy = step.sem("cross_sample_probabilities_copied" + L)
            s_so = step.sem("cross_sample_output_copied" + L)
            s_sot = step.sem("cross_sample_output_transposed" + L)

            @block.tensor
            def _(pe):
                def scores(h):
                    if h >= 2:
                        pe.wait_ge(s_e, h - 1)
                    for t in range(2):
                        for c in range(2):
                            last = nc.tensor.matmul(ps[:, h % 2, t * NMEM:(t + 1) * NMEM],
                                                    step.q[:, 2 * h + c, t * P:(t + 1) * P], step.mem_k[:, 2 * h + c, :],
                                                    start=(c == 0), stop=(c == 1))
                    last.then_inc(s_s, 1)

                def transposes(h):
                    pe.wait_ge(s_p, h + 1)
                    if h >= 2:
                        pe.wait_ge(s_pt, h - 1)
                    for m in range(2):
                        for t in range(2):
                            col = m * TP + t * P
                            last = nc.tensor.transpose(ps[:, 2 + h % 2, col:col + P], pr[:, h % 2, t, m * P:(m + 1) * P],
                                                       step.ident)
                    last.then_inc(s_t, 1)

                def values(h):
                    pe.wait_ge(s_pt, h + 1)
                    if h >= 2:
                        pe.wait_ge(s_oc, h - 1)
                    for d in range(2):
                        for m in range(2):
                            f = h * MHD + d * P
                            last = nc.tensor.matmul(ps[:, 4 + h % 2, d * TP:(d + 1) * TP], step.mem_v[:, m, f:f + P],
                                                    pt[:, h % 2, m, :], start=(m == 0), stop=(m == 1))
                    last.then_inc(s_o, 1)

                def left(b, h, c):
                    col = ((b * MH + h) * 2 + c) * NR
                    return own[:, col:col + NR]

                def sample_scores(b):
                    pe.wait_ge(step.cache_ready[0], 16 * TS)
                    for h in range(MH):
                        for c in range(2):
                            last = nc.tensor.matmul(ps[0:NR, 6, 0:NMEM], left(b, h, c), ck[:, b, 2 * h + c, :],
                                                    start=(b + h + c == 0), stop=(b == TS - 1 and h == MH - 1 and c == 1))
                    if b == TS - 1:
                        last.then_inc(s_ks, 1)

                def sample_transpose():
                    pe.wait_ge(s_sp, 1)
                    for m in range(2):
                        last = nc.tensor.transpose(ps[:, 7, 256 + m * NR:256 + (m + 1) * NR], ss[:, m * P:(m + 1) * P],
                                                   step.ident[0:NR, 0:NR])
                    last.then_inc(s_st, 1)

                def sample_values(b):
                    pe.wait_ge(step.cache_ready[1], 16 * TS)
                    for h in range(MH):
                        for m in range(2):
                            last = nc.tensor.matmul(ps[0:NR, 6, 0:MHD], left(b, h, m), cv[:, b, m, h * MHD:(h + 1) * MHD],
                                                    start=(b + h + m == 0), stop=(b == TS - 1 and h == MH - 1 and m == 1))
                    if b == TS - 1:
                        last.then_inc(s_vs, 1)

                scores(0)
                scores(1)
                pe.wait_ge(s_sq, 1)
                for h in range(2):
                    for b in (4 * h, 4 * h + 1):
                        sample_scores(b)
                    transposes(h)
                    for b in (4 * h + 2, 4 * h + 3):
                        sample_scores(b)
                    values(h)
                    scores(h + 2)
                transposes(2)
                values(2)
                sample_transpose()
                transposes(3)
                pe.wait_ge(s_sy, 1)
                for b in range(4):
                    sample_values(b)
                values(3)
                for b in range(4, TS):
                    sample_values(b)
                pe.wait_ge(s_so, 1)
                for d in range(2):
                    last = nc.tensor.transpose(ps[:, 7, d * NR:(d + 1) * NR], ss[:, d * P:(d + 1) * P],
                                               step.ident[0:NR, 0:NR])
                last.then_inc(s_sot, 1)

            @block.scalar
            def _(act):
                def head_exp(h):
                    act.wait_ge(s_m, h + 1)
                    if h >= 2:
                        act.wait_ge(s_t, h - 1)
                    for t in range(2):
                        last = nc.scalar.activation(pr[:, h % 2, t, :], ps[:, h % 2, t * NMEM:(t + 1) * NMEM], ACT.Exp,
                                                    bias=sm[:, h % 2, 0, t:t + 1], accum_out=sm[:, h % 2, 1, t:t + 1])
                    last.then_inc(s_e, 1)

                def head_copy(h):
                    act.wait_ge(s_t, h + 1)
                    if h >= 2:
                        act.wait_ge(s_o, h - 1)
                    nc.scalar.activation(pt[:, h % 2].rearrange("p a b -> p (a b)"), ps[:, 2 + h % 2, :],
                                         ACT.Copy).then_inc(s_pt, 1)
                act.wait_ge(s_zero, 1)
                nc.scalar.activation(own_row, step.q[:, :, TP:T].rearrange("p (h c) b -> p b h c", h=MH),
                                     ACT.Copy).then_inc(s_sq, 1)
                head_exp(0)
                head_exp(1)
                head_copy(0)
                head_exp(2)
                head_copy(1)
                act.wait_ge(s_sm, 1)
                nc.scalar.activation(ss[:], ps[0:NR, 6, 0:NMEM], ACT.Exp, bias=ssm[:, 0:1],
                                     accum_out=ssm[:, 1:2]).then_inc(s_se, 1)
                head_exp(3)
                head_copy(2)
                act.wait_ge(s_st, 1)
                nc.scalar.activation(own_row, ps[:, 7, 256:256 + 2 * NR].rearrange("p (c b h) -> p b h c", c=2, b=TS),
                                     ACT.Copy).then_inc(s_sy, 1)
                head_copy(3)
                act.wait_ge(s_vs, 1)
                nc.scalar.activation(ss[:], ps[0:NR, 6, 0:MHD], ACT.Copy).then_inc(s_so, 1)

            @block.vector
            def _(dve):
                link = lambda ins, wait=True: step.link(dve, "vector", ins, wait)

                def head_max(h):
                    dve.wait_ge(s_s, h + 1)
                    if h >= 2:
                        dve.wait_ge(s_p, h - 1)
                    nc.vector.tensor_reduce(sm[:, h % 2, 0, :], ps[:, h % 2, :].rearrange("p (t m) -> p t m", t=2), AX,
                                            ALU.max, negate=True).then_inc(s_m, 1)

                def head_norm(h):
                    dve.wait_ge(s_e, h + 1)
                    link(nc.vector.reciprocal(sm[:, h % 2, 1, :], sm[:, h % 2, 1, :]))
                    for t in range(2):
                        last = nc.vector.tensor_scalar(pr[:, h % 2, t, :], pr[:, h % 2, t, :], sm[:, h % 2, 1, t:t + 1],
                                                       None, ALU.mult)
                    last.then_inc(s_p, 1)

                def head_out(h):
                    dve.wait_ge(s_o, h + 1)
                    nc.vector.tensor_copy(step.mixed[:, 2 * h:2 * h + 2, 0:TP],
                                          ps[:, 4 + h % 2, :].rearrange("p (d t) -> p d t", d=2)).then_inc(s_oc, 1)

                head_max(0)
                head_max(1)
                head_norm(0)
                head_max(2)
                head_norm(1)
                head_out(0)
                dve.wait_ge(s_ks, 1)
                nc.vector.tensor_reduce(ssm[:, 0:1], ps[0:NR, 6, 0:NMEM], AX, ALU.max, negate=True).then_inc(s_sm, 1)
                head_max(3)
                head_norm(2)
                head_out(1)
                dve.wait_ge(s_se, 1)
                link(nc.vector.reciprocal(ssm[:, 1:2], ssm[:, 1:2]))
                nc.vector.tensor_scalar(ss[:], ss[:], ssm[:, 1:2], None, ALU.mult).then_inc(s_sp, 1)
                head_norm(3)
                head_out(2)
                head_out(3)
                dve.wait_ge(s_sot, 1)
                nc.vector.tensor_copy(step.mixed[:, :, TP:T].rearrange("p (h d) b -> p d b h", h=MH),
                                      ps[:, 7, 0:2 * NR].rearrange("p (d b h) -> p d b h", d=2, b=TS))


TILES = ((0, P), (P, TP), (TP, T))


def peer(step, layer):
    nc, io, ps = step.nc, step.io, step.ps
    L = f"_{layer}"
    with ExitStack() as ctx:
        big = step.sb("expert_activations" + L, [P, NKEYS, T], ctx=ctx)
        qT = big[:, NKEYS - 2 * PH:, :]
        FIRST_BORROWED = NKEYS - 48
        scratch = big[:, FIRST_BORROWED:NKEYS - 2 * PH, :].rearrange("p a b -> p (a b)")
        pick = step.sb("selections" + L, [P, 3, 3, P], ctx=ctx)
        with ExitStack() as c1:
            keys_ready = step.sem("subkeys_ready" + L)
            peer_query(step, layer, qT, scratch[:, 0:2 * PH * P], keys_ready)
            peer_up(step, layer, big, qT, scratch, pick, keys_ready, FIRST_BORROWED)
        with ExitStack() as c1:
            selT = step.sb("selections_T" + L, [P, 3, T], ctx=c1)
            peer_gates(step, layer, big, pick, selT, c1)
        peer_down(step, layer, big)


def peer_query(step, layer, qT, keys, keys_ready):
    nc, io, ps = step.nc, step.io, step.ps
    L = f"_{layer}"
    base = step.used
    NQ = 2 * PH
    number_slabs(step, base, NQ)
    with nc.Block("peer_query" + L, no_gpsimd_drain=True) as block:
        s_cp = step.sem("peer_query_chunk_copied" + L)

        @block.sync
        def _(sp):
            sp.dma_start(keys, io["subkeys"][layer]).then_inc(keys_ready, 16)
            step.load_until(sp, base + NQ + SLOTS)

        @block.tensor
        def _(pe):
            for j in range(NQ):
                if j >= 4:
                    pe.wait_ge(s_cp, j - 3)
                product(step, pe, base + j, j % 4)

        @block.gpsimd
        def _(pool):
            for j in range(1, NQ):
                split_low(step, pool, base + j)
            slabs_split(step, pool, base + NQ - 1)

        @block.scalar
        def _(act):
            split_high(step, act, base + 1)
            for j in range(NQ):
                act.wait_ge(step.product_done, step.product_count(base + j))
                if j + 2 < NQ:
                    split_high(step, act, base + j + 2)
                nc.scalar.activation(qT[:, j, :], ps[:, j % 4, 0:T], ACT.Copy).then_inc(s_cp, 1)
    step.used += NQ


def peer_up(step, layer, big, qT, scratch, pick, keys_ready, first_borrowed):
    nc, io, ps = step.nc, step.io, step.ps
    L = f"_{layer}"
    base = step.used
    ub = step.slabs[base][1]
    keys = scratch[:, 0:2 * PH * P].rearrange("p (k n) -> p k n", n=P)
    xh, xl = step.operand
    with ExitStack() as c1, nc.Block("peer_up" + L, no_gpsimd_drain=True) as block:
        hi = step.sb("u_hi" + L, [P, 4, HC, P], F32R, ctx=c1)
        lo = step.sb("u_lo" + L, [P, 4, HC, P], F32R, ctx=c1)
        s_hi = step.sem("u_hi_ready" + L)
        s_h = step.sem("up_half_product_ready" + L)
        s_g = step.sem("up_product_read" + L)
        s_sc = step.sem("routing_scores_ready" + L)
        s_sr = step.sem("routing_scores_read" + L)
        s_rt = step.sem("routing_done" + L)
        SPLIT = (0, 8, 28, NKEYS)

        @block.sync
        def _(sp):
            with sp.Fori(1, NKEYS // SLOTS) as i:
                for s in range(SLOTS):
                    sp.wait_ge(step.u_split, 2 * (ub + SLOTS * i + s + 1 - SLOTS))
                    sp.dma_start(step.ring[:, s, :], io["u"][layer * P + SLOTS * i + s]).then_inc(step.slab_ready[s], 16)
            step.loaded = base + NKEYS
            step.load_until(sp, base + NKEYS + SLOTS)

        def ready(i):
            return 16 * (base // SLOTS + 1) + 16 * i

        @block.gpsimd
        def _(pool):
            def split(i, s):
                for g in range(2):
                    pool.wait_ge(s_hi, 2 * (SLOTS * i + s) + g + 1)
                    buf = (2 * s + g) % 4
                    nc.gpsimd.tensor_tensor(lo[:, buf], step.slab(s)[:, g * HC:(g + 1) * HC, :], hi[:, buf].bitcast(F32),
                                            ALU.subtract).then_inc(step.u_split, 1)
            with pool.Fori(0, NKEYS // SLOTS) as i:
                for s in range(SLOTS):
                    split(i, s)
            pool.wait_ge(step.u_split, 2 * (ub + NKEYS))

        @block.tensor
        def _(pe):
            def scores(t):
                a, b = TILES[t]
                if t:
                    pe.wait_ge(s_sr, t)
                else:
                    pe.wait_ge(keys_ready, 16)
                for k in range(2 * PH):
                    last = nc.tensor.matmul(ps[0:b - a, 2 + k // 4, (k % 4) * P:(k % 4 + 1) * P], qT[:, k, a:b], keys[:, k, :],
                                            start=True, stop=True)
                last.then_inc(s_sc, 1)

            def up(i, s, first):
                if not (first and s < 2):
                    pe.wait_ge(s_g, SLOTS * i + s - 1)
                bank = ps[:, s % 2, 0:T]
                for g in range(2):
                    pe.wait_ge(step.u_split, 2 * (ub + SLOTS * i + s) + g + 1)
                    buf = (2 * s + g) % 4
                    for k in range(HC):
                        c = g * HC + k
                        nc.tensor.matmul(bank, hi[:, buf, k, :], xh[:, c, :], start=(c == 0), stop=False)
                        nc.tensor.matmul(bank, hi[:, buf, k, :], xl[:, c, :], start=False, stop=False)
                        last = nc.tensor.matmul(bank, lo[:, buf, k, :], xh[:, c, :], start=False, stop=(c == DC - 1))
                    last.then_inc(s_h, 1)

            scores(0)
            for s in range(SLOTS):
                up(0, s, True)
            for t in range(3):
                if t:
                    scores(t)
                with pe.Fori(max(1, SPLIT[t] // SLOTS), SPLIT[t + 1] // SLOTS) as i:
                    for s in range(SLOTS):
                        up(i, s, False)

        @block.scalar
        def _(act):
            def high(i, s, g, first=False):
                if g == 0:
                    act.wait_ge(step.slab_ready[s], ready(i))
                if not first:
                    act.wait_ge(s_h, 2 * (SLOTS * i + s) + g - 3)
                buf = (2 * s + g) % 4
                nc.scalar.activation(hi[:, buf], step.slab(s)[:, g * HC:(g + 1) * HC, :], ACT.Copy).then_inc(s_hi, 1)

            def gelu(i, s):
                act.wait_ge(s_h, 2 * (SLOTS * i + s) + 2)
                nc.scalar.activation(big[:, SLOTS * i + s, :], ps[:, s % 2, 0:T], ACT.Gelu_apprx_tanh).then_inc(s_g, 1)

            nc.scalar.preload_act_table(ACT.Gelu_apprx_tanh)
            for s in range(2):
                for g in range(2):
                    high(0, s, g, first=True)
            for lo_i, hi_i in ((0, first_borrowed // SLOTS), (first_borrowed // SLOTS, NKEYS // SLOTS - 1)):
                if lo_i:
                    act.wait_ge(s_rt, 3)
                with act.Fori(lo_i, hi_i) as i:
                    for s in range(SLOTS):
                        ahead = (i, s + 2) if s < 2 else (i + 1, s - 2)
                        high(*ahead, 0)
                        gelu(i, s)
                        high(*ahead, 1)
            final = NKEYS // SLOTS - 1
            for s in range(SLOTS):
                if s < 2:
                    high(final, s + 2, 0)
                gelu(final, s)
                if s < 2:
                    high(final, s + 2, 1)

        @block.vector
        def _(dve):
            link = lambda ins, wait=True: step.link(dve, "vector", ins, wait)
            at = 2 * PH * P

            def take(n, dt=F32):
                nonlocal at
                at += n
                v = scratch[:, at - n:at]
                return v if dt == F32 else v.bitcast(dt)
            NQ = 2 * PH
            rest = take(NQ * P).rearrange("p (k n) -> p k n", n=P)
            val = take(NQ * TOPK).rearrange("p (k n) -> p k n", n=TOPK)
            idx = take(NQ * TOPK, U32).rearrange("p (k n) -> p k n", n=TOPK)
            idxf = take(NQ * TOPK).rearrange("p (h q n) -> p h q n", h=PH, q=2)
            cand = take(PH * TOPK * TOPK).rearrange("p (h n) -> p h n", h=PH)
            best = take(PH * TOPK).rearrange("p (h n) -> p h n", h=PH)
            sel = take(PH * TOPK, U32).rearrange("p (h n) -> p h n", h=PH)
            part = take(PH * TOPK, U32).rearrange("p (h n) -> p h n", h=PH)
            partf = take(PH * TOPK).rearrange("p (h n) -> p h n", h=PH)
            cand2 = rest.rearrange("p k n -> p (k n)").rearrange("p (h n) -> p h n", h=PH)
            for t, (a, b) in enumerate(TILES):
                n = b - a
                r = slice(0, n)
                dve.wait_ge(s_sc, t + 1)
                score = lambda k: ps[r, 2 + k // 4, (k % 4) * P:(k % 4 + 1) * P]
                for k in range(NQ):
                    last = nc.vector.max(val[r, k, 0:8], score(k))
                link(last)
                for k in range(NQ):
                    nc.vector.max_index(idx[r, k, 0:8], val[r, k, 0:8], score(k))
                    last = nc.vector.match_replace(out=rest[r, k, :], in_to_replace=val[r, k, 0:8], in_values=score(k),
                                                   imm_value=LOWEST)
                last.then_inc(s_sr, 1)
                dve.wait_ge(s_sr, t + 1)
                for k in range(NQ):
                    last = nc.vector.max(val[r, k, 8:16], rest[r, k, :])
                link(last)
                for k in range(NQ):
                    last = nc.vector.max_index(idx[r, k, 8:16], val[r, k, 8:16], rest[r, k, :])
                v4 = val.rearrange("p (h q) n -> p h q n", h=PH)
                shape = [n, PH, TOPK, TOPK]
                link(nc.vector.tensor_tensor(cand[r].rearrange("p h (a b) -> p h a b", a=TOPK),
                                             v4[r, :, 0, :].unsqueeze(3).to_broadcast(shape),
                                             v4[r, :, 1, :].unsqueeze(2).to_broadcast(shape), ALU.add))
                link(nc.vector.tensor_copy(idxf[r].rearrange("p h q n -> p (h q n)"), idx[r].rearrange("p k n -> p (k n)")))
                for h in range(PH):
                    last = nc.vector.max(best[r, h, 0:8], cand[r, h, :])
                link(last)
                for h in range(PH):
                    nc.vector.max_index(sel[r, h, 0:8], best[r, h, 0:8], cand[r, h, :])
                    last = nc.vector.match_replace(out=cand2[r, h, :], in_to_replace=best[r, h, 0:8],
                                                   in_values=cand[r, h, :], imm_value=LOWEST)
                link(last)
                for h in range(PH):
                    last = nc.vector.max(best[r, h, 8:16], cand2[r, h, :])
                link(last)
                for h in range(PH):
                    last = nc.vector.max_index(sel[r, h, 8:16], best[r, h, 8:16], cand2[r, h, :])
                nc.vector.tensor_tensor(pick[r, t, 2, :].rearrange("p (h n) -> p h n", h=PH), best[r],
                                        best[r, :, 0:1].to_broadcast([n, PH, TOPK]), ALU.subtract)
                link(last)
                for half, (op, by) in enumerate(((ALU.logical_shift_right, 4), (ALU.bitwise_and, TOPK - 1))):
                    link(nc.vector.tensor_scalar(part[r], sel[r], by, None, op))
                    link(nc.vector.tensor_copy(partf[r], part[r]))
                    eq = cand[r].rearrange("p h (k a) -> p (h k) a", k=TOPK)
                    link(nc.vector.tensor_tensor(eq, partf[r].rearrange("p h n -> p (h n)").unsqueeze(2)
                                                 .to_broadcast([n, PH * TOPK, TOPK]),
                                                 step.iota[r, 0:TOPK].unsqueeze(1).to_broadcast([n, PH * TOPK, TOPK]),
                                                 ALU.is_equal))
                    e4 = cand[r].rearrange("p h (k a) -> p h k a", k=TOPK)
                    link(nc.vector.tensor_tensor(e4, e4, idxf[r, :, half, :].unsqueeze(2).to_broadcast(shape), ALU.mult))
                    link(nc.vector.reduce_sum(pick[r, t, half, :], eq, axis=AX))
                nc.vector.tensor_copy(partf[r, 0, 0:1], part[r, 0, 0:1]).then_inc(s_rt, 1)
    step.used += NKEYS


def peer_gates(step, layer, big, pick, selT, ctx):
    nc, ps = step.nc, step.ps
    L = f"_{layer}"
    with ExitStack() as c1, nc.Block("peer_softmax" + L, no_gpsimd_drain=True) as block:
        den = step.sb("gate_sums" + L, [P, 3, PH], ctx=c1)
        s_e = step.sem("gate_exp_ready" + L)
        s_w = step.sem("gates_ready" + L)
        s_t = step.sem("selections_transposed" + L)
        s_c = step.sem("selections_copied" + L)

        @block.scalar
        def _(act):
            for t, (a, b) in enumerate(TILES):
                w = pick[0:b - a, t, 2, :]
                nc.scalar.activation(w, w, ACT.Exp).then_inc(s_e, 1)

        @block.vector
        def _(dve):
            link = lambda ins, wait=True: step.link(dve, "vector", ins, wait)
            for t, (a, b) in enumerate(TILES):
                n = b - a
                dve.wait_ge(s_e, t + 1)
                w = pick[0:n, t, 2, :].rearrange("p (h k) -> p h k", h=PH)
                d = den[0:n, t, :]
                link(nc.vector.reduce_sum(d, w, axis=AX))
                link(nc.vector.reciprocal(d, d))
                nc.vector.tensor_tensor(w, w, d.unsqueeze(2).to_broadcast([n, PH, TOPK]), ALU.mult).then_inc(s_w, 1)
                dve.wait_ge(s_t, t + 1)
                src = ps[:, t, 0:3 * P].rearrange("p (w n) -> p w n", w=3)[:, :, 0:n]
                nc.vector.tensor_copy(selT[:, :, a:b], src).then_inc(s_c, 1)

        @block.tensor
        def _(pe):
            for t, (a, b) in enumerate(TILES):
                n = b - a
                pe.wait_ge(s_w, t + 1)
                for w in range(3):
                    last = nc.tensor.transpose(ps[:, t, w * P:w * P + n], pick[0:n, t, w, :], step.ident[0:n, 0:n])
                last.then_inc(s_t, 1)

    GT = 4
    NG = T // GT
    with ExitStack() as c1, nc.Block("peer_gate_matrix" + L, no_gpsimd_drain=True) as block:
        rows = step.sb("one_hot_weighted" + L, [P, 2, GT, P], ctx=c1)
        cols = step.sb("one_hot" + L, [P, 2, GT, P], ctx=c1)
        s_r = step.sem("one_hot_rows_ready" + L)
        dist = step.sb("distances" + L, [P, 2, GT, P], ctx=c1)
        s_d = step.sem("distances_ready" + L)
        s_ab = step.sem("absolute_distances_ready" + L)
        s_c = step.sem("one_hot_columns_ready" + L)
        s_g = step.sem("gate_product_ready" + L)
        s_gm = step.sem("gate_applied" + L)

        @block.gpsimd
        def _(pool):
            def distances(i, b, first):
                if not first:
                    pool.wait_ge(s_c, 2 * i + b - 1)
                shape = [P, GT, P]
                sel = selT[:, 1, bass.ds((2 * i + b) * GT, GT)]
                nc.gpsimd.tensor_tensor(dist[:, b], step.iota.unsqueeze(1).to_broadcast(shape),
                                        sel.unsqueeze(2).to_broadcast(shape), ALU.subtract).then_inc(s_d, 1)
            for b in range(2):
                distances(0, b, True)
            with pool.Fori(1, NG // 2) as i:
                for b in range(2):
                    distances(i, b, False)
            pool.wait_ge(s_d, NG)

        @block.scalar
        def _(act):
            def columns(i, b, first):
                act.wait_ge(s_d, 2 * i + b + 1)
                nc.scalar.activation(dist[:, b], dist[:, b], ACT.Abs).then_inc(s_ab, 1)
                if not first:
                    act.wait_ge(s_g, 2 * i + b - 1)
                act.wait_ge(s_ab, 2 * i + b + 1)
                nc.scalar.activation(cols[:, b], dist[:, b], ACT.Relu, scale=-1.0,
                                     bias=step.ones[:, 0:1]).then_inc(s_c, 1)
            nc.scalar.preload_act_table(ACT.Relu)
            for b in range(2):
                columns(0, b, True)
            with act.Fori(1, NG // 2) as i:
                for b in range(2):
                    columns(i, b, False)

        @block.vector
        def _(dve):
            def weighted_rows(i, b, first):
                if not first:
                    dve.wait_ge(s_g, 2 * i + b - 1)
                for k in range(GT):
                    tok = (2 * i + b) * GT + k
                    last = nc.vector.tensor_scalar(rows[:, b, k, :], step.iota, selT[:, 0, bass.ds(tok, 1)],
                                                   selT[:, 2, bass.ds(tok, 1)], ALU.is_equal, ALU.mult)
                last.then_inc(s_r, 1)

            def apply(i, b):
                dve.wait_ge(s_g, 2 * i + b + 1)
                h = big[:, :, bass.ds((2 * i + b) * GT, GT)]
                nc.vector.tensor_tensor(h, ps[:, b, :].rearrange("p (k n) -> p n k", k=GT), h,
                                        ALU.mult).then_inc(s_gm, 1)
            for b in range(2):
                weighted_rows(0, b, True)
            with dve.Fori(1, NG // 2) as i:
                for b in range(2):
                    apply(i - 1, b)
                    weighted_rows(i, b, False)
            for b in range(2):
                apply(NG // 2 - 1, b)

        @block.tensor
        def _(pe):
            def products(i, b, first):
                pe.wait_ge(s_r, 2 * i + b + 1)
                pe.wait_ge(s_c, 2 * i + b + 1)
                if not first:
                    pe.wait_ge(s_gm, 2 * i + b - 1)
                for k in range(GT):
                    last = nc.tensor.matmul(ps[:, b, k * P:(k + 1) * P], rows[:, b, k, :], cols[:, b, k, :],
                                            start=True, stop=True)
                last.then_inc(s_g, 1)
            for b in range(2):
                products(0, b, True)
            with pe.Fori(1, NG // 2) as i:
                for b in range(2):
                    products(i, b, False)


def peer_down(step, layer, big):
    nc, io, ps = step.nc, step.io, step.ps
    L = f"_{layer}"
    base = step.used
    vb = step.slabs[base][1]
    with ExitStack() as c1, nc.Block("peer_down" + L, no_gpsimd_drain=True) as block:
        HALF = D // 2
        hi, lo = (part[:].rearrange("p c t -> p (c t)")[:, 0:4 * HALF].rearrange("p (b f) -> p b f", b=4)
                  for part in step.operand)
        wh = step.sb("w_hi" + L, [P, 2, T], F32R, ctx=c1)
        wl = step.sb("w_lo" + L, [P, 2, T], F32R, ctx=c1)
        s_hi = step.sem("v_hi_ready" + L)
        s_wh = step.sem("w_hi_ready" + L)
        s_wl = step.sem("w_lo_ready" + L)
        s_y = step.sem("down_half_product_ready" + L)

        @block.sync
        def _(sp):
            with sp.Fori(1, NKEYS // SLOTS) as i:
                for s in range(SLOTS):
                    sp.wait_ge(step.v_split, 2 * (vb + SLOTS * i + s + 1 - SLOTS))
                    sp.dma_start(step.ring[:, s, :], io["v"][layer * P + SLOTS * i + s]).then_inc(step.slab_ready[s], 16)
            step.loaded = base + NKEYS
            step.load_until(sp, base + NKEYS + SLOTS)

        @block.scalar
        def _(act):
            def high(i, s, first):
                n = SLOTS * i + s
                act.wait_ge(step.slab_ready[s], 16 * (base // SLOTS + 1) + 16 * i)
                for g in range(2):
                    if not (first and s < 2):
                        act.wait_ge(s_y, 2 * n + g - 3)
                    if g:
                        nc.scalar.activation(wh[:, s % 2, :], big[:, n, :], ACT.Copy).then_inc(s_wh, 1)
                    nc.scalar.activation(hi[:, (2 * s + g) % 4, :], step.ring[:, s, g * HALF:(g + 1) * HALF],
                                         ACT.Copy).then_inc(s_hi, 1)
            nc.scalar.preload_act_table(ACT.Copy)
            for s in range(SLOTS):
                high(0, s, True)
            with act.Fori(1, NKEYS // SLOTS) as i:
                for s in range(SLOTS):
                    high(i, s, False)

        @block.vector
        def _(dve):
            with dve.Fori(0, NKEYS // SLOTS) as i:
                for s in range(SLOTS):
                    n = SLOTS * i + s
                    for g in range(2):
                        if g:
                            dve.wait_ge(s_wh, n + 1)
                            nc.vector.tensor_tensor(wl[:, s % 2, :], big[:, n, :], wh[:, s % 2, :].bitcast(F32),
                                                    ALU.subtract).then_inc(s_wl, 1)
                        dve.wait_ge(s_hi, 2 * n + g + 1)
                        buf = (2 * s + g) % 4
                        nc.vector.tensor_tensor(lo[:, buf, :], step.ring[:, s, g * HALF:(g + 1) * HALF],
                                                hi[:, buf, :].bitcast(F32), ALU.subtract).then_inc(step.v_split, 1)

        @block.tensor
        def _(pe):
            def down(i, s, first, final):
                n = SLOTS * i + s
                b = s % 2
                pe.wait_ge(s_wl, n + 1)
                for g in range(2):
                    pe.wait_ge(step.v_split, 2 * (vb + n) + g + 1)
                    buf = (2 * s + g) % 4
                    for k in range(HC):
                        cs = slice(k * P, (k + 1) * P)
                        bank = ps[:, g * HC + k, 0:T]
                        nc.tensor.matmul(bank, hi[:, buf, cs], wh[:, b, :], start=first, stop=False)
                        nc.tensor.matmul(bank, hi[:, buf, cs], wl[:, b, :], start=False, stop=False)
                        last = nc.tensor.matmul(bank, lo[:, buf, cs], wh[:, b, :], start=False, stop=final)
                    last.then_inc(s_y, 1)
            for s in range(SLOTS):
                down(0, s, s == 0, False)
            with pe.Fori(1, NKEYS // SLOTS - 1) as i:
                for s in range(SLOTS):
                    down(i, s, False, False)
            for s in range(SLOTS):
                down(NKEYS // SLOTS - 1, s, False, s == SLOTS - 1)
    step.used += NKEYS

    with ExitStack() as c1, nc.Block("peer_norm" + L, no_gpsimd_drain=True) as block:
        res = step.sb("res_peer" + L, [P, DC, T], ctx=c1)

        def residual_steps(dve, j):
            return nc.vector.scalar_tensor_tensor(out=res[:, j, :], in0=step.x[:, j, :], scalar=ALPHA,
                                                  in1=ps[:, j, 0:T], op0=ALU.mult, op1=ALU.add)
        emit_norm(step, block, "peer" + L, layer * 3 + 2, res, (0, 1), residual_steps,
                  lambda pe, j, s_res: None, step.used if layer + 1 < LAYERS else None)


_PROJ_COUNTS = (20 + 16 + 8 + 8 + 8 + 16, 12 + 16 + 8 + 8 + 8 + 16)

_OUTS = {
    "y": (P, DC, T),
    "hgrn_prompt": (P, HEADS_A, P), "hgrn_sample": (P, HEADS_A * TS, P),
    "pool_prompt": (P, HEADS_A, CTX), "pool_sample": (P, HEADS_A, TS, CTX),
    "window_k_prompt": (HD, KV, P), "window_k_sample": (HD, TS, KV, P),
    "window_v_prompt": (P, KV, HD), "window_v_sample": (P, TS, KV, HD),
    "mem_k_out": (LAYERS, P, DC, NMEM), "mem_v_out": (LAYERS, P, NMEM // P, D),
}


def _constants():
    import numpy as np
    c = np.zeros((P, C_END), np.float32)
    c[:, C_ID:C_ID + P] = np.eye(P)
    c[:, C_ONE:C_ONE + P] = 1
    c[:, C_MEAN:C_MEAN + P] = 1 / D
    c[:, C_HEAD:C_HEAD + P] = 1 / P
    c[:, C_IOTA:C_IOTA + P] = np.arange(P)
    q = np.arange(P)[:, None]
    k = np.arange(P)[None, :]
    c[:, C_MASK:C_MASK + P] = np.where(k <= q, 0, LOWEST)
    k = np.arange(2 * P)[None, :]
    c[:, C_MASK + P:C_MASK + 3 * P] = np.where((k > q) & (k <= q + P), 0, LOWEST)
    c[:, C_EPS] = EPS
    scan = np.ones((P, TP), np.float32)
    scan[:, ::BLK] = 0
    inv = np.zeros((P, HEADS_A, T), np.float32)
    for g, w in enumerate(POOL_SIZES):
        inv[:, g, :TP] = 1 / np.minimum(np.arange(TP) + 1, w)
        inv[:, g, TP:] = 1 / w
    return c, scan, inv


def kernel(**inputs):
    import numpy as np
    import concourse.bacc as bacc
    from concourse.bass_utils import run_bass_kernel_spmd

    a = {k: np.asarray(v) for k, v in inputs.items()}

    def chunks(m):
        return m.reshape(m.shape[0], -1, P).transpose(2, 1, 0)

    def slabs(w):
        return w.reshape(DC, P, -1, P).transpose(2, 1, 0, 3).reshape(-1, P, D)

    const, scan, inv = _constants()
    arrays = {"const": const, "scan_mask": scan, "inv_count": inv}
    arrays["x"] = chunks(np.concatenate([a["x_prompt"][0], a["x_sample"][:, 0]]))
    arrays["mem"] = chunks(a["mem_prompt"][0])
    arrays["ln"] = np.stack([a["ln_g"], a["ln_b"]], 2).reshape(LAYERS * 3, 2, DC, P).transpose(3, 0, 1, 2)
    arrays["gamma"] = a["hgrn_gamma"].reshape(2, HEADS_A, P).transpose(2, 0, 1)
    arrays["norm_g"] = a["hgrn_norm_g"][0].reshape(HEADS_A, P).T
    arrays["pool_scale"] = a["pool_scale"][0].reshape(HEADS_A, P).T
    arrays["pool_w"] = a["pool_w"][0].transpose(1, 0, 2)
    arrays["pool_ctx"] = a["state_pool"][0].reshape(TS, CTX, HEADS_A, P).transpose(3, 2, 0, 1)
    arrays["state"] = a["state_hgrn"][0].transpose(2, 1, 0, 3).reshape(P, -1, P)
    wc = a["w_in_c"][0]
    nq = HEADS_C * HD
    dup = [wc[:, nq + i * HD:nq + (i + 1) * HD] for i in (0, 0, 1, 1, 2, 2, 3, 3)]
    w = a["w_in_a"][0]
    part = [w[:, i * 512:(i + 1) * 512] for i in (0, 1, 3, 2, 4)]
    first = (part, [wc[:, :nq]] + dup)
    outs = (a["w_out_a"][0], a["w_out_c"][0])
    cols = []
    for layer in range(LAYERS):
        cols += [*first[layer], a["mem_wkv"][layer], outs[layer], a["mem_wq"][layer], a["mem_wo"][layer],
                 a["peer_wq"][layer]]
    arrays["proj"] = slabs(np.concatenate(cols, 1))
    arrays["u"] = a["peer_u"].reshape(LAYERS, P, P, DC, P).transpose(0, 2, 4, 3, 1).reshape(-1, P, D)
    arrays["v"] = a["peer_v"].reshape(LAYERS, P, P, D).transpose(0, 2, 1, 3).reshape(-1, P, D)
    arrays["subkeys"] = a["peer_subkeys"].transpose(0, 4, 1, 2, 3).reshape(LAYERS, P, -1)
    ckm = a["cache_mem_k"].reshape(LAYERS, TS, NMEM, DC, P)
    arrays["cache_k"] = ckm.transpose(0, 1, 4, 3, 2)
    arrays["cache_v"] = a["cache_mem_v"].reshape(LAYERS, TS, 2, P, D).transpose(0, 1, 3, 2, 4)
    k = a["cache_swa_k"][0][:, 1:].transpose(3, 0, 2, 1)
    arrays["window_k"] = np.concatenate([k, k])
    v = a["cache_swa_v"][0][:, 1:].transpose(1, 0, 2, 3)
    arrays["window_v"] = np.concatenate([v, v], 3)
    s = a["attn_sinks"][0]
    order = s.reshape(KV, 4, 2).transpose(0, 2, 1).reshape(-1)
    arrays["sinks"] = np.concatenate([np.tile(s, (P, 1)), np.tile(order, TS)[:, None]], 1)
    arrays = {k: np.ascontiguousarray(v) for k, v in arrays.items()}

    nc = bacc.Bacc("TRN2", target_bir_lowering=False, num_devices=1)
    io = {k: nc.dram_tensor(f"in_{k}", v.shape, F32, kind="ExternalInput").ap() for k, v in arrays.items()}
    for k, shape in _OUTS.items():
        io[k] = nc.dram_tensor(f"out_{k}", shape, F32, kind="ExternalOutput").ap()
    io["proj_counts"] = _PROJ_COUNTS
    hybrid_step(nc, io)
    r = run_bass_kernel_spmd(nc, [{f"in_{k}": v for k, v in arrays.items()}], core_ids=[0]).results[0]
    o = {k: r[f"out_{k}"] for k in _OUTS}

    y = o["y"].transpose(2, 1, 0).reshape(T, D)
    return (
        y[None, :TP], y[TP:, None],
        o["hgrn_prompt"].transpose(1, 0, 2)[None, None],
        o["hgrn_sample"].reshape(P, HEADS_A, TS, P).transpose(2, 1, 0, 3)[None],
        o["pool_prompt"].transpose(2, 1, 0).reshape(CTX, -1)[None, None],
        o["pool_sample"].transpose(2, 3, 1, 0).reshape(TS, CTX, -1)[None],
        o["window_k_prompt"].transpose(2, 1, 0)[None, None],
        o["window_k_sample"].transpose(1, 3, 2, 0)[None],
        o["window_v_prompt"][None, None],
        o["window_v_sample"].transpose(1, 0, 2, 3)[None],
        o["mem_k_out"].transpose(0, 3, 2, 1).reshape(LAYERS, 1, NMEM, MH, MHD),
        o["mem_v_out"].transpose(0, 2, 1, 3).reshape(LAYERS, 1, NMEM, MH, MHD),
    )
```

```python
from contextlib import ExitStack

import concourse.bass as bass
from concourse import mybir

F32 = mybir.dt.float32
F32R = mybir.dt.float32r
U32 = mybir.dt.uint32
ALU = mybir.AluOpType
ACT = mybir.ActivationFunctionType
AX = mybir.AxisListType.X

P = 128
D = 1024
DC = D // P
TP = 256
TS = 8
T = TP + TS
LAYERS = 2
ALPHA = float((2 * LAYERS) ** 0.25)
EPS = 1e-5
HEADS_A = 4
BLK = 16
NBLK = TP // BLK
POOL_SIZES = (2, 4, 8, 16)
CTX = 15
KV = 2
HEADS_C = 16
HD = 64
MH = 4
MHD = 256
NMEM = 256
PH = 8
TOPK = 16
NKEYS = 128
LOWEST = -3.0e38
SLOTS = 4
HC = DC // 2
KEYS_LATER = 3

C_ID, C_ONE, C_MEAN, C_HEAD, C_IOTA = (n * P for n in range(5))
C_MASK = 5 * P
C_EPS = C_MASK + 3 * P
C_BLK = C_EPS + 1
C_END = C_BLK + P // BLK


def hybrid_step(nc, io):
    with ExitStack() as top:
        step = Step(nc, io, top)
        step.load_constants()
        for layer in range(LAYERS):
            with ExitStack() as attn:
                step.open_attention(layer, attn)
                if layer == 0:
                    hgrn_pool_mixer(step, layer)
                else:
                    window_mixer(step, layer)
                step.open_caches(layer, attn)
                project_and_norm(step, layer, 0)
                cross_attention(step, layer)
                project_and_norm(step, layer, 1)
            peer(step, layer)
            step.end_layer()
        step.store_result()


class Step:

    def __init__(self, nc, io, top):
        self.nc, self.io = nc, io
        self.sb = lambda name, shape, dt=F32, ctx=top: ctx.enter_context(nc.sbuf_tensor(name, shape, dt))
        self.ring, self.ring_lo = self.pair("slab_ring", [P, SLOTS, D], "slab_ring_lo", [P, SLOTS, DC, P])
        self.x = self.sb("x_T", [P, DC, T])
        self.const = self.sb("constants", [P, C_END])
        self.ln = self.sb("ln_scale_shift", [P, LAYERS * 3, 2, DC])
        self.own, operand_hi = self.pair("sample_own_rows", [P, DC * T], "operand_hi", [P, DC, T])
        self.mixed, operand_lo = self.pair("mixed_T", [P, DC, T], "operand_lo", [P, DC, T])
        self.operand = (operand_hi, operand_lo)
        self.squares, self.slab_hi = self.pair("squares", [P, DC, T], "slab_hi", [P, 2, DC, P])
        self.ps = top.enter_context(nc.psum_tensor("banks", [P, 8, 512], F32))
        self.slab_ready = [nc.alloc_semaphore(f"slab_ready{s}") for s in range(SLOTS)]
        self.product_done = nc.alloc_semaphore("projection_product_done")
        self.slab_hi_ready = nc.alloc_semaphore("projection_slab_hi_ready")
        self.slab_lo_ready = [nc.alloc_semaphore(f"projection_slab_lo{g}_ready") for g in range(2)]
        self.half_product_done = nc.alloc_semaphore("projection_half_product_done")
        self.split_number = {}
        self.u_split = nc.alloc_semaphore("u_half_slab_split")
        self.v_split = nc.alloc_semaphore("v_half_slab_split")
        self.stored = nc.alloc_semaphore("outputs_stored")
        self.constants_ready = nc.alloc_semaphore("constants_ready")
        self.vector_done = nc.alloc_semaphore("vector_instruction_done")
        self.scalar_done = nc.alloc_semaphore("scalar_instruction_done")
        self.gpsimd_done = nc.alloc_semaphore("gpsimd_instruction_done")
        self.count = {"vector": 0, "scalar": 0, "gpsimd": 0}
        self.stores = 0
        self.layer_sems = []
        self.slabs = []
        kinds = {"projection": 0, "u": 0, "v": 0}
        for layer in range(LAYERS):
            n = io["proj_counts"][layer]
            run = [("projection", io["proj"], sum(io["proj_counts"][:layer]) + k) for k in range(n)]
            run += [("u", io["u"], layer * P + k) for k in range(P)]
            run += [("v", io["v"], layer * P + k) for k in range(P)]
            for kind, src, k in run:
                self.slabs.append((kind, kinds[kind], src, k))
                kinds[kind] += 1
        self.used = 0
        self.loaded = 0

    def pair(self, name, shape, name_r, shape_r):
        address = (self.nc.sbuf_base + 31) // 32 * 32
        one = self.sb(name, shape)
        return one, self.nc.alloc_sbuf_tensor_at(name_r, shape_r, F32R, offset=address)

    ident = property(lambda s: s.const[:, C_ID:C_ID + P])
    ones = property(lambda s: s.const[:, C_ONE:C_ONE + P])
    mean_d = property(lambda s: s.const[:, C_MEAN:C_MEAN + P])
    mean_head = property(lambda s: s.const[:, C_HEAD:C_HEAD + P])
    iota = property(lambda s: s.const[:, C_IOTA:C_IOTA + P])
    masks = property(lambda s: s.const[:, C_MASK:C_MASK + 3 * P])
    eps = property(lambda s: s.const[:, C_EPS:C_EPS + 1])
    block_rows = property(lambda s: s.const[:, C_BLK:C_BLK + P // BLK])

    def sem(self, name):
        s = self.nc.alloc_semaphore(name)
        self.layer_sems.append(s)
        return s

    def end_layer(self):
        self.nc.clear_and_free_semaphores(self.layer_sems)
        self.layer_sems = []
        self.nc.all_engine_barrier()

    def link(self, engine, name, instruction, wait=True):
        sem = {"vector": self.vector_done, "scalar": self.scalar_done, "gpsimd": self.gpsimd_done}[name]
        self.count[name] += 1
        instruction.then_inc(sem, 1)
        if wait:
            engine.wait_ge(sem, self.count[name])

    def store(self, engine, dst, src):
        self.stores += 1
        engine.dma_start(dst, src).then_inc(self.stored, 16)

    def slot_free(self, sp, n):
        if n < SLOTS:
            return
        kind, k = self.slabs[n - SLOTS][:2]
        if kind == "projection":
            sp.wait_ge(self.product_done, k + 1)
        else:
            sp.wait_ge(self.u_split if kind == "u" else self.v_split, 2 * (k + 1))

    def load_until(self, sp, end):
        for n in range(self.loaded, min(end, len(self.slabs))):
            _, _, src, k = self.slabs[n]
            self.slot_free(sp, n)
            sp.dma_start(self.ring[:, n % SLOTS, :], src[k]).then_inc(self.slab_ready[n % SLOTS], 16)
        self.loaded = max(self.loaded, min(end, len(self.slabs)))

    def wait_slab(self, engine, n):
        engine.wait_ge(self.slab_ready[n % SLOTS], 16 * (n // SLOTS + 1))

    def slab(self, n):
        return self.ring[:, n % SLOTS, :].rearrange("p (c m) -> p c m", c=DC)

    def product_count(self, n):
        assert self.slabs[n][0] == "projection"
        return self.slabs[n][1] + 1

    def open_attention(self, layer, ctx):
        self.q = self.sb(f"query_T{layer}", [P, DC, T], ctx=ctx)
        self.mem_k = self.sb(f"mem_k_T{layer}", [P, DC, NMEM], ctx=ctx)
        self.mem_v = self.sb(f"mem_v{layer}", [P, NMEM // P, D], ctx=ctx)

    def open_caches(self, layer, ctx):
        self.cache = [self.sb(f"cache_k_T{layer}", [P, TS, DC, NMEM], ctx=ctx),
                      self.sb(f"cache_v{layer}", [P, TS, NMEM // P, D], ctx=ctx)]
        self.cache_ready = [self.sem(f"cache_{w}_ready{layer}") for w in "kv"]

    def load_cache(self, sp, layer, which, b):
        name = ("cache_k", "cache_v")[which]
        sp.dma_start(self.cache[which][:, b], self.io[name][layer, b]).then_inc(self.cache_ready[which], 16)

    def load_constants(self):
        nc, io = self.nc, self.io
        x_ready = [self.sem(f"x_half_loaded{g}") for g in range(2)]
        with nc.Block("constants", no_gpsimd_drain=True) as block:
            @block.sync
            def _(sp):
                for g in range(2):
                    cs = slice(g * HC, (g + 1) * HC)
                    sp.dma_start(self.x[:, cs], io["x"][:, cs]).then_inc(x_ready[g], 16)
                self.load_until(sp, 2)
                sp.dma_start(self.const[:], io["const"]).then_inc(self.constants_ready, 16)
                sp.dma_start(self.ln[:], io["ln"]).then_inc(self.constants_ready, 16)
                self.load_until(sp, SLOTS)
                sp.wait_ge(self.constants_ready, 32)

            number_slabs(self, 0, 1)
            xh, xl = self.operand
            x_split = self.sem("x_hi_ready")
            halves = [slice(g * HC, (g + 1) * HC) for g in range(2)]

            @block.scalar
            def _(act):
                for g, cs in enumerate(halves):
                    act.wait_ge(x_ready[g], 16)
                    nc.scalar.activation(xh[:, cs], self.x[:, cs], ACT.Copy).then_inc(x_split, 1)
                split_high(self, act, 0)

            @block.vector
            def _(dve):
                for g, cs in enumerate(halves):
                    dve.wait_ge(x_split, g + 1)
                    nc.vector.tensor_tensor(xl[:, cs], self.x[:, cs], xh[:, cs].bitcast(F32), ALU.subtract)

            @block.gpsimd
            def _(pool):
                split_low(self, pool, 0, (0, 1))
                slabs_split(self, pool, 0, (0, 1))

    def store_result(self):
        nc, io = self.nc, self.io
        with nc.Block("result", no_gpsimd_drain=True) as block:
            @block.sync
            def _(sp):
                self.store(sp, io["y"], self.x[:])
                sp.wait_ge(self.stored, 16 * self.stores)


def number_slabs(step, first, count):
    for n in range(first, first + count):
        step.split_number.setdefault(n, len(step.split_number))


def split_high(step, act, n):
    nc, k = step.nc, step.split_number[n]
    step.wait_slab(act, n)
    for g in range(2):
        if n - 2 in step.split_number:
            if g == 0:
                act.wait_ge(step.half_product_done, step.split_number[n - 2] + 1)
            else:
                act.wait_ge(step.product_done, step.product_count(n - 2))
        cs = slice(g * HC, (g + 1) * HC)
        nc.scalar.activation(step.slab_hi[:, (k + 1) % 2, cs], step.slab(n)[:, cs], ACT.Copy).then_inc(step.slab_hi_ready, 1)


def split_low(step, engine, n, halves):
    nc, k = step.nc, step.split_number[n]
    for g in halves:
        cs = slice(g * HC, (g + 1) * HC)
        engine.wait_ge(step.slab_hi_ready, 2 * k + g + 1)
        (nc.gpsimd if engine is nc.gpsimd else nc.vector).tensor_tensor(
            step.ring_lo[:, n % SLOTS, cs], step.slab(n)[:, cs], step.slab_hi[:, (k + 1) % 2, cs].bitcast(F32),
            ALU.subtract).then_inc(step.slab_lo_ready[g], 1)


def slabs_split(step, pool, n, halves=(0,)):
    for g in halves:
        pool.wait_ge(step.slab_lo_ready[g], step.split_number[n] + 1)


def product(step, pe, n, bank, s_part=None):
    nc, k = step.nc, step.split_number[n]
    xh, xl = step.operand
    wh, wl = step.slab_hi[:, (k + 1) % 2], step.ring_lo[:, n % SLOTS]
    for c in range(DC):
        if c % HC == 0:
            pe.wait_ge(step.slab_lo_ready[c // HC], k + 1)
        if s_part is not None:
            pe.wait_ge(s_part, c + 1)
        nc.tensor.matmul(step.ps[:, bank, 0:T], wh[:, c, :], xh[:, c, :], start=(c == 0), stop=False)
        nc.tensor.matmul(step.ps[:, bank, 0:T], wh[:, c, :], xl[:, c, :], start=False, stop=False)
        last = nc.tensor.matmul(step.ps[:, bank, 0:T], wl[:, c, :], xh[:, c, :], start=False, stop=(c == DC - 1))
        if c == HC - 1:
            last.then_inc(step.half_product_done, 1)
    last.then_inc(step.product_done, 1)


def emit_norm(step, block, tag, sub, res, base_bank, residual_steps, tensor_steps, next_slab, early=None, partial=None):
    nc = step.nc
    squares = step.squares
    early = early or {}
    mean_bank, var_bank = base_bank
    s_res = step.sem(f"residual_chunk_ready_{tag}")
    s_mean = step.sem(f"mean_ready_{tag}")
    s_cent = step.sem(f"centred_chunk_ready_{tag}")
    s_sq = step.sem(f"squared_chunk_ready_{tag}")
    s_var = step.sem(f"variance_ready_{tag}")
    s_std = step.sem(f"deviation_ready_{tag}")
    s_rstd = step.sem(f"reciprocal_ready_{tag}")
    s_norm = step.sem(f"normed_chunk_ready_{tag}")
    s_x = step.sem(f"x_chunk_ready_{tag}")
    s_xh = step.sem(f"x_chunk_hi_ready_{tag}")
    s_xl = step.sem(f"x_chunk_lo_ready_{tag}")
    xh, xl = step.operand
    if next_slab is not None:
        number_slabs(step, next_slab, 1)
    rstd = squares[:, 0, :]
    mean = step.ps[:, mean_bank, 0:T]
    var = step.ps[:, var_bank, 0:T]

    @block.tensor
    def _(pe):
        for j in range(DC):
            tensor_steps(pe, j, s_res)
            if j >= 1 and partial is None:
                pe.wait_ge(s_res, j)
                nc.tensor.matmul(mean, step.mean_d, res[:, j - 1, :], start=(j == 1), stop=False)
        if partial is not None:
            pe.wait_ge(partial[1], DC - 2)
            nc.tensor.matmul(mean, step.mean_d, partial[0][:], start=True, stop=False)
        pe.wait_ge(s_res, DC)
        nc.tensor.matmul(mean, step.mean_d, res[:, DC - 1, :], start=False, stop=True).then_inc(s_mean, 1)
        for j in range(DC):
            pe.wait_ge(s_sq, j + 1)
            last = nc.tensor.matmul(var, step.mean_d, squares[:, j, :], start=(j == 0), stop=(j == DC - 1))
        last.then_inc(s_var, 1)

    @block.vector
    def _(dve):
        if "vector" in early:
            early["vector"](dve)
        for j in range(DC):
            residual_steps(dve, j).then_inc(s_res, 1)
        dve.wait_ge(s_mean, 1)
        dve.wait_ge(s_res, DC)
        for j in range(DC):
            nc.vector.tensor_tensor(res[:, j, :], res[:, j, :], mean, ALU.subtract).then_inc(s_cent, 1)
        dve.wait_ge(s_std, 1)
        nc.vector.reciprocal(rstd, rstd).then_inc(s_rstd, 1)
        dve.wait_ge(s_rstd, 1)
        for j in range(DC + 2):
            if j < DC:
                nc.vector.tensor_tensor(res[:, j, :], res[:, j, :], rstd, ALU.mult).then_inc(s_norm, 1)
            if j >= 2 and next_slab is not None:
                c = j - 2
                dve.wait_ge(s_x, c + 1)
                nc.vector.tensor_copy(xh[:, c, :], step.x[:, c, :]).then_inc(s_xh, 1)
                if c % 2:
                    dve.wait_ge(s_xh, c + 1)
                    nc.vector.tensor_tensor(xl[:, c, :], step.x[:, c, :], xh[:, c, :].bitcast(F32), ALU.subtract)

    @block.gpsimd
    def _(pool):
        if "gpsimd" in early:
            early["gpsimd"](pool, s_res)
        if next_slab is None:
            return
        split_low(step, pool, next_slab, (0, 1))
        for j in range(0, DC, 2):
            pool.wait_ge(s_xh, j + 1)
            nc.gpsimd.tensor_tensor(xl[:, j, :], step.x[:, j, :], xh[:, j, :].bitcast(F32),
                                    ALU.subtract).then_inc(s_xl, 1)
        pool.wait_ge(s_xl, DC // 2)

    @block.scalar
    def _(act):
        if "scalar" in early:
            early["scalar"](act)
        for j in range(DC):
            act.wait_ge(s_cent, j + 1)
            nc.scalar.activation(squares[:, j, :], res[:, j, :], ACT.Square).then_inc(s_sq, 1)
        act.wait_ge(s_var, 1)
        nc.scalar.activation(rstd, var, ACT.Sqrt, bias=step.eps).then_inc(s_std, 1)
        if next_slab is not None:
            split_high(step, act, next_slab)
        for j in range(DC):
            act.wait_ge(s_norm, j + 1)
            nc.scalar.activation(step.x[:, j, :], res[:, j, :], ACT.Identity,
                                 scale=step.ln[:, sub, 0, j:j + 1], bias=step.ln[:, sub, 1, j:j + 1]).then_inc(s_x, 1)


def project_and_norm(step, layer, which):
    nc = step.nc
    base = step.used
    tag = f"{'mixer' if which == 0 else 'cross'}_{layer}"
    number_slabs(step, base, DC)
    hi, lo = step.operand
    res = step.q
    with ExitStack() as ctx, nc.Block(f"out_{tag}", no_gpsimd_drain=True) as block:
        total = step.sb(f"residual_sum_{tag}", [P, T], ctx=ctx)
        s_total = step.sem(f"residual_chunk_added_{tag}")
        s_mh = step.sem(f"mixed_chunk_hi_ready_{tag}")
        s_part = step.sem(f"mixed_chunk_split_{tag}")

        @block.sync
        def _(sp):
            if which == 0:
                sp.wait_ge(step.stored, 16 * step.stores)
            for j in range(DC):
                step.load_until(sp, base + j + 1 + SLOTS)
                if which == 0 and j >= KEYS_LATER:
                    step.load_cache(sp, layer, 0, j - KEYS_LATER)

        def scalar_early(act):
            split_high(step, act, base)
            for c in range(DC):
                nc.scalar.activation(hi[:, c, :], step.mixed[:, c, :], ACT.Copy).then_inc(s_mh, 1)
            for j in range(1, DC):
                split_high(step, act, base + j)

        def vector_early(dve):
            for c in range(DC):
                dve.wait_ge(s_mh, c + 1)
                nc.vector.tensor_tensor(lo[:, c, :], step.mixed[:, c, :], hi[:, c, :].bitcast(F32),
                                        ALU.subtract).then_inc(s_part, 1)
                if c == HC - 1:
                    split_low(step, dve, base, (1,))
            split_low(step, dve, base + 1, (1,))

        def gpsimd_early(pool, s_res):
            for j in range(DC + 1):
                if j < DC:
                    split_low(step, pool, base + j, (0,))
                c = j - 2
                if c >= 1:
                    pool.wait_ge(s_res, c + 1)
                    if c >= 2:
                        pool.wait_ge(s_total, c - 1)
                    nc.gpsimd.tensor_tensor(total[:], total[:] if c >= 2 else res[:, 0, :], res[:, c, :],
                                            ALU.add).then_inc(s_total, 1)

        def tensor_steps(pe, j, s_res):
            if j >= 3:
                pe.wait_ge(s_res, j - 2)
            product(step, pe, base + j, j % 3, s_part if j == 0 else None)

        def residual_steps(dve, j):
            if j + 2 < DC:
                split_low(step, dve, base + j + 2, (1,))
            dve.wait_ge(step.product_done, step.product_count(base + j))
            return nc.vector.scalar_tensor_tensor(out=res[:, j, :], in0=step.x[:, j, :], scalar=ALPHA,
                                                  in1=step.ps[:, j % 3, 0:T], op0=ALU.mult, op1=ALU.add)

        emit_norm(step, block, tag, layer * 3 + which, res, (3, 4), residual_steps, tensor_steps, base + DC,
                  {"scalar": scalar_early, "vector": vector_early, "gpsimd": gpsimd_early}, (total, s_total))
    step.used += DC


def memory_product(step, pe, n, k, mem, bank, s_read):
    nc = step.nc
    if k >= 2:
        pe.wait_ge(s_read, k - 1)
    step.wait_slab(pe, n)
    w = step.slab(n)
    if k < DC:
        for c in range(DC):
            last = nc.tensor.matmul(step.ps[:, bank, 0:NMEM], w[:, c, :], mem[:, c, :],
                                    start=(c == 0), stop=(c == DC - 1))
    else:
        for m in range(NMEM // P):
            for c in range(DC):
                last = nc.tensor.matmul(step.ps[:, bank, m * P:(m + 1) * P], mem[:, c, m * P:(m + 1) * P],
                                        w[:, c, :], start=(c == 0), stop=(c == DC - 1))
    last.then_inc(step.product_done, 1)


def memory_copy(step, act, n, k, bank, s_read):
    nc = step.nc
    act.wait_ge(step.product_done, step.product_count(n))
    if k < DC:
        nc.scalar.activation(step.mem_k[:, k, :], step.ps[:, bank, 0:NMEM], ACT.Copy).then_inc(s_read, 1)
    else:
        out = step.mem_v[:, :, (k - DC) * P:(k - DC + 1) * P]
        nc.scalar.activation(out, step.ps[:, bank, 0:NMEM].rearrange("p (m f) -> p m f", m=NMEM // P),
                             ACT.Copy).then_inc(s_read, 1)


def hgrn_pool_mixer(step, layer):
    nc, io, ps = step.nc, step.io, step.ps
    H4 = HEADS_A
    NP, NS = H4 * TP, H4 * TS
    base = step.used
    with ExitStack() as ctx:
        def sb(name, shape, c=ctx):
            return step.sb(name, shape, ctx=c)

        qs = sb("silu_q", [P, NP + NS])
        fg = sb("forget_gate", [P, NP + NS])
        kk = sb("key_gate", [P, NP + NS])
        lf = sb("log_forget", [P, NP + NS])
        vi = sb("value_i", [P, NP + NS])
        sg = sb("silu_g", [P, NP + NS])
        out_h = sb("hgrn_out", [P, NP + NS])
        u_ext = sb("pool_prompt_ext", [P, H4, CTX + TP])
        s_ext = sb("pool_sample_ext", [P, H4, TS, CTX + 1])
        gam = sb("gamma_T", [P, 2, H4])
        lbt = sb("lower_bound", [P, 6, H4])
        ng = sb("norm_gain", [P, H4])
        psc = sb("pool_scale_T", [P, H4])
        pw = sb("pool_weights", [P, H4, P])
        inv = sb("window_inverse", [P, H4, T])
        smask = sb("scan_mask", [P, TP])
        s0 = sb("sample_state", [P, NS, P])
        mem = sb("memory_T", [P, DC, NMEM])
        params = step.sem("mixer_params_ready")
        late = step.sem("mixer_late_params_ready")
        state_ready = step.sem("sample_state_loaded")
        lb, oml = lbt[:, 4, :], lbt[:, 5, :]

        with ExitStack() as c1, nc.Block("mixer_in", no_gpsimd_drain=True) as block:
            sig = sb("sigmoids", [P, 2, T], c1)
            s_sig = step.sem("sigmoid_ready")
            s_use = step.sem("sigmoid_used")
            s_cp = step.sem("chunk_copied")
            order = ["q"] * 4 + ["f"] * 4 + ["g"] * 4 + ["i"] * 4 + ["u"] * 4
            N_SIG = 12
            number_slabs(step, base, 20)

            @block.sync
            def _(sp):
                for dst, name in ((gam, "gamma"), (ng, "norm_g"), (psc, "pool_scale")):
                    sp.dma_start(dst[:], io[name]).then_inc(params, 16)
                step.load_until(sp, base + 20 + SLOTS)

            @block.gpsimd
            def _(pool):
                late_loads = ((pw[:], "pool_w"), (inv[:], "inv_count"), (smask[:], "scan_mask"),
                              (s_ext[:, :, :, 0:CTX], "pool_ctx"), (mem[:], "mem"))
                for j in range(1, 20):
                    split_low(step, pool, base + j, (0,))
                    if j <= len(late_loads):
                        dst, name = late_loads[j - 1]
                        pool.dma_start(dst, io[name]).then_inc(late, 16)
                step.link(pool, "gpsimd", nc.gpsimd.memset(u_ext[:, :, 0:CTX], 0.0))
                slabs_split(step, pool, base + 19)

            @block.tensor
            def _(pe):
                for j in range(20):
                    if 4 <= j < N_SIG + 4:
                        pe.wait_ge(s_use, j - 3)
                    elif j >= N_SIG + 4:
                        pe.wait_ge(s_cp, j - 3 - N_SIG)
                    product(step, pe, base + j, j % 4)

            @block.scalar
            def _(act):
                act.wait_ge(params, 48)
                act.wait_ge(step.vector_done, step.count["vector"] + 2)
                nc.scalar.activation(lbt[:, 1:3, :], lbt[:, 1:3, :], ACT.Exp).then_inc(s_sig, 1)
                split_high(step, act, base + 1)
                for j, what in enumerate(order):
                    if j + 2 < 20:
                        split_high(step, act, base + j + 2)
                    act.wait_ge(step.product_done, step.product_count(base + j))
                    bank, h = ps[:, j % 4, :], j % 4
                    if j < N_SIG:
                        if j >= 2:
                            act.wait_ge(s_use, j - 1)
                        nc.scalar.activation(sig[:, j % 2, :], bank[:, 0:T], ACT.Sigmoid).then_inc(s_sig, 1)
                    elif what == "i":
                        nc.scalar.activation(vi[:, h * TP:(h + 1) * TP], bank[:, 0:TP], ACT.Copy)
                        nc.scalar.activation(vi[:, NP + h * TS:NP + (h + 1) * TS], bank[:, TP:T],
                                             ACT.Copy).then_inc(s_cp, 1)
                    else:
                        nc.scalar.activation(u_ext[:, h, CTX:CTX + TP], bank[:, 0:TP], ACT.Copy)
                        nc.scalar.activation(s_ext[:, h, :, CTX], bank[:, TP:T], ACT.Copy).then_inc(s_cp, 1)

            @block.vector
            def _(dve):
                link = lambda ins, wait=True: step.link(dve, "vector", ins, wait)
                dve.wait_ge(params, 48)
                link(nc.vector.tensor_tensor(lbt[:, 0, :], gam[:, 0, :], gam[:, 1, :], ALU.max))
                link(nc.vector.tensor_tensor(lbt[:, 1:3, :], gam[:], lbt[:, 0:1, :].to_broadcast([P, 2, H4]),
                                             ALU.subtract))
                dve.wait_ge(s_sig, 1)
                link(nc.vector.tensor_tensor(lbt[:, 3, :], lbt[:, 1, :], lbt[:, 2, :], ALU.add))
                link(nc.vector.reciprocal(lbt[:, 3, :], lbt[:, 3, :]))
                link(nc.vector.tensor_tensor(lb, lbt[:, 1, :], lbt[:, 3, :], ALU.mult))
                link(nc.vector.tensor_scalar(oml, lb, -1.0, 1.0, ALU.mult, ALU.add))
                split_low(step, dve, base + 1, (1,))
                for j, what in enumerate(order):
                    if j + 2 < 20:
                        split_low(step, dve, base + j + 2, (1,))
                    if j >= N_SIG:
                        continue
                    dve.wait_ge(s_sig, j + 2)
                    h, sj = j % 4, sig[:, j % 2, :]
                    for lo, hi, a, b in ((0, TP, h * TP, (h + 1) * TP), (TP, T, NP + h * TS, NP + (h + 1) * TS)):
                        if what == "f":
                            last = nc.vector.tensor_scalar(fg[:, a:b], sj[:, lo:hi], oml[:, h:h + 1], lb[:, h:h + 1],
                                                           ALU.mult, ALU.add)
                        else:
                            dst = qs if what == "q" else sg
                            last = nc.vector.tensor_tensor(dst[:, a:b], sj[:, lo:hi], ps[:, j % 4, lo:hi], ALU.mult)
                    last.then_inc(s_use, 1)
        step.used += 20

        base = step.used
        with ExitStack() as ctx2:
            cum = sb("cumulative_log", [P, NP], ctx2)
            ecum = sb("exp_cumulative", [P, NP], ctx2)
            qe = sb("q_decayed", [P, NP], ctx2)
            kd = sb("k_to_block_end", [P, NP], ctx2)
            with ExitStack() as c1, nc.Block("mixer_lags", no_gpsimd_drain=True) as block:
                dif = sb("lag_decay", [P, 2, NP], c1)
                qk = sb("lag_qk", [P, 2, NP], c1)
                pr = sb("lag_product", [P, 2, NP], c1)
                term = sb("lag_term", [P, 2, NP], c1)
                s_ln = step.sem("log_ready")
                s_b = step.sem("cumulative_ready")
                s_eb = step.sem("exp_cumulative_ready")
                s_kd = step.sem("block_end_decay_ready")
                s_ekd = step.sem("block_end_exp_ready")
                s_dif = step.sem("lag_difference_ready")
                s_edif = step.sem("lag_exp_ready")
                s_qk = step.sem("lag_qk_ready")
                s_pr = step.sem("lag_product_ready")
                s_att = step.sem("lag_attention_ready")
                s_term = step.sem("lag_term_ready")
                s_sum = step.sem("lag_term_added")
                s_mem = step.sem("memory_chunk_copied")
                blocks = lambda ap: ap.rearrange("p (n t) -> p n t", t=BLK)
                prompt = lambda t: blocks(t[:, 0:NP])
                LAG = [BLK - j for j in range(BLK)]
                HALF = NP // BLK // 2
                packed = lambda t, j: t[:, j % 2, 0:2 * HALF * LAG[j]].rearrange("p (n t) -> p n t", t=LAG[j])

                @block.sync
                def _(sp):
                    step.load_until(sp, base + 16 + SLOTS)

                @block.tensor
                def _(pe):
                    pe.wait_ge(late, 80)
                    for j in range(BLK):
                        memory_product(step, pe, base + j, j, mem, 4 + j % 2, s_mem)
                        pe.wait_ge(s_pr, j + 1)
                        if j >= 2:
                            pe.wait_ge(s_term, j - 1)
                        for half in range(2):
                            w = HALF * LAG[j]
                            last = nc.tensor.matmul(ps[:, 2 * (j % 2) + half, 0:w], step.ones,
                                                    pr[:, j % 2, half * w:(half + 1) * w], start=True, stop=True)
                        last.then_inc(s_att, 1)

                @block.scalar
                def _(act):
                    nc.scalar.activation(lf[:], fg[:], ACT.Ln).then_inc(s_ln, 1)
                    act.wait_ge(s_b, 1)
                    nc.scalar.activation(ecum[:], cum[:], ACT.Exp).then_inc(s_eb, 1)
                    act.wait_ge(s_kd, 1)
                    nc.scalar.activation(kd[:], kd[:], ACT.Exp).then_inc(s_ekd, 1)
                    for j in range(BLK):
                        if j:
                            act.wait_ge(s_dif, j)
                            nc.scalar.activation(packed(dif, j), packed(dif, j), ACT.Exp).then_inc(s_edif, 1)
                        memory_copy(step, act, base + j, j, 4 + j % 2, s_mem)

                @block.gpsimd
                def _(pool):
                    def make_qk(j):
                        if j >= 2:
                            pool.wait_ge(s_pr, j - 1)
                        nc.gpsimd.tensor_tensor(packed(qk, j), prompt(qs)[:, :, j:], prompt(kk)[:, :, :LAG[j]],
                                                ALU.mult).then_inc(s_qk, 1)
                    pool.dma_start(s0[:], io["state"]).then_inc(state_ready, 16)
                    pool.wait_ge(s_kd, 1)
                    make_qk(0)
                    make_qk(1)
                    for j in range(1, BLK):
                        if j + 1 < BLK:
                            make_qk(j + 1)
                        pool.wait_ge(s_term, j + 1)
                        if j >= 2:
                            pool.wait_ge(s_sum, j - 1)
                        o = prompt(out_h)[:, :, j:]
                        nc.gpsimd.tensor_tensor(o, o, packed(term, j), ALU.add).then_inc(s_sum, 1)
                    pool.wait_ge(s_sum, BLK - 1)

                @block.vector
                def _(dve):
                    link = lambda ins, wait=True: step.link(dve, "vector", ins, wait)
                    dve.wait_ge(late, 80)
                    link(nc.vector.tensor_scalar(kk[:], fg[:], -1.0, 1.0, ALU.mult, ALU.add))
                    dve.wait_ge(s_ln, 1)
                    for h in range(H4):
                        cols = slice(h * TP, (h + 1) * TP)
                        last = nc.vector.tensor_tensor_scan(cum[:, cols], smask[:], lf[:, cols], 0.0,
                                                            ALU.mult, ALU.add)
                    last.then_inc(s_b, 1)
                    dve.wait_ge(s_b, 1)
                    cb = blocks(cum[:])
                    ends = cb[:, :, BLK - 1:BLK].to_broadcast([P, NP // BLK, BLK])
                    nc.vector.tensor_tensor(blocks(kd[:]), ends, cb, ALU.subtract).then_inc(s_kd, 1)
                    dve.wait_ge(s_eb, 1)
                    nc.vector.tensor_tensor(qe[:], qs[:, 0:NP], ecum[:], ALU.mult)
                    dve.wait_ge(s_ekd, 1)
                    link(nc.vector.tensor_tensor(kd[:], kd[:], kk[:, 0:NP], ALU.mult))

                    def difference(j):
                        if j >= 3:
                            dve.wait_ge(s_pr, j - 1)
                        nc.vector.tensor_tensor(packed(dif, j), cb[:, :, j:], cb[:, :, :LAG[j]],
                                                ALU.subtract).then_inc(s_dif, 1)

                    def accumulate(j):
                        dve.wait_ge(s_att, j + 1)
                        if j >= 3:
                            dve.wait_ge(s_sum, j - 2)
                        for half in range(2):
                            w = HALF * LAG[j]
                            a = ps[:, 2 * (j % 2) + half, 0:w].rearrange("p (n t) -> p n t", t=LAG[j])
                            v = prompt(vi)[:, half * HALF:(half + 1) * HALF, :LAG[j]]
                            if j == 0:
                                dst = prompt(out_h)[:, half * HALF:(half + 1) * HALF, :]
                            else:
                                dst = packed(term, j)[:, half * HALF:(half + 1) * HALF, :]
                            last = nc.vector.tensor_tensor(dst, a, v, ALU.mult)
                        last.then_inc(s_term, 1)

                    difference(1)
                    for j in range(BLK):
                        if j + 1 < BLK and j >= 1:
                            difference(j + 1)
                        dve.wait_ge(s_qk, j + 1)
                        if j >= 2:
                            dve.wait_ge(s_att, j - 1)
                        if j == 0:
                            nc.vector.tensor_copy(pr[:, 0, :], qk[:, 0, :]).then_inc(s_pr, 1)
                        else:
                            dve.wait_ge(s_edif, j)
                            w = 2 * HALF * LAG[j]
                            nc.vector.scalar_tensor_tensor(out=pr[:, j % 2, 0:w], in0=dif[:, j % 2, 0:w], scalar=1.0,
                                                           in1=qk[:, j % 2, 0:w], op0=ALU.min,
                                                           op1=ALU.mult).then_inc(s_pr, 1)
                        if j >= 1:
                            accumulate(j - 1)
                    accumulate(BLK - 1)
            step.used += 16

            with ExitStack() as c1, nc.Block("mixer_chain", no_gpsimd_drain=True) as block:
                tok_v = sb("token_major_values", [P, 2, H4 * P], c1)
                tok_k = sb("token_major_block_keys", [P, 2, H4 * P], c1)
                PER = P // BLK
                state = sb("state", [P, 3, H4, P], c1)
                diag = sb("diagonal_values", [P, NS, P], c1)
                s_tr = step.sem("tile_transposed")
                s_ck = step.sem("block_keys_copied")
                s_cv = step.sem("tile_values_copied")
                s_up = step.sem("block_update_ready")
                s_st = step.sem("state_ready")
                s_oi = step.sem("inter_block_ready")
                s_dg = step.sem("diagonal_ready")
                s_fs = step.sem("sample_state_decayed")
                s_vb = step.sem("sample_values_spread")
                s_kv = step.sem("sample_outer_product_ready")
                s_os = step.sem("sample_out_ready")
                SPREAD = NS * P // 512
                FIRST = 6

                @block.sync
                def _(sp):
                    for k in range(DC):
                        step.store(sp, io["mem_k_out"][layer, :, k, :], step.mem_k[:, k, :])
                    step.store(sp, io["mem_v_out"][layer], step.mem_v[:])
                    sp.wait_ge(s_st, H4 * NBLK)
                    step.store(sp, io["hgrn_prompt"], state[:, NBLK % 3, :, :])
                    sp.wait_ge(s_kv, 2 * SPREAD)
                    step.store(sp, io["hgrn_sample"], s0[:])

                @block.tensor
                def _(pe):
                    def transposes(tile):
                        if tile:
                            pe.wait_ge(s_ck, PER * tile)
                            pe.wait_ge(s_cv, tile)
                        for which, src in enumerate((kd, vi)):
                            for h in range(H4):
                                cols = slice(h * TP + tile * P, h * TP + (tile + 1) * P)
                                last = nc.tensor.transpose(ps[:, 6 + which, h * P:(h + 1) * P], src[:, cols],
                                                           step.ident)
                        last.then_inc(s_tr, 1)

                    def spread(k):
                        pe.wait_ge(s_dg, 1)
                        if k >= 1:
                            pe.wait_ge(s_kv, 2 * k - 1)
                        nc.tensor.matmul(ps[:, 4, :], step.ones,
                                         diag[:, 4 * k:4 * k + 4, :].rearrange("p a b -> p (a b)"),
                                         start=True, stop=True).then_inc(s_vb, 1)

                    def sample_out(k):
                        pe.wait_ge(s_kv, 2 * k + 2)
                        for c in range(4 * k, 4 * k + 4):
                            last = nc.tensor.matmul(ps[:, 5, c:c + 1], s0[:, c, :], qs[:, NP + c:NP + c + 1],
                                                    start=True, stop=True)
                        if k == SPREAD - 1:
                            last.then_inc(s_os, 1)

                    transposes(0)
                    for n in range(NBLK):
                        if n == PER - 1:
                            transposes(1)
                        if FIRST <= n < FIRST + SPREAD:
                            spread(n - FIRST)
                        if FIRST + 1 < n <= FIRST + 1 + SPREAD:
                            sample_out(n - FIRST - 2)
                        pe.wait_ge(s_ck, n + 1)
                        pe.wait_ge(s_cv, n // PER + 1)
                        if n >= 2:
                            pe.wait_ge(s_st, H4 * (n - 1))
                        for h in range(H4):
                            nc.tensor.matmul(ps[:, n % 2, h * P:(h + 1) * P], tok_k[:, n % 2, h * P:(h + 1) * P],
                                             tok_v[:, n // PER, h * P:(h + 1) * P], start=True, stop=True).then_inc(s_up, 1)
                        if n:
                            for h in range(H4):
                                pe.wait_ge(s_st, H4 * (n - 1) + h + 1)
                                col = (h % 2) * TP + n * BLK
                                nc.tensor.matmul(ps[:, 2 + h // 2, col:col + BLK], state[:, n % 3, h, :],
                                                 qe[:, h * TP + n * BLK:h * TP + (n + 1) * BLK],
                                                 start=True, stop=True).then_inc(s_oi, 1)

                @block.scalar
                def _(act):
                    for n in range(NBLK):
                        act.wait_ge(s_tr, n // PER + 1)
                        if n >= 2:
                            act.wait_ge(s_up, H4 * (n - 1))
                        nc.scalar.activation(tok_k[:, n % 2, :], ps[:, 6, :], ACT.Copy,
                                             scale=step.block_rows[:, n % PER:n % PER + 1]).then_inc(s_ck, 1)

                @block.gpsimd
                def _(pool):
                    nc.gpsimd.tensor_tensor(diag[:], step.ident.unsqueeze(1).to_broadcast([P, NS, P]),
                                            vi[:, NP:NP + NS].unsqueeze(2).to_broadcast([P, NS, P]),
                                            ALU.mult).then_inc(s_dg, 1)
                    pool.wait_ge(state_ready, 16)
                    nc.gpsimd.tensor_tensor(s0[:], s0[:], fg[:, NP:NP + NS].unsqueeze(2).to_broadcast([P, NS, P]),
                                            ALU.mult).then_inc(s_fs, 1)
                    pool.wait_ge(s_fs, 1)

                @block.vector
                def _(dve):
                    def sample_state(k):
                        dve.wait_ge(s_fs, 1)
                        dve.wait_ge(s_vb, k + 1)
                        part = diag[:, 4 * k:4 * k + 4, :]
                        nc.vector.tensor_tensor(part, ps[:, 4, :].rearrange("p (a b) -> p a b", a=4),
                                                kk[:, NP + 4 * k:NP + 4 * k + 4].unsqueeze(2).to_broadcast([P, 4, P]),
                                                ALU.mult).then_inc(s_kv, 1)
                        dve.wait_ge(s_kv, 2 * k + 1)
                        st = s0[:, 4 * k:4 * k + 4, :]
                        nc.vector.tensor_tensor(st, st, part, ALU.add).then_inc(s_kv, 1)

                    for n in range(NBLK):
                        if n % PER == 0:
                            dve.wait_ge(s_tr, n // PER + 1)
                            nc.vector.tensor_copy(tok_v[:, n // PER, :], ps[:, 7, :]).then_inc(s_cv, 1)
                        for h in range(H4):
                            dve.wait_ge(s_up, H4 * (n + 1))
                            if n == 0:
                                ins = nc.vector.tensor_copy(state[:, 1, h, :], ps[:, 0, h * P:(h + 1) * P])
                            else:
                                dve.wait_ge(s_st, H4 * (n - 1) + h + 1)
                                if n >= 3:
                                    dve.wait_ge(s_oi, H4 * (n - 3) + h + 1)
                                end = h * TP + (n + 1) * BLK - 1
                                ins = nc.vector.scalar_tensor_tensor(
                                    out=state[:, (n + 1) % 3, h, :], in0=state[:, n % 3, h, :],
                                    scalar=ecum[:, end:end + 1], in1=ps[:, n % 2, h * P:(h + 1) * P],
                                    op0=ALU.mult, op1=ALU.add)
                            ins.then_inc(s_st, 1)
                        if FIRST <= n < FIRST + SPREAD:
                            sample_state(n - FIRST)
                    link = lambda ins, wait=True: step.link(dve, "vector", ins, wait)
                    dve.wait_ge(s_oi, H4 * (NBLK - 1))
                    for h in range(H4):
                        o = out_h[:, h * TP + BLK:(h + 1) * TP]
                        nc.vector.tensor_tensor(o, o, ps[:, 2 + h // 2, (h % 2) * TP + BLK:(h % 2 + 1) * TP], ALU.add)
                    dve.wait_ge(s_os, 1)
                    nc.vector.tensor_copy(out_h[:, NP:NP + NS], ps[:, 5, 0:NS])

        with ExitStack() as c1, nc.Block("mixer_gate", no_gpsimd_drain=True) as block:
            sq = sb("head_squares", [P, NP + NS], c1)
            win = sb("window_sums", [P, 2, H4, CTX + TP], c1)
            pooled = sb("pooled", [P, H4, T], c1)
            sums = sb("sample_window_sums", [P, H4, TS], c1)
            s_sq = step.sem("head_squares_ready")
            s_ms = step.sem("head_mean_ready")
            s_sd = step.sem("head_deviation_ready")
            s_win = step.sem("window_sums_ready")
            s_pool = step.sem("pooled_ready")
            s_py = step.sem("pool_product_ready")
            PARTS = ((0, 512), (512, NP), (NP, NP + NS))

            @block.sync
            def _(sp):
                step.store(sp, io["pool_prompt"], u_ext[:, :, TP:TP + CTX])
                step.store(sp, io["pool_sample"], s_ext[:, :, :, 1:CTX + 1])

            @block.gpsimd
            def _(pool):
                src, first = u_ext, 0
                for lev in range(H4):
                    shift = 1 << lev
                    first += shift
                    dst = win[:, lev % 2]
                    if lev:
                        pool.wait_ge(s_win, lev)
                    nc.gpsimd.tensor_tensor(dst[:, lev:, first:], src[:, lev:, first:],
                                            src[:, lev:, first - shift:CTX + TP - shift], ALU.add).then_inc(s_win, 1)
                    pool.wait_ge(s_win, lev + 1)
                    step.link(pool, "gpsimd", nc.gpsimd.tensor_tensor(
                        pooled[:, lev, 0:TP], dst[:, lev, CTX:], inv[:, lev, 0:TP], ALU.mult))
                    src = dst
                nc.gpsimd.tensor_tensor(pooled[:, :, 0:TP], pooled[:, :, 0:TP], u_ext[:, :, CTX:],
                                        ALU.subtract).then_inc(s_pool, 1)
                pool.wait_ge(s_pool, 2)

            @block.tensor
            def _(pe):
                pe.wait_ge(s_sq, 1)
                for k, (a, b) in enumerate(PARTS):
                    last = nc.tensor.matmul(ps[:, k, 0:b - a], step.mean_head, sq[:, a:b], start=True, stop=True)
                last.then_inc(s_ms, 1)
                pe.wait_ge(s_pool, 2)
                for g in range(H4):
                    nc.tensor.matmul(ps[:, 4 + g, 0:T], pw[:, g, :], pooled[:, g, :], start=True,
                                     stop=True).then_inc(s_py, 1)

            @block.scalar
            def _(act):
                nc.scalar.activation(sq[:], out_h[:], ACT.Square).then_inc(s_sq, 1)
                act.wait_ge(s_ms, 1)
                for k, (a, b) in enumerate(PARTS):
                    last = nc.scalar.activation(sq[:, a:b], ps[:, k, 0:b - a], ACT.Sqrt, bias=step.eps)
                last.then_inc(s_sd, 1)
                for g in range(H4):
                    act.wait_ge(s_py, g + 1)
                    nc.scalar.activation(step.mixed[:, H4 + g, :], ps[:, 4 + g, 0:T], ACT.Copy, scale=psc[:, g:g + 1])

            @block.vector
            def _(dve):
                link = lambda ins, wait=True: step.link(dve, "vector", ins, wait)
                for g, w in enumerate(POOL_SIZES):
                    last = nc.vector.reduce_sum(sums[:, g, :], s_ext[:, g, :, CTX + 1 - w:], axis=AX)
                link(last)
                link(nc.vector.tensor_tensor(sums[:], sums[:], inv[:, :, TP:T], ALU.mult))
                nc.vector.tensor_tensor(pooled[:, :, TP:T], sums[:], s_ext[:, :, :, CTX],
                                        ALU.subtract).then_inc(s_pool, 1)
                dve.wait_ge(s_sd, 1)
                link(nc.vector.reciprocal(sq[:], sq[:]))
                link(nc.vector.tensor_tensor(out_h[:], out_h[:], sq[:], ALU.mult))
                for h in range(H4):
                    for lo, hi, a, b in ((0, TP, h * TP, (h + 1) * TP), (TP, T, NP + h * TS, NP + (h + 1) * TS)):
                        nc.vector.scalar_tensor_tensor(out=step.mixed[:, h, lo:hi], in0=out_h[:, a:b],
                                                       scalar=ng[:, h:h + 1], in1=sg[:, a:b],
                                                       op0=ALU.mult, op1=ALU.mult)


def window_mixer(step, layer):
    nc, io, ps = step.nc, step.io, step.ps
    base = step.used
    with ExitStack() as ctx:
        def sb(name, shape, c=ctx):
            return step.sb(name, shape, ctx=c)
        kT = sb("window_k_T", [P, KV, T])
        vt = sb("window_v", [P, 2, KV, P])
        vs = sb("window_v_sample", [TS, KV, P])
        kx = sb("sample_k_T", [P, TS, KV, P])
        vx = sb("sample_v", [P, TS, KV, P])
        snk = sb("sinks", [P, HEADS_C + 1])
        nsnk = sb("negative_sinks", [P, HEADS_C + 1])
        mem = sb("memory_T1", [P, DC, NMEM])
        late = step.sem("window_inputs_ready")
        windows_ready = step.sem("sample_windows_ready")
        s_vrow = step.sem("sample_value_row_stored")

        with nc.Block("window_in", no_gpsimd_drain=True) as block:
            s_cp = step.sem("window_chunk_copied")
            number_slabs(step, base, 10)

            @block.sync
            def _(sp):
                step.load_until(sp, base + 12 + SLOTS)

            @block.gpsimd
            def _(pool):
                for dst, name in ((snk[:], "sinks"), (mem[:], "mem")):
                    pool.dma_start(dst, io[name]).then_inc(late, 16)
                for j in range(1, 10):
                    split_low(step, pool, base + j, (0,))
                slabs_split(step, pool, base + 9)

            @block.vector
            def _(dve):
                for j in range(1, 10):
                    split_low(step, dve, base + j, (1,))

            @block.tensor
            def _(pe):
                for j in range(12):
                    if j >= 4:
                        pe.wait_ge(s_cp, j - 3)
                    if j < 10:
                        product(step, pe, base + j, j % 4)
                        continue
                    step.wait_slab(pe, base + j)
                    w = step.slab(base + j)
                    for t, (a, b) in enumerate(((0, P), (P, TP), (TP, T))):
                        for c in range(DC):
                            last = nc.tensor.matmul(ps[0:b - a, j % 4, t * P:(t + 1) * P], step.x[:, c, a:b], w[:, c, :],
                                                    start=(c == 0), stop=(c == DC - 1))
                    last.then_inc(step.product_done, 1)

            @block.scalar
            def _(act):
                split_high(step, act, base + 1)
                for j in range(12):
                    if j + 2 < 10:
                        split_high(step, act, base + j + 2)
                    act.wait_ge(step.product_done, step.product_count(base + j))
                    if j < 8:
                        ins = nc.scalar.activation(step.q[:, j, :], ps[:, j % 4, 0:T], ACT.Copy, scale=HD ** -0.5)
                    elif j < 10:
                        ins = nc.scalar.activation(kT[:, j - 8, :], ps[:, j % 4, 0:T], ACT.Copy)
                    else:
                        nc.scalar.activation(vt[:, :, j - 10, :], ps[:, j % 4, 0:TP].rearrange("p (a b) -> p a b", a=2),
                                             ACT.Copy)
                        ins = nc.scalar.activation(vs[:, j - 10, :], ps[0:TS, j % 4, TP:TP + P], ACT.Copy)
                    ins.then_inc(s_cp, 1)
        step.used += 12

        base = step.used
        with ExitStack() as c1, nc.Block("window_prompt", no_gpsimd_drain=True) as block:
            NB = 3
            sc = sb("scores", [P, NB, 3 * P], c1)
            pt = sb("probabilities_T", [P, 2, 3 * P], c1)
            neg = sb("negative_maxima", [P, NB, 2], c1)
            den = sb("denominators", [P, NB, 2], c1)
            esk = sb("sink_terms", [P, NB, 2], c1)
            s_s = step.sem("window_scores_ready")
            s_mk = step.sem("window_scores_masked")
            s_m = step.sem("window_maxima_ready")
            s_e = step.sem("window_exp_ready")
            s_p = step.sem("window_probabilities_ready")
            s_t = step.sem("window_transposed")
            s_pt = step.sem("window_transposed_copied")
            s_o = step.sem("window_output_ready")
            s_oc = step.sem("window_output_copied")
            s_mem = step.sem("memory_chunk_copied1")
            QK = ((0, P), (P, 3 * P))

            @block.gpsimd
            def _(pool):
                for dst, name in ((kx[:, :, :, 0:P - 1], "window_k"), (vx[0:P - 1], "window_v")):
                    pool.dma_start(dst, io[name]).then_inc(windows_ready, 16)

            @block.sync
            def _(sp):
                sp.dma_start(vx[P - 1:P], vs[:]).then_inc(s_vrow, 16)
                step.store(sp, io["window_k_prompt"], kT[0:HD, :, P:TP])
                step.store(sp, io["window_v_prompt"], vt[:, 1, :, 0:HD])
                step.load_until(sp, base + 16 + SLOTS)

            @block.tensor
            def _(pe):
                def scores(h):
                    e, j, kv = h % 2, h // 2, h // (HEADS_C // KV)
                    rows = slice(e * HD, (e + 1) * HD)
                    if h >= 2:
                        pe.wait_ge(s_mk, h - 1)
                    nc.tensor.matmul(ps[:, h % 2, 0:P], step.q[rows, j, 0:P], kT[rows, kv, 0:P], start=True, stop=True)
                    nc.tensor.matmul(ps[:, h % 2, P:3 * P], step.q[rows, j, P:TP], kT[rows, kv, 0:TP], start=True,
                                     stop=True).then_inc(s_s, 1)

                def transposes(h):
                    pe.wait_ge(s_p, h + 1)
                    if h >= 2:
                        pe.wait_ge(s_pt, h - 1)
                    for k in range(3):
                        last = nc.tensor.transpose(ps[:, 2 + h % 2, k * P:(k + 1) * P], sc[:, h % NB, k * P:(k + 1) * P],
                                                   step.ident)
                    last.then_inc(s_t, 1)

                def values(h):
                    kv = h // (HEADS_C // KV)
                    pe.wait_ge(s_pt, h + 1)
                    if h >= 2:
                        pe.wait_ge(s_oc, h - 1)
                    bank = ps[:, 4 + h % 2, :]
                    nc.tensor.matmul(bank[:, 0:P], vt[:, 0, kv, :], pt[:, h % 2, 0:P], start=True, stop=True)
                    nc.tensor.matmul(bank[:, P:TP], vt[:, 0, kv, :], pt[:, h % 2, P:2 * P], start=True, stop=False)
                    nc.tensor.matmul(bank[:, P:TP], vt[:, 1, kv, :], pt[:, h % 2, 2 * P:3 * P], start=False,
                                     stop=True).then_inc(s_o, 1)

                pe.wait_ge(late, 32)
                scores(0)
                scores(1)
                for h in range(HEADS_C):
                    memory_product(step, pe, base + h, h, mem, 6 + h % 2, s_mem)
                    if h + 2 < HEADS_C:
                        scores(h + 2)
                    transposes(h)
                    if h:
                        values(h - 1)
                values(HEADS_C - 1)

            @block.vector
            def _(dve):
                link = lambda ins, wait=True: step.link(dve, "vector", ins, wait)
                dve.wait_ge(late, 32)
                link(nc.vector.tensor_scalar(nsnk[:], snk[:], -1.0, None, ALU.mult))

                def head_scores(h):
                    b = h % NB
                    dve.wait_ge(s_s, h + 1)
                    if h >= NB:
                        dve.wait_ge(s_t, h - NB + 1)
                    nc.vector.tensor_tensor(sc[:, b, :], ps[:, h % 2, 0:3 * P], step.masks, ALU.add).then_inc(s_mk, 1)
                    dve.wait_ge(s_mk, h + 1)
                    for t, (lo, hi) in enumerate(QK):
                        last = nc.vector.tensor_reduce(neg[:, b, t:t + 1], sc[:, b, lo:hi], AX, ALU.max, negate=True)
                    link(last)
                    nc.vector.tensor_scalar(neg[:, b, :], neg[:, b, :], nsnk[:, h:h + 1], None, ALU.min).then_inc(s_m, 1)

                def head_rest(h):
                    b = h % NB
                    dve.wait_ge(s_e, h + 1)
                    link(nc.vector.tensor_tensor(den[:, b, :], den[:, b, :], esk[:, b, :], ALU.add))
                    link(nc.vector.reciprocal(den[:, b, :], den[:, b, :]))
                    for t, (lo, hi) in enumerate(QK):
                        last = nc.vector.tensor_scalar(sc[:, b, lo:hi], sc[:, b, lo:hi], den[:, b, t:t + 1], None, ALU.mult)
                    last.then_inc(s_p, 1)

                def head_out(h):
                    e = h % 2
                    rows = slice(e * HD, (e + 1) * HD)
                    dve.wait_ge(s_o, h + 1)
                    nc.vector.tensor_copy(step.mixed[rows, h // 2, 0:TP], ps[rows, 4 + h % 2, 0:TP]).then_inc(s_oc, 1)

                head_scores(0)
                for h in range(HEADS_C):
                    if h + 1 < HEADS_C:
                        head_scores(h + 1)
                    head_rest(h)
                    if h >= 2:
                        head_out(h - 2)
                for h in range(HEADS_C - 2, HEADS_C):
                    head_out(h)

            @block.scalar
            def _(act):
                def head_exp(h):
                    b = h % NB
                    act.wait_ge(s_m, h + 1)
                    if h >= NB:
                        act.wait_ge(s_p, h - NB + 1)
                    for t, (lo, hi) in enumerate(QK):
                        nc.scalar.activation(sc[:, b, lo:hi], sc[:, b, lo:hi], ACT.Exp, bias=neg[:, b, t:t + 1],
                                             accum_out=den[:, b, t:t + 1])
                    nc.scalar.activation(esk[:, b, :], neg[:, b, :], ACT.Exp, bias=snk[:, h:h + 1]).then_inc(s_e, 1)

                def head_copy(h):
                    act.wait_ge(s_t, h + 1)
                    if h >= 2:
                        act.wait_ge(s_o, h - 1)
                    nc.scalar.activation(pt[:, h % 2, :], ps[:, 2 + h % 2, 0:3 * P], ACT.Copy).then_inc(s_pt, 1)

                for h in range(HEADS_C):
                    head_exp(h)
                    if h:
                        head_copy(h - 1)
                    memory_copy(step, act, base + h, h, 6 + h % 2, s_mem)
                head_copy(HEADS_C - 1)
        step.used += 16

        with ExitStack() as c1, nc.Block("window_sample", no_gpsimd_drain=True) as block:
            st = sb("sample_scores_T", [P, P], c1)
            ss = sb("sample_scores", [P, P], c1)
            sp_t = sb("sample_probabilities_T", [P, P], c1)
            sm = sb("sample_small", [P, 3], c1)
            s_k = step.sem("sample_key_column_ready")
            s_s = step.sem("sample_scores_T_ready")
            s_sc = step.sem("sample_scores_T_copied")
            s_t = step.sem("sample_scores_ready")
            s_m = step.sem("sample_maxima_ready")
            s_e = step.sem("sample_exp_ready")
            s_p = step.sem("sample_probabilities_ready")
            s_pt = step.sem("sample_probabilities_T_ready")
            s_pc = step.sem("sample_probabilities_T_copied")
            s_o = step.sem("sample_output_ready")

            @block.sync
            def _(sp):
                for k in range(DC):
                    step.store(sp, io["mem_k_out"][layer, :, k, :], step.mem_k[:, k, :])
                step.store(sp, io["mem_v_out"][layer], step.mem_v[:])
                sp.wait_ge(windows_ready, 32)
                sp.wait_ge(s_k, 1)
                step.store(sp, io["window_k_sample"], kx[0:HD])
                sp.wait_ge(s_vrow, 16)
                step.store(sp, io["window_v_sample"], vx[:, :, :, 0:HD])

            @block.tensor
            def _(pe):
                pe.wait_ge(windows_ready, 32)
                pe.wait_ge(s_k, 1)
                for b in range(TS):
                    for kv in range(KV):
                        for e in range(2):
                            rows = slice(e * HD, (e + 1) * HD)
                            col = (b * KV + kv) * 4
                            last = nc.tensor.matmul(ps[:, 4 * e, col:col + 4], kx[rows, b, kv, :],
                                                    step.q[rows, kv * 4:kv * 4 + 4, TP + b], start=True, stop=True)
                last.then_inc(s_s, 1)
                pe.wait_ge(s_sc, 1)
                nc.tensor.transpose(ps[:, 1, 0:P], st[:], step.ident).then_inc(s_t, 1)
                pe.wait_ge(s_p, 1)
                nc.tensor.transpose(ps[:, 2, 0:P], ss[:], step.ident).then_inc(s_pt, 1)
                pe.wait_ge(s_pc, 1)
                pe.wait_ge(s_vrow, 16)
                for b in range(TS):
                    for kv in range(KV):
                        col = (b * KV + kv) * 8
                        last = nc.tensor.matmul(ps[:, 3, col:col + 8], vx[:, b, kv, :], sp_t[:, col:col + 8],
                                                start=True, stop=True)
                last.then_inc(s_o, 1)

            @block.scalar
            def _(act):
                act.wait_ge(s_m, 1)
                nc.scalar.activation(ss[:], ss[:], ACT.Exp, bias=sm[:, 0:1], accum_out=sm[:, 1:2])
                nc.scalar.activation(sm[:, 2:3], sm[:, 0:1], ACT.Exp, bias=snk[:, HEADS_C:]).then_inc(s_e, 1)
                act.wait_ge(s_pt, 1)
                nc.scalar.activation(sp_t[:], ps[:, 2, 0:P], ACT.Copy).then_inc(s_pc, 1)

            @block.vector
            def _(dve):
                link = lambda ins, wait=True: step.link(dve, "vector", ins, wait)
                nc.vector.tensor_copy(kx[:, :, :, P - 1], kT[:, :, TP:T].rearrange("p k b -> p b k")).then_inc(s_k, 1)
                dve.wait_ge(s_s, 1)
                for e in range(2):
                    last = nc.vector.tensor_copy(st[:].rearrange("p (g e j) -> p g e j", e=2, j=4)[:, :, e],
                                                 ps[:, 4 * e, 0:HD].rearrange("p (g j) -> p g j", j=4))
                last.then_inc(s_sc, 1)
                dve.wait_ge(s_t, 1)
                link(nc.vector.tensor_copy(ss[:], ps[:, 1, 0:P]))
                link(nc.vector.tensor_reduce(sm[:, 0:1], ss[:], AX, ALU.max, negate=True))
                nc.vector.tensor_scalar(sm[:, 0:1], sm[:, 0:1], nsnk[:, HEADS_C:], None, ALU.min).then_inc(s_m, 1)
                dve.wait_ge(s_e, 1)
                link(nc.vector.tensor_tensor(sm[:, 1:2], sm[:, 1:2], sm[:, 2:3], ALU.add))
                link(nc.vector.reciprocal(sm[:, 1:2], sm[:, 1:2]))
                nc.vector.tensor_scalar(ss[:], ss[:], sm[:, 1:2], None, ALU.mult).then_inc(s_p, 1)
                dve.wait_ge(s_o, 1)
                o = ps[:, 3, 0:P].rearrange("p (b k e j) -> p k e j b", b=TS, k=KV, e=2)
                dst = step.mixed[:].rearrange("p (k j) t -> p k j t", k=KV)
                for e in range(2):
                    rows = slice(e * HD, (e + 1) * HD)
                    nc.vector.tensor_copy(dst[rows, :, :, TP:T], o[rows, :, e])


def cross_attention(step, layer):
    nc, io, ps = step.nc, step.io, step.ps
    base = step.used
    L = f"_{layer}"
    ck, cv = step.cache
    NR = MH * TS
    with ExitStack() as ctx:
        own = step.own[:, 0:TS * MH * 2 * NR]
        own_row = bass.AP(step.own, 0, [step.own[:].ap[0], [MH * 2 * NR + MH, TS], [2 * NR + 1, MH], [NR, 2]])
        number_slabs(step, base, DC)
        with nc.Block("cross_query" + L, no_gpsimd_drain=True) as block:
            s_cp = step.sem("query_chunk_copied" + L)

            @block.gpsimd
            def _(pool):
                for j in range(1, DC):
                    split_low(step, pool, base + j, (0,))
                slabs_split(step, pool, base + DC - 1)

            @block.vector
            def _(dve):
                for j in range(1, DC):
                    split_low(step, dve, base + j, (1,))

            @block.sync
            def _(sp):
                for j in range(DC):
                    step.load_until(sp, base + j + 1 + SLOTS)
                    if j < KEYS_LATER:
                        step.load_cache(sp, layer, 0, TS - KEYS_LATER + j)

            @block.tensor
            def _(pe):
                for j in range(DC):
                    if j >= 4:
                        pe.wait_ge(s_cp, j - 3)
                    product(step, pe, base + j, j % 4)

            @block.scalar
            def _(act):
                split_high(step, act, base + 1)
                for j in range(DC):
                    if j + 2 < DC:
                        split_high(step, act, base + j + 2)
                    act.wait_ge(step.product_done, step.product_count(base + j))
                    nc.scalar.activation(step.q[:, j, :], ps[:, j % 4, 0:T], ACT.Copy, scale=MHD ** -0.5).then_inc(s_cp, 1)
        step.used += DC

        with ExitStack() as c1, nc.Block("cross_attention" + L, no_gpsimd_drain=True) as block:
            room = step.squares[:].rearrange("p c t -> p (c t)")
            pr = room[:, 0:4 * NMEM].rearrange("p (a b m) -> p a b m", a=2, b=2)
            pt = room[:, 4 * NMEM:4 * NMEM + 4 * TP].rearrange("p (a b t) -> p a b t", a=2, b=2)
            sm = step.sb("cross_small" + L, [P, 2, 2, 2], ctx=c1)
            ss = step.sb("cross_sample_p" + L, [NR, NMEM], ctx=c1)
            ssm = step.sb("cross_sample_small" + L, [NR, 2], ctx=c1)
            s_ks = step.sem("cross_sample_scores_made" + L)
            s_vs = step.sem("cross_sample_values_made" + L)
            s_s = step.sem("cross_scores_ready" + L)
            s_m = step.sem("cross_maxima_ready" + L)
            s_e = step.sem("cross_exp_ready" + L)
            s_p = step.sem("cross_probabilities_ready" + L)
            s_t = step.sem("cross_transposed" + L)
            s_pt = step.sem("cross_transposed_copied" + L)
            s_o = step.sem("cross_output_ready" + L)
            s_oc = step.sem("cross_output_copied" + L)
            s_sq = step.sem("cross_sample_queries_placed" + L)
            s_zero = step.sem("cross_own_rows_zeroed" + L)

            @block.sync
            def _(sp):
                for b in range(TS):
                    step.load_cache(sp, layer, 1, b)

            @block.gpsimd
            def _(pool):
                nc.gpsimd.memset(own, 0.0).then_inc(s_zero, 1)
                pool.wait_ge(s_zero, 1)
            s_sm = step.sem("cross_sample_maxima_ready" + L)
            s_se = step.sem("cross_sample_exp_ready" + L)
            s_sp = step.sem("cross_sample_probabilities_ready" + L)
            s_st = step.sem("cross_sample_probabilities_transposed" + L)
            s_sy = step.sem("cross_sample_probabilities_copied" + L)
            s_so = step.sem("cross_sample_output_copied" + L)
            s_sot = step.sem("cross_sample_output_transposed" + L)

            @block.tensor
            def _(pe):
                def scores(h):
                    if h >= 2:
                        pe.wait_ge(s_e, h - 1)
                    for t in range(2):
                        for c in range(2):
                            last = nc.tensor.matmul(ps[:, h % 2, t * NMEM:(t + 1) * NMEM],
                                                    step.q[:, 2 * h + c, t * P:(t + 1) * P], step.mem_k[:, 2 * h + c, :],
                                                    start=(c == 0), stop=(c == 1))
                    last.then_inc(s_s, 1)

                def transposes(h):
                    pe.wait_ge(s_p, h + 1)
                    if h >= 2:
                        pe.wait_ge(s_pt, h - 1)
                    for m in range(2):
                        for t in range(2):
                            col = m * TP + t * P
                            last = nc.tensor.transpose(ps[:, 2 + h % 2, col:col + P], pr[:, h % 2, t, m * P:(m + 1) * P],
                                                       step.ident)
                    last.then_inc(s_t, 1)

                def values(h):
                    pe.wait_ge(s_pt, h + 1)
                    if h >= 2:
                        pe.wait_ge(s_oc, h - 1)
                    for d in range(2):
                        for m in range(2):
                            f = h * MHD + d * P
                            last = nc.tensor.matmul(ps[:, 4 + h % 2, d * TP:(d + 1) * TP], step.mem_v[:, m, f:f + P],
                                                    pt[:, h % 2, m, :], start=(m == 0), stop=(m == 1))
                    last.then_inc(s_o, 1)

                def left(b, h, c):
                    col = ((b * MH + h) * 2 + c) * NR
                    return own[:, col:col + NR]

                def sample_scores(b):
                    pe.wait_ge(step.cache_ready[0], 16 * TS)
                    for h in range(MH):
                        for c in range(2):
                            last = nc.tensor.matmul(ps[0:NR, 6, 0:NMEM], left(b, h, c), ck[:, b, 2 * h + c, :],
                                                    start=(b + h + c == 0), stop=(b == TS - 1 and h == MH - 1 and c == 1))
                    if b == TS - 1:
                        last.then_inc(s_ks, 1)

                def sample_transpose():
                    pe.wait_ge(s_sp, 1)
                    for m in range(2):
                        last = nc.tensor.transpose(ps[:, 7, 256 + m * NR:256 + (m + 1) * NR], ss[:, m * P:(m + 1) * P],
                                                   step.ident[0:NR, 0:NR])
                    last.then_inc(s_st, 1)

                def sample_values(b):
                    pe.wait_ge(step.cache_ready[1], 16 * TS)
                    for h in range(MH):
                        for m in range(2):
                            last = nc.tensor.matmul(ps[0:NR, 6, 0:MHD], left(b, h, m), cv[:, b, m, h * MHD:(h + 1) * MHD],
                                                    start=(b + h + m == 0), stop=(b == TS - 1 and h == MH - 1 and m == 1))
                    if b == TS - 1:
                        last.then_inc(s_vs, 1)

                scores(0)
                scores(1)
                pe.wait_ge(s_sq, 1)
                for h in range(2):
                    for b in (4 * h, 4 * h + 1):
                        sample_scores(b)
                    transposes(h)
                    for b in (4 * h + 2, 4 * h + 3):
                        sample_scores(b)
                    values(h)
                    scores(h + 2)
                transposes(2)
                values(2)
                sample_transpose()
                transposes(3)
                pe.wait_ge(s_sy, 1)
                for b in range(4):
                    sample_values(b)
                values(3)
                for b in range(4, TS):
                    sample_values(b)
                pe.wait_ge(s_so, 1)
                for d in range(2):
                    last = nc.tensor.transpose(ps[:, 7, d * NR:(d + 1) * NR], ss[:, d * P:(d + 1) * P],
                                               step.ident[0:NR, 0:NR])
                last.then_inc(s_sot, 1)

            @block.scalar
            def _(act):
                def head_exp(h):
                    act.wait_ge(s_m, h + 1)
                    if h >= 2:
                        act.wait_ge(s_t, h - 1)
                    for t in range(2):
                        last = nc.scalar.activation(pr[:, h % 2, t, :], ps[:, h % 2, t * NMEM:(t + 1) * NMEM], ACT.Exp,
                                                    bias=sm[:, h % 2, 0, t:t + 1], accum_out=sm[:, h % 2, 1, t:t + 1])
                    last.then_inc(s_e, 1)

                def head_copy(h):
                    act.wait_ge(s_t, h + 1)
                    if h >= 2:
                        act.wait_ge(s_o, h - 1)
                    nc.scalar.activation(pt[:, h % 2].rearrange("p a b -> p (a b)"), ps[:, 2 + h % 2, :],
                                         ACT.Copy).then_inc(s_pt, 1)
                act.wait_ge(s_zero, 1)
                nc.scalar.activation(own_row, step.q[:, :, TP:T].rearrange("p (h c) b -> p b h c", h=MH),
                                     ACT.Copy).then_inc(s_sq, 1)
                head_exp(0)
                head_exp(1)
                head_copy(0)
                head_exp(2)
                head_copy(1)
                act.wait_ge(s_sm, 1)
                nc.scalar.activation(ss[:], ps[0:NR, 6, 0:NMEM], ACT.Exp, bias=ssm[:, 0:1],
                                     accum_out=ssm[:, 1:2]).then_inc(s_se, 1)
                head_exp(3)
                head_copy(2)
                act.wait_ge(s_st, 1)
                nc.scalar.activation(own_row, ps[:, 7, 256:256 + 2 * NR].rearrange("p (c b h) -> p b h c", c=2, b=TS),
                                     ACT.Copy).then_inc(s_sy, 1)
                head_copy(3)
                act.wait_ge(s_vs, 1)
                nc.scalar.activation(ss[:], ps[0:NR, 6, 0:MHD], ACT.Copy).then_inc(s_so, 1)

            @block.vector
            def _(dve):
                link = lambda ins, wait=True: step.link(dve, "vector", ins, wait)

                def head_max(h):
                    dve.wait_ge(s_s, h + 1)
                    if h >= 2:
                        dve.wait_ge(s_p, h - 1)
                    nc.vector.tensor_reduce(sm[:, h % 2, 0, :], ps[:, h % 2, :].rearrange("p (t m) -> p t m", t=2), AX,
                                            ALU.max, negate=True).then_inc(s_m, 1)

                def head_norm(h):
                    dve.wait_ge(s_e, h + 1)
                    link(nc.vector.reciprocal(sm[:, h % 2, 1, :], sm[:, h % 2, 1, :]))
                    for t in range(2):
                        last = nc.vector.tensor_scalar(pr[:, h % 2, t, :], pr[:, h % 2, t, :], sm[:, h % 2, 1, t:t + 1],
                                                       None, ALU.mult)
                    last.then_inc(s_p, 1)

                def head_out(h):
                    dve.wait_ge(s_o, h + 1)
                    nc.vector.tensor_copy(step.mixed[:, 2 * h:2 * h + 2, 0:TP],
                                          ps[:, 4 + h % 2, :].rearrange("p (d t) -> p d t", d=2)).then_inc(s_oc, 1)

                head_max(0)
                head_max(1)
                head_norm(0)
                head_max(2)
                head_norm(1)
                head_out(0)
                dve.wait_ge(s_ks, 1)
                nc.vector.tensor_reduce(ssm[:, 0:1], ps[0:NR, 6, 0:NMEM], AX, ALU.max, negate=True).then_inc(s_sm, 1)
                head_max(3)
                head_norm(2)
                head_out(1)
                dve.wait_ge(s_se, 1)
                link(nc.vector.reciprocal(ssm[:, 1:2], ssm[:, 1:2]))
                nc.vector.tensor_scalar(ss[:], ss[:], ssm[:, 1:2], None, ALU.mult).then_inc(s_sp, 1)
                head_norm(3)
                head_out(2)
                head_out(3)
                dve.wait_ge(s_sot, 1)
                nc.vector.tensor_copy(step.mixed[:, :, TP:T].rearrange("p (h d) b -> p d b h", h=MH),
                                      ps[:, 7, 0:2 * NR].rearrange("p (d b h) -> p d b h", d=2, b=TS))


TILES = ((0, P), (P, TP), (TP, T))


def peer(step, layer):
    nc, io, ps = step.nc, step.io, step.ps
    L = f"_{layer}"
    with ExitStack() as ctx:
        big = step.sb("expert_activations" + L, [P, NKEYS, T], ctx=ctx)
        qT = big[:, NKEYS - 2 * PH:, :]
        FIRST_BORROWED = NKEYS - 48
        scratch = big[:, FIRST_BORROWED:NKEYS - 2 * PH, :].rearrange("p a b -> p (a b)")
        pick = step.sb("selections" + L, [P, 3, 3, P], ctx=ctx)
        selT = step.squares[:, 0:3, :]
        keys_ready = step.sem("subkeys_ready" + L)
        peer_query(step, layer, qT, scratch[:, 0:2 * PH * P], keys_ready)
        peer_up(step, layer, big, qT, scratch, pick, selT, keys_ready, FIRST_BORROWED)
        peer_gates(step, layer, big, selT)
        peer_down(step, layer, big)


def peer_query(step, layer, qT, keys, keys_ready):
    nc, io, ps = step.nc, step.io, step.ps
    L = f"_{layer}"
    base = step.used
    NQ = 2 * PH
    number_slabs(step, base, NQ)
    with nc.Block("peer_query" + L, no_gpsimd_drain=True) as block:
        s_cp = step.sem("peer_query_chunk_copied" + L)

        @block.sync
        def _(sp):
            sp.dma_start(keys, io["subkeys"][layer]).then_inc(keys_ready, 16)
            step.load_until(sp, base + NQ + SLOTS)

        @block.tensor
        def _(pe):
            for j in range(NQ):
                if j >= 4:
                    pe.wait_ge(s_cp, j - 3)
                product(step, pe, base + j, j % 4)

        @block.gpsimd
        def _(pool):
            for j in range(1, NQ):
                split_low(step, pool, base + j, (0,))
            slabs_split(step, pool, base + NQ - 1)

        @block.vector
        def _(dve):
            for j in range(1, NQ):
                split_low(step, dve, base + j, (1,))

        @block.scalar
        def _(act):
            split_high(step, act, base + 1)
            for j in range(NQ):
                if j + 2 < NQ:
                    split_high(step, act, base + j + 2)
                act.wait_ge(step.product_done, step.product_count(base + j))
                nc.scalar.activation(qT[:, j, :], ps[:, j % 4, 0:T], ACT.Copy).then_inc(s_cp, 1)
    step.used += NQ


def peer_up(step, layer, big, qT, scratch, pick, selT, keys_ready, first_borrowed):
    nc, io, ps = step.nc, step.io, step.ps
    L = f"_{layer}"
    base = step.used
    ub = step.slabs[base][1]
    keys = scratch[:, 0:2 * PH * P].rearrange("p (k n) -> p k n", n=P)
    xh, xl = step.operand
    with ExitStack() as c1, nc.Block("peer_up" + L, no_gpsimd_drain=True) as block:
        hi = step.sb("u_hi" + L, [P, 4, HC, P], F32R, ctx=c1)
        lo = step.sb("u_lo" + L, [P, 4, HC, P], F32R, ctx=c1)
        s_hi = step.sem("u_hi_ready" + L)
        s_h = step.sem("up_half_product_ready" + L)
        s_g = step.sem("up_product_read" + L)
        s_sc = step.sem("routing_scores_ready" + L)
        s_sr = step.sem("routing_scores_read" + L)
        s_rt = step.sem("routing_done" + L)
        den = step.sb("gate_sums" + L, [P, 3, PH], ctx=c1)
        s_e = step.sem("gate_exp_ready" + L)
        s_w = step.sem("gates_ready" + L)
        s_t = step.sem("selections_transposed" + L)
        GATES = 100
        SPLIT = (0, 8, 28, GATES, NKEYS)

        @block.sync
        def _(sp):
            with sp.Fori(1, NKEYS // SLOTS) as i:
                for s in range(SLOTS):
                    sp.wait_ge(step.u_split, 2 * (ub + SLOTS * i + s + 1 - SLOTS))
                    sp.dma_start(step.ring[:, s, :], io["u"][layer * P + SLOTS * i + s]).then_inc(step.slab_ready[s], 16)
            step.loaded = base + NKEYS
            step.load_until(sp, base + NKEYS + SLOTS)

        def ready(i):
            return 16 * (base // SLOTS + 1) + 16 * i

        @block.gpsimd
        def _(pool):
            def split(i, s):
                for g in range(2):
                    pool.wait_ge(s_hi, 2 * (SLOTS * i + s) + g + 1)
                    buf = (2 * s + g) % 4
                    nc.gpsimd.tensor_tensor(lo[:, buf], step.slab(s)[:, g * HC:(g + 1) * HC, :], hi[:, buf].bitcast(F32),
                                            ALU.subtract).then_inc(step.u_split, 1)
            with pool.Fori(0, NKEYS // SLOTS) as i:
                for s in range(SLOTS):
                    split(i, s)
            pool.wait_ge(step.u_split, 2 * (ub + NKEYS))

        @block.tensor
        def _(pe):
            def scores(t):
                a, b = TILES[t]
                if t:
                    pe.wait_ge(s_sr, t)
                else:
                    pe.wait_ge(keys_ready, 16)
                for k in range(2 * PH):
                    last = nc.tensor.matmul(ps[0:b - a, 2 + k // 4, (k % 4) * P:(k % 4 + 1) * P], qT[:, k, a:b], keys[:, k, :],
                                            start=True, stop=True)
                last.then_inc(s_sc, 1)

            def up(i, s, first):
                if not (first and s < 2):
                    pe.wait_ge(s_g, SLOTS * i + s - 1)
                bank = ps[:, s % 2, 0:T]
                for g in range(2):
                    pe.wait_ge(step.u_split, 2 * (ub + SLOTS * i + s) + g + 1)
                    buf = (2 * s + g) % 4
                    for k in range(HC):
                        c = g * HC + k
                        nc.tensor.matmul(bank, hi[:, buf, k, :], xh[:, c, :], start=(c == 0), stop=False)
                        nc.tensor.matmul(bank, hi[:, buf, k, :], xl[:, c, :], start=False, stop=False)
                        last = nc.tensor.matmul(bank, lo[:, buf, k, :], xh[:, c, :], start=False, stop=(c == DC - 1))
                    last.then_inc(s_h, 1)

            scores(0)
            for s in range(SLOTS):
                up(0, s, True)
            def transposes(t):
                a, b = TILES[t]
                pe.wait_ge(s_w, t + 1)
                for w in range(3):
                    last = nc.tensor.transpose(ps[:, 2 + t, w * P:w * P + b - a], pick[0:b - a, t, w, :],
                                               step.ident[0:b - a, 0:b - a])
                last.then_inc(s_t, 1)

            for t in range(4):
                if 1 <= t < 3:
                    scores(t)
                elif t == 3:
                    for tile in range(3):
                        transposes(tile)
                with pe.Fori(max(1, SPLIT[t] // SLOTS), SPLIT[t + 1] // SLOTS) as i:
                    for s in range(SLOTS):
                        up(i, s, False)

        @block.scalar
        def _(act):
            def high(i, s, g, first=False):
                if g == 0:
                    act.wait_ge(step.slab_ready[s], ready(i))
                if not first:
                    act.wait_ge(s_h, 2 * (SLOTS * i + s) + g - 3)
                buf = (2 * s + g) % 4
                nc.scalar.activation(hi[:, buf], step.slab(s)[:, g * HC:(g + 1) * HC, :], ACT.Copy).then_inc(s_hi, 1)

            def gelu(i, s):
                act.wait_ge(s_h, 2 * (SLOTS * i + s) + 2)
                nc.scalar.activation(big[:, SLOTS * i + s, :], ps[:, s % 2, 0:T], ACT.Gelu_apprx_tanh).then_inc(s_g, 1)

            nc.scalar.preload_act_table(ACT.Gelu_apprx_tanh)
            for s in range(2):
                for g in range(2):
                    high(0, s, g, first=True)
            for lo_i, hi_i in ((0, first_borrowed // SLOTS), (first_borrowed // SLOTS, NKEYS // SLOTS - 1)):
                if lo_i:
                    act.wait_ge(s_rt, 3)
                    for t, (a, b) in enumerate(TILES):
                        w = pick[0:b - a, t, 2, :]
                        nc.scalar.activation(w, w, ACT.Exp).then_inc(s_e, 1)
                    nc.scalar.preload_act_table(ACT.Gelu_apprx_tanh)
                with act.Fori(lo_i, hi_i) as i:
                    for s in range(SLOTS):
                        ahead = (i, s + 2) if s < 2 else (i + 1, s - 2)
                        high(*ahead, 0)
                        gelu(i, s)
                        high(*ahead, 1)
            final = NKEYS // SLOTS - 1
            for s in range(SLOTS):
                if s < 2:
                    high(final, s + 2, 0)
                gelu(final, s)
                if s < 2:
                    high(final, s + 2, 1)

        @block.vector
        def _(dve):
            link = lambda ins, wait=True: step.link(dve, "vector", ins, wait)
            at = 2 * PH * P

            def take(n, dt=F32):
                nonlocal at
                at += n
                v = scratch[:, at - n:at]
                return v if dt == F32 else v.bitcast(dt)
            NQ = 2 * PH
            rest = take(NQ * P).rearrange("p (k n) -> p k n", n=P)
            val = take(NQ * TOPK).rearrange("p (k n) -> p k n", n=TOPK)
            idx = take(NQ * TOPK, U32).rearrange("p (k n) -> p k n", n=TOPK)
            idxf = take(NQ * TOPK).rearrange("p (h q n) -> p h q n", h=PH, q=2)
            cand = take(PH * TOPK * TOPK).rearrange("p (h n) -> p h n", h=PH)
            best = take(PH * TOPK).rearrange("p (h n) -> p h n", h=PH)
            sel = take(PH * TOPK, U32).rearrange("p (h n) -> p h n", h=PH)
            part = take(PH * TOPK, U32).rearrange("p (h n) -> p h n", h=PH)
            partf = take(PH * TOPK).rearrange("p (h n) -> p h n", h=PH)
            cand2 = rest.rearrange("p k n -> p (k n)").rearrange("p (h n) -> p h n", h=PH)
            for t, (a, b) in enumerate(TILES):
                n = b - a
                r = slice(0, n)
                dve.wait_ge(s_sc, t + 1)
                score = lambda k: ps[r, 2 + k // 4, (k % 4) * P:(k % 4 + 1) * P]
                for k in range(NQ):
                    last = nc.vector.max(val[r, k, 0:8], score(k))
                link(last)
                for k in range(NQ):
                    nc.vector.max_index(idx[r, k, 0:8], val[r, k, 0:8], score(k))
                    last = nc.vector.match_replace(out=rest[r, k, :], in_to_replace=val[r, k, 0:8], in_values=score(k),
                                                   imm_value=LOWEST)
                last.then_inc(s_sr, 1)
                dve.wait_ge(s_sr, t + 1)
                for k in range(NQ):
                    last = nc.vector.max(val[r, k, 8:16], rest[r, k, :])
                link(last)
                for k in range(NQ):
                    last = nc.vector.max_index(idx[r, k, 8:16], val[r, k, 8:16], rest[r, k, :])
                v4 = val.rearrange("p (h q) n -> p h q n", h=PH)
                shape = [n, PH, TOPK, TOPK]
                link(nc.vector.tensor_tensor(cand[r].rearrange("p h (a b) -> p h a b", a=TOPK),
                                             v4[r, :, 0, :].unsqueeze(3).to_broadcast(shape),
                                             v4[r, :, 1, :].unsqueeze(2).to_broadcast(shape), ALU.add))
                link(nc.vector.tensor_copy(idxf[r].rearrange("p h q n -> p (h q n)"), idx[r].rearrange("p k n -> p (k n)")))
                for h in range(PH):
                    last = nc.vector.max(best[r, h, 0:8], cand[r, h, :])
                link(last)
                for h in range(PH):
                    nc.vector.max_index(sel[r, h, 0:8], best[r, h, 0:8], cand[r, h, :])
                    last = nc.vector.match_replace(out=cand2[r, h, :], in_to_replace=best[r, h, 0:8],
                                                   in_values=cand[r, h, :], imm_value=LOWEST)
                link(last)
                for h in range(PH):
                    last = nc.vector.max(best[r, h, 8:16], cand2[r, h, :])
                link(last)
                for h in range(PH):
                    last = nc.vector.max_index(sel[r, h, 8:16], best[r, h, 8:16], cand2[r, h, :])
                nc.vector.tensor_tensor(pick[r, t, 2, :].rearrange("p (h n) -> p h n", h=PH), best[r],
                                        best[r, :, 0:1].to_broadcast([n, PH, TOPK]), ALU.subtract)
                link(last)
                for half, (op, by) in enumerate(((ALU.logical_shift_right, 4), (ALU.bitwise_and, TOPK - 1))):
                    link(nc.vector.tensor_scalar(part[r], sel[r], by, None, op))
                    link(nc.vector.tensor_copy(partf[r], part[r]))
                    eq = cand[r].rearrange("p h (k a) -> p (h k) a", k=TOPK)
                    link(nc.vector.tensor_tensor(eq, partf[r].rearrange("p h n -> p (h n)").unsqueeze(2)
                                                 .to_broadcast([n, PH * TOPK, TOPK]),
                                                 step.iota[r, 0:TOPK].unsqueeze(1).to_broadcast([n, PH * TOPK, TOPK]),
                                                 ALU.is_equal))
                    e4 = cand[r].rearrange("p h (k a) -> p h k a", k=TOPK)
                    link(nc.vector.tensor_tensor(e4, e4, idxf[r, :, half, :].unsqueeze(2).to_broadcast(shape), ALU.mult))
                    link(nc.vector.reduce_sum(pick[r, t, half, :], eq, axis=AX))
                nc.vector.tensor_copy(partf[r, 0, 0:1], part[r, 0, 0:1]).then_inc(s_rt, 1)
            for t, (a, b) in enumerate(TILES):
                n = b - a
                dve.wait_ge(s_e, t + 1)
                w = pick[0:n, t, 2, :].rearrange("p (h k) -> p h k", h=PH)
                d = den[0:n, t, :]
                link(nc.vector.reduce_sum(d, w, axis=AX))
                link(nc.vector.reciprocal(d, d))
                nc.vector.tensor_tensor(w, w, d.unsqueeze(2).to_broadcast([n, PH, TOPK]), ALU.mult).then_inc(s_w, 1)
            for t, (a, b) in enumerate(TILES):
                dve.wait_ge(s_t, t + 1)
                src = ps[:, 2 + t, 0:3 * P].rearrange("p (w n) -> p w n", w=3)[:, :, 0:b - a]
                nc.vector.tensor_copy(selT[:, :, a:b], src)
    step.used += NKEYS


def peer_gates(step, layer, big, selT):
    nc, ps = step.nc, step.ps
    L = f"_{layer}"
    GT = 4
    NG = T // GT
    NB = 3
    STEP = 2 * NB
    N = NG // STEP
    with ExitStack() as c1, nc.Block("peer_gate_matrix" + L, no_gpsimd_drain=True) as block:
        rows = step.sb("one_hot_rows" + L, [P, NB, GT, P], ctx=c1)
        cols = step.sb("one_hot_columns" + L, [P, NB, GT, P], ctx=c1)
        dist = step.sb("distances" + L, [P, 2, GT, P], ctx=c1)
        s_r = step.sem("one_hot_rows_ready" + L)
        s_d = step.sem("distances_ready" + L)
        s_ab = step.sem("absolute_distances_ready" + L)
        s_c = step.sem("one_hot_columns_ready" + L)
        s_w = step.sem("columns_times_gates_ready" + L)
        s_g = step.sem("gate_product_ready" + L)
        s_gm = step.sem("gate_applied" + L)
        tokens = lambda i, g: bass.ds((STEP * i + g) * GT, GT)
        token = lambda i, g, k: bass.ds((STEP * i + g) * GT + k, 1)
        shape = [P, GT, P]
        spread = lambda w, i, g: selT[:, w, tokens(i, g)].unsqueeze(2).to_broadcast(shape)
        iota = step.iota.unsqueeze(1).to_broadcast(shape)

        @block.gpsimd
        def _(pool):
            def distances(i, g, first=False):
                if not (first and g < 2):
                    pool.wait_ge(s_c, STEP * i + g - 1)
                nc.gpsimd.tensor_tensor(dist[:, g % 2], iota, spread(1, i, g), ALU.subtract).then_inc(s_d, 1)

            def gates(i, g):
                pool.wait_ge(s_c, STEP * i + g + 1)
                nc.gpsimd.tensor_tensor(cols[:, 0], cols[:, 0], spread(2, i, g), ALU.mult).then_inc(s_w, 1)

            def iteration(i, first):
                for g in range(STEP):
                    distances(i, g, first)
                    if g % NB == 2:
                        gates(i, g - 2)
            iteration(0, True)
            with pool.Fori(1, N) as i:
                iteration(i, False)
            pool.wait_ge(s_w, 2 * N)

        @block.scalar
        def _(act):
            def columns(i, g, first=False):
                b = g % NB
                act.wait_ge(s_d, STEP * i + g + 1)
                nc.scalar.activation(dist[:, g % 2], dist[:, g % 2], ACT.Abs).then_inc(s_ab, 1)
                if not (first and g < NB):
                    act.wait_ge(s_g, STEP * i + g + 1 - NB)
                act.wait_ge(s_ab, STEP * i + g + 1)
                nc.scalar.activation(cols[:, b], dist[:, g % 2], ACT.Relu, scale=-1.0,
                                     bias=step.ones[:, 0:1]).then_inc(s_c, 1)
            nc.scalar.preload_act_table(ACT.Relu)
            for g in range(STEP):
                columns(0, g, True)
            with act.Fori(1, N) as i:
                for g in range(STEP):
                    columns(i, g)

        @block.vector
        def _(dve):
            def one_hot_rows(i, g, first=False):
                b = g % NB
                if not (first and g < NB):
                    dve.wait_ge(s_g, STEP * i + g + 1 - NB)
                if b == 0:
                    nc.vector.tensor_tensor(rows[:, b], iota, spread(0, i, g), ALU.is_equal).then_inc(s_r, 1)
                    return
                for k in range(GT):
                    last = nc.vector.tensor_scalar(rows[:, b, k, :], step.iota, selT[:, 0, token(i, g, k)],
                                                   selT[:, 2, token(i, g, k)], ALU.is_equal, ALU.mult)
                last.then_inc(s_r, 1)

            def apply(i, g):
                dve.wait_ge(s_g, STEP * i + g + 1)
                h = big[:, :, tokens(i, g)]
                nc.vector.tensor_tensor(h, ps[:, g, :].rearrange("p (k n) -> p n k", k=GT), h,
                                        ALU.mult).then_inc(s_gm, 1)

            def iteration(i, first):
                for g in range(STEP):
                    one_hot_rows(i, g, first)
                    if not (first and g < NB):
                        apply(i if g >= NB else i - 1, (g - NB) % STEP)
            iteration(0, True)
            with dve.Fori(1, N) as i:
                iteration(i, False)
            for g in range(STEP - NB, STEP):
                apply(N - 1, g)

        @block.tensor
        def _(pe):
            def products(i, g, first=False):
                b = g % NB
                pe.wait_ge(s_r, STEP * i + g + 1)
                if b == 0:
                    pe.wait_ge(s_w, 2 * i + g // NB + 1)
                else:
                    pe.wait_ge(s_c, STEP * i + g + 1)
                if not first:
                    pe.wait_ge(s_gm, STEP * (i - 1) + g + 1)
                for k in range(GT):
                    last = nc.tensor.matmul(ps[:, g, k * P:(k + 1) * P], rows[:, b, k, :], cols[:, b, k, :],
                                            start=True, stop=True)
                last.then_inc(s_g, 1)
            for g in range(STEP):
                products(0, g, True)
            with pe.Fori(1, N) as i:
                for g in range(STEP):
                    products(i, g)


def peer_down(step, layer, big):
    nc, io, ps = step.nc, step.io, step.ps
    L = f"_{layer}"
    base = step.used
    vb = step.slabs[base][1]
    with ExitStack() as c1, nc.Block("peer_down" + L, no_gpsimd_drain=True) as block:
        HALF = D // 2
        hi, lo = (part[:].rearrange("p c t -> p (c t)")[:, 0:4 * HALF].rearrange("p (b f) -> p b f", b=4)
                  for part in step.operand)
        wh = step.sb("w_hi" + L, [P, 2, T], F32R, ctx=c1)
        wl = step.sb("w_lo" + L, [P, 2, T], F32R, ctx=c1)
        s_hi = step.sem("v_hi_ready" + L)
        s_wh = step.sem("w_hi_ready" + L)
        s_wl = step.sem("w_lo_ready" + L)
        s_y = step.sem("down_half_product_ready" + L)

        @block.sync
        def _(sp):
            with sp.Fori(1, NKEYS // SLOTS) as i:
                for s in range(SLOTS):
                    sp.wait_ge(step.v_split, 2 * (vb + SLOTS * i + s + 1 - SLOTS))
                    sp.dma_start(step.ring[:, s, :], io["v"][layer * P + SLOTS * i + s]).then_inc(step.slab_ready[s], 16)
            step.loaded = base + NKEYS
            step.load_until(sp, base + NKEYS + SLOTS)

        @block.scalar
        def _(act):
            def high(i, s, first):
                n = SLOTS * i + s
                act.wait_ge(step.slab_ready[s], 16 * (base // SLOTS + 1) + 16 * i)
                for g in range(2):
                    if not (first and s < 2):
                        act.wait_ge(s_y, 2 * n + g - 3)
                    if g:
                        nc.scalar.activation(wh[:, s % 2, :], big[:, n, :], ACT.Copy).then_inc(s_wh, 1)
                    nc.scalar.activation(hi[:, (2 * s + g) % 4, :], step.ring[:, s, g * HALF:(g + 1) * HALF],
                                         ACT.Copy).then_inc(s_hi, 1)
            for s in range(SLOTS):
                high(0, s, True)
            with act.Fori(1, NKEYS // SLOTS) as i:
                for s in range(SLOTS):
                    high(i, s, False)

        @block.vector
        def _(dve):
            with dve.Fori(0, NKEYS // SLOTS) as i:
                for s in range(SLOTS):
                    n = SLOTS * i + s
                    for g in range(2):
                        if g:
                            dve.wait_ge(s_wh, n + 1)
                            nc.vector.tensor_tensor(wl[:, s % 2, :], big[:, n, :], wh[:, s % 2, :].bitcast(F32),
                                                    ALU.subtract).then_inc(s_wl, 1)
                        dve.wait_ge(s_hi, 2 * n + g + 1)
                        buf = (2 * s + g) % 4
                        nc.vector.tensor_tensor(lo[:, buf, :], step.ring[:, s, g * HALF:(g + 1) * HALF],
                                                hi[:, buf, :].bitcast(F32), ALU.subtract).then_inc(step.v_split, 1)

        @block.tensor
        def _(pe):
            def down(i, s, first, final):
                n = SLOTS * i + s
                b = s % 2
                pe.wait_ge(s_wl, n + 1)
                for g in range(2):
                    pe.wait_ge(step.v_split, 2 * (vb + n) + g + 1)
                    buf = (2 * s + g) % 4
                    for k in range(HC):
                        cs = slice(k * P, (k + 1) * P)
                        bank = ps[:, g * HC + k, 0:T]
                        nc.tensor.matmul(bank, hi[:, buf, cs], wh[:, b, :], start=first, stop=False)
                        nc.tensor.matmul(bank, hi[:, buf, cs], wl[:, b, :], start=False, stop=False)
                        last = nc.tensor.matmul(bank, lo[:, buf, cs], wh[:, b, :], start=False, stop=final)
                    last.then_inc(s_y, 1)
            for s in range(SLOTS):
                down(0, s, s == 0, False)
            with pe.Fori(1, NKEYS // SLOTS - 1) as i:
                for s in range(SLOTS):
                    down(i, s, False, False)
            for s in range(SLOTS):
                down(NKEYS // SLOTS - 1, s, False, s == SLOTS - 1)
    step.used += NKEYS

    with ExitStack() as c1, nc.Block("peer_norm" + L, no_gpsimd_drain=True) as block:
        res = step.sb("res_peer" + L, [P, DC, T], ctx=c1)

        def residual_steps(dve, j):
            return nc.vector.scalar_tensor_tensor(out=res[:, j, :], in0=step.x[:, j, :], scalar=ALPHA,
                                                  in1=ps[:, j, 0:T], op0=ALU.mult, op1=ALU.add)
        emit_norm(step, block, "peer" + L, layer * 3 + 2, res, (0, 1), residual_steps,
                  lambda pe, j, s_res: None, step.used if layer + 1 < LAYERS else None)


_PROJ_COUNTS = (20 + 16 + 8 + 8 + 8 + 16, 12 + 16 + 8 + 8 + 8 + 16)

_OUTS = {
    "y": (P, DC, T),
    "hgrn_prompt": (P, HEADS_A, P), "hgrn_sample": (P, HEADS_A * TS, P),
    "pool_prompt": (P, HEADS_A, CTX), "pool_sample": (P, HEADS_A, TS, CTX),
    "window_k_prompt": (HD, KV, P), "window_k_sample": (HD, TS, KV, P),
    "window_v_prompt": (P, KV, HD), "window_v_sample": (P, TS, KV, HD),
    "mem_k_out": (LAYERS, P, DC, NMEM), "mem_v_out": (LAYERS, P, NMEM // P, D),
}


def _constants():
    import numpy as np
    c = np.zeros((P, C_END), np.float32)
    c[:, C_ID:C_ID + P] = np.eye(P)
    c[:, C_ONE:C_ONE + P] = 1
    c[:, C_BLK:C_END] = np.kron(np.eye(P // BLK), np.ones((BLK, 1)))
    c[:, C_MEAN:C_MEAN + P] = 1 / D
    c[:, C_HEAD:C_HEAD + P] = 1 / P
    c[:, C_IOTA:C_IOTA + P] = np.arange(P)
    q = np.arange(P)[:, None]
    k = np.arange(P)[None, :]
    c[:, C_MASK:C_MASK + P] = np.where(k <= q, 0, LOWEST)
    k = np.arange(2 * P)[None, :]
    c[:, C_MASK + P:C_MASK + 3 * P] = np.where((k > q) & (k <= q + P), 0, LOWEST)
    c[:, C_EPS] = EPS
    scan = np.ones((P, TP), np.float32)
    scan[:, ::BLK] = 0
    inv = np.zeros((P, HEADS_A, T), np.float32)
    for g, w in enumerate(POOL_SIZES):
        inv[:, g, :TP] = 1 / np.minimum(np.arange(TP) + 1, w)
        inv[:, g, TP:] = 1 / w
    return c, scan, inv


def kernel(**inputs):
    import numpy as np
    import concourse.bacc as bacc
    from concourse.bass_utils import run_bass_kernel_spmd

    a = {k: np.asarray(v) for k, v in inputs.items()}

    def chunks(m):
        return m.reshape(m.shape[0], -1, P).transpose(2, 1, 0)

    def slabs(w):
        return w.reshape(DC, P, -1, P).transpose(2, 1, 0, 3).reshape(-1, P, D)

    const, scan, inv = _constants()
    arrays = {"const": const, "scan_mask": scan, "inv_count": inv}
    arrays["x"] = chunks(np.concatenate([a["x_prompt"][0], a["x_sample"][:, 0]]))
    arrays["mem"] = chunks(a["mem_prompt"][0])
    arrays["ln"] = np.stack([a["ln_g"], a["ln_b"]], 2).reshape(LAYERS * 3, 2, DC, P).transpose(3, 0, 1, 2)
    arrays["gamma"] = a["hgrn_gamma"].reshape(2, HEADS_A, P).transpose(2, 0, 1)
    arrays["norm_g"] = a["hgrn_norm_g"][0].reshape(HEADS_A, P).T
    arrays["pool_scale"] = a["pool_scale"][0].reshape(HEADS_A, P).T
    arrays["pool_w"] = a["pool_w"][0].transpose(1, 0, 2)
    arrays["pool_ctx"] = a["state_pool"][0].reshape(TS, CTX, HEADS_A, P).transpose(3, 2, 0, 1)
    arrays["state"] = a["state_hgrn"][0].transpose(2, 1, 0, 3).reshape(P, -1, P)
    wc = a["w_in_c"][0]
    nq = HEADS_C * HD
    dup = [wc[:, nq + i * HD:nq + (i + 1) * HD] for i in (0, 0, 1, 1, 2, 2, 3, 3)]
    w = a["w_in_a"][0]
    part = [w[:, i * 512:(i + 1) * 512] for i in (0, 1, 3, 2, 4)]
    first = (part, [wc[:, :nq]] + dup)
    outs = (a["w_out_a"][0], a["w_out_c"][0])
    cols = []
    for layer in range(LAYERS):
        cols += [*first[layer], a["mem_wkv"][layer], outs[layer], a["mem_wq"][layer], a["mem_wo"][layer],
                 a["peer_wq"][layer]]
    arrays["proj"] = slabs(np.concatenate(cols, 1))
    arrays["u"] = a["peer_u"].reshape(LAYERS, P, P, DC, P).transpose(0, 2, 4, 3, 1).reshape(-1, P, D)
    arrays["v"] = a["peer_v"].reshape(LAYERS, P, P, D).transpose(0, 2, 1, 3).reshape(-1, P, D)
    arrays["subkeys"] = a["peer_subkeys"].transpose(0, 4, 1, 2, 3).reshape(LAYERS, P, -1)
    ckm = a["cache_mem_k"].reshape(LAYERS, TS, NMEM, DC, P)
    arrays["cache_k"] = ckm.transpose(0, 1, 4, 3, 2)
    arrays["cache_v"] = a["cache_mem_v"].reshape(LAYERS, TS, 2, P, D).transpose(0, 1, 3, 2, 4)
    k = a["cache_swa_k"][0][:, 1:].transpose(3, 0, 2, 1)
    arrays["window_k"] = np.concatenate([k, k])
    v = a["cache_swa_v"][0][:, 1:].transpose(1, 0, 2, 3)
    arrays["window_v"] = np.concatenate([v, v], 3)
    s = a["attn_sinks"][0]
    order = s.reshape(KV, 4, 2).transpose(0, 2, 1).reshape(-1)
    arrays["sinks"] = np.concatenate([np.tile(s, (P, 1)), np.tile(order, TS)[:, None]], 1)
    arrays = {k: np.ascontiguousarray(v) for k, v in arrays.items()}

    nc = bacc.Bacc("TRN2", target_bir_lowering=False, num_devices=1)
    io = {k: nc.dram_tensor(f"in_{k}", v.shape, F32, kind="ExternalInput").ap() for k, v in arrays.items()}
    for k, shape in _OUTS.items():
        io[k] = nc.dram_tensor(f"out_{k}", shape, F32, kind="ExternalOutput").ap()
    io["proj_counts"] = _PROJ_COUNTS
    hybrid_step(nc, io)
    r = run_bass_kernel_spmd(nc, [{f"in_{k}": v for k, v in arrays.items()}], core_ids=[0]).results[0]
    o = {k: r[f"out_{k}"] for k in _OUTS}

    y = o["y"].transpose(2, 1, 0).reshape(T, D)
    return (
        y[None, :TP], y[TP:, None],
        o["hgrn_prompt"].transpose(1, 0, 2)[None, None],
        o["hgrn_sample"].reshape(P, HEADS_A, TS, P).transpose(2, 1, 0, 3)[None],
        o["pool_prompt"].transpose(2, 1, 0).reshape(CTX, -1)[None, None],
        o["pool_sample"].transpose(2, 3, 1, 0).reshape(TS, CTX, -1)[None],
        o["window_k_prompt"].transpose(2, 1, 0)[None, None],
        o["window_k_sample"].transpose(1, 3, 2, 0)[None],
        o["window_v_prompt"][None, None],
        o["window_v_sample"].transpose(1, 0, 2, 3)[None],
        o["mem_k_out"].transpose(0, 3, 2, 1).reshape(LAYERS, 1, NMEM, MH, MHD),
        o["mem_v_out"].transpose(0, 2, 1, 3).reshape(LAYERS, 1, NMEM, MH, MHD),
    )
```
